# Optimizing a Trainium2 kernel written in Bass

```python
import jax, jax.numpy as jnp
from jax import lax
import numpy as np

D_MODEL = 1024
BATCH = 1
SEQ = 256
DEPTH = 2
DEC_BATCH = 1
DEC_SEQ = 1024
PAST_LEN = 128

HEAD_DIM = 64
D_MIX = D_MODEL
ATT_WIDTH = D_MIX // 4
ATT_HEADS = ATT_WIDTH // HEAD_DIM
ATT_KV_HEADS = ATT_HEADS // 2
ATT_GROUP = ATT_HEADS // ATT_KV_HEADS
WINDOW = 128
BLOCK = 128
REL_BUCKETS = 32
REL_MAX_DIST = 128
SSD_WIDTH = D_MIX // 2
SSD_HEADS = SSD_WIDTH // HEAD_DIM
SSD_STATE = 64
SSD_GROUPS = 2
SSD_CONV = 5
SSD_CHUNK = 128
SSD_CONV_DIM = SSD_WIDTH + 2 * SSD_GROUPS * SSD_STATE
MLSTM_WIDTH = D_MIX // 4
MLSTM_HEADS = MLSTM_WIDTH // HEAD_DIM
MLSTM_CHUNK = 128
N_EXPERTS = 16
EC_CAPACITY = 2
EXPERT_FF = D_MODEL // 2
RMS_EPS = 1e-6
IN_SPLITS = (ATT_WIDTH, ATT_KV_HEADS * HEAD_DIM, ATT_KV_HEADS * HEAD_DIM,
             SSD_WIDTH, SSD_CONV_DIM, 2 * SSD_HEADS,
             MLSTM_WIDTH, MLSTM_WIDTH, MLSTM_WIDTH, MLSTM_WIDTH, 2 * MLSTM_HEADS, 2 * MLSTM_HEADS)
D_IN = sum(IN_SPLITS)

kernel_name = 'hybrid_bidir_attn_ssd_mlstm_ec_moe'

def _rmsnorm(x, g):
    xf = x.astype(jnp.float32)
    y = xf * lax.rsqrt(jnp.mean(xf * xf, axis=-1, keepdims=True) + RMS_EPS)
    return (y * g.astype(jnp.float32)).astype(x.dtype)

def _flip(t):
    return t[:, ::-1]

def _t5_buckets(rel):
    half = REL_BUCKETS // 2
    exact = half // 2
    n = np.abs(rel)
    large = exact + (np.log(np.maximum(n, 1) / exact) / np.log(REL_MAX_DIST / exact)
                     * (half - exact)).astype(np.int32)
    large = np.minimum(large, half - 1)
    return (rel > 0).astype(np.int32) * half + np.where(n < exact, n, large)

def _window_attention(q, k, v, q_gain, k_gain, sink, rel_bias):
    B, S = q.shape[0], q.shape[1]
    nb = S // BLOCK
    q = _rmsnorm(q, q_gain)
    k = _rmsnorm(k, k_gain)
    qb = q.reshape(B, nb, BLOCK, ATT_KV_HEADS, ATT_GROUP, HEAD_DIM)
    pad = ((0, 0), (BLOCK, BLOCK), (0, 0), (0, 0))
    kp = jnp.pad(k, pad).reshape(B, nb + 2, BLOCK, ATT_KV_HEADS, HEAD_DIM)
    vp = jnp.pad(v, pad).reshape(B, nb + 2, BLOCK, ATT_KV_HEADS, HEAD_DIM)
    kw = jnp.concatenate([kp[:, :-2], kp[:, 1:-1], kp[:, 2:]], axis=2)
    vw = jnp.concatenate([vp[:, :-2], vp[:, 1:-1], vp[:, 2:]], axis=2)
    s = jnp.einsum('bnqhgd,bnkhd->bnhgqk', qb, kw,
                   preferred_element_type=jnp.float32) * (HEAD_DIM ** -0.5)
    kpos = np.arange(3 * BLOCK)[None, :] - BLOCK
    rel = kpos - np.arange(BLOCK)[:, None]
    bias = rel_bias.astype(jnp.float32)[_t5_buckets(rel)]
    bias = bias.transpose(2, 0, 1).reshape(ATT_KV_HEADS, ATT_GROUP, BLOCK, 3 * BLOCK)
    abs_k = np.arange(nb)[:, None] * BLOCK + kpos
    valid = (np.abs(rel) <= WINDOW)[None] & ((abs_k >= 0) & (abs_k < S))[:, None, :]
    s = jnp.where(valid[None, :, None, None], s + bias, -jnp.inf)
    sink_l = sink.astype(jnp.float32).reshape(ATT_KV_HEADS, ATT_GROUP)[None, None, :, :, None, None]
    m = jnp.maximum(jnp.max(s, axis=-1, keepdims=True), sink_l)
    p = jnp.exp(s - m)
    denom = jnp.sum(p, axis=-1, keepdims=True) + jnp.exp(sink_l - m)
    o = jnp.einsum('bnhgqk,bnkhd->bnqhgd', (p / denom).astype(v.dtype), vw)
    return o.reshape(B, S, ATT_WIDTH)

def _segsum(a):
    cs = jnp.cumsum(a, axis=-1)
    L = a.shape[-1]
    mask = np.tril(np.ones((L, L), dtype=bool))
    return jnp.where(mask, cs[..., :, None] - cs[..., None, :], -jnp.inf)

def _ssd_scan(x, dt, A, Bm, Cm):
    Bsz, S, H, P = x.shape
    N = Bm.shape[-1]
    nc = S // SSD_CHUNK
    xdt = (x * dt[..., None]).reshape(Bsz, nc, SSD_CHUNK, H, P)
    Bc = Bm.reshape(Bsz, nc, SSD_CHUNK, H, N)
    Cc = Cm.reshape(Bsz, nc, SSD_CHUNK, H, N)
    a = (dt * A).reshape(Bsz, nc, SSD_CHUNK, H).transpose(0, 3, 1, 2)
    a_cs = jnp.cumsum(a, axis=-1)
    cb = jnp.einsum('bclhn,bcshn->bhcls', Cc, Bc) * jnp.exp(_segsum(a))
    y_diag = jnp.einsum('bhcls,bcshp->bclhp', cb, xdt)
    decay_to_end = jnp.exp(a_cs[..., -1:] - a_cs)
    states = jnp.einsum('bclhn,bhcl,bclhp->bchpn', Bc, decay_to_end, xdt)
    chunk_decay = jnp.exp(a_cs[..., -1])

    def step(h, inp):
        st, dec = inp
        return h * dec[..., None, None] + st, h

    _, prev = lax.scan(step, jnp.zeros((Bsz, H, P, N), jnp.float32),
                       (states.transpose(1, 0, 2, 3, 4), chunk_decay.transpose(2, 0, 1)))
    prev = prev.transpose(1, 0, 2, 3, 4)
    y_off = jnp.einsum('bclhn,bchpn,bhcl->bclhp', Cc, prev, jnp.exp(a_cs))
    return (y_diag + y_off).reshape(Bsz, S, H, P)

def _ssd_mixer(z, xbc, dt_raw, conv_w, conv_b, dt_bias, a_log, d_skip, norm_g):
    B, S = z.shape[0], z.shape[1]
    half = SSD_CONV // 2
    xp = jnp.pad(xbc, ((0, 0), (half, half), (0, 0)))
    conv = conv_b + sum(xp[:, j:j + S] * conv_w[j] for j in range(SSD_CONV))
    xbc = jax.nn.silu(conv)
    xs, Bm, Cm = jnp.split(xbc, [SSD_WIDTH, SSD_WIDTH + SSD_GROUPS * SSD_STATE], axis=-1)
    rep = SSD_HEADS // SSD_GROUPS
    xs = xs.reshape(B, S, SSD_HEADS, HEAD_DIM).astype(jnp.float32)
    Bm = jnp.repeat(Bm.reshape(B, S, SSD_GROUPS, SSD_STATE), rep, axis=2).astype(jnp.float32)
    Cm = jnp.repeat(Cm.reshape(B, S, SSD_GROUPS, SSD_STATE), rep, axis=2).astype(jnp.float32)
    dt = jax.nn.softplus(dt_raw.astype(jnp.float32).reshape(B, S, 2, SSD_HEADS)
                         + dt_bias.astype(jnp.float32))
    A = -jnp.exp(a_log.astype(jnp.float32))
    y_f = _ssd_scan(xs, dt[:, :, 0], A[0], Bm, Cm)
    y_b = _flip(_ssd_scan(_flip(xs), _flip(dt[:, :, 1]), A[1], _flip(Bm), _flip(Cm)))
    y = y_f + y_b + xs * d_skip.astype(jnp.float32)[:, None]
    y = y.reshape(B, S, SSD_WIDTH) * jax.nn.silu(z.astype(jnp.float32))
    return _rmsnorm(y, norm_g).astype(z.dtype)

def _mlstm_scan(q, k, v, li, lf):
    Bsz, S, H, Dh = q.shape
    L = MLSTM_CHUNK
    nc = S // L
    qc = q.reshape(Bsz, nc, L, H, Dh)
    kc = k.reshape(Bsz, nc, L, H, Dh)
    vc = v.reshape(Bsz, nc, L, H, Dh)
    li = li.reshape(Bsz, nc, L, H).transpose(0, 3, 1, 2)
    lf = lf.reshape(Bsz, nc, L, H).transpose(0, 3, 1, 2)
    b = jnp.cumsum(lf, axis=-1)
    g = b[..., -1]
    a = g[..., None] - b + li
    m_loc = jnp.max(a, axis=-1)
    w = jnp.exp(a - m_loc[..., None])
    c_loc = jnp.einsum('bhcs,bcshe,bcshd->bched', w, vc, kc)
    n_loc = jnp.einsum('bhcs,bcshd->bchd', w, kc)

    def step(carry, inp):
        C, n, m = carry
        cl, nl, ml, gl = inp
        m_new = jnp.maximum(gl + m, ml)
        s_old = jnp.exp(gl + m - m_new)
        s_new = jnp.exp(ml - m_new)
        C_new = C * s_old[..., None, None] + cl * s_new[..., None, None]
        n_new = n * s_old[..., None] + nl * s_new[..., None]
        return (C_new, n_new, m_new), (C, n, m)

    init = (jnp.zeros((Bsz, H, Dh, Dh), jnp.float32), jnp.zeros((Bsz, H, Dh), jnp.float32),
            jnp.full((Bsz, H), -jnp.inf, jnp.float32))
    _, (c_prev, n_prev, m_prev) = lax.scan(
        step, init,
        (c_loc.transpose(1, 0, 2, 3, 4), n_loc.transpose(1, 0, 2, 3),
         m_loc.transpose(2, 0, 1), g.transpose(2, 0, 1)))
    c_prev = c_prev.transpose(1, 0, 2, 3, 4)
    n_prev = n_prev.transpose(1, 0, 2, 3)
    m_prev = m_prev.transpose(1, 2, 0)
    mask = np.tril(np.ones((L, L), dtype=bool))
    dmat = jnp.where(mask, b[..., :, None] - b[..., None, :] + li[..., None, :], -jnp.inf)
    m_inter = b + m_prev[..., None]
    m_l = jnp.maximum(jnp.max(dmat, axis=-1), m_inter)
    wq = jnp.exp(dmat - m_l[..., None]) * jnp.einsum('bclhd,bcshd->bhcls', qc, kc)
    sc = jnp.exp(m_inter - m_l)
    num = jnp.einsum('bhcls,bcshd->bclhd', wq, vc) + jnp.einsum('bclhd,bched,bhcl->bclhe', qc, c_prev, sc)
    den = jnp.sum(wq, axis=-1) + jnp.einsum('bclhd,bchd,bhcl->bhcl', qc, n_prev, sc)
    den = jnp.maximum(jnp.abs(den), jnp.exp(-m_l)).transpose(0, 2, 3, 1)
    return (num / den[..., None]).reshape(Bsz, S, H, Dh)

def _mlstm_mixer(q, k, v, o, ig, fg, i_bias, f_bias, norm_g):
    B, S = q.shape[0], q.shape[1]
    shp = (B, S, MLSTM_HEADS, HEAD_DIM)
    q = q.reshape(shp).astype(jnp.float32)
    k = k.reshape(shp).astype(jnp.float32) * (HEAD_DIM ** -0.5)
    v = v.reshape(shp).astype(jnp.float32)
    li = ig.astype(jnp.float32).reshape(B, S, 2, MLSTM_HEADS) + i_bias.astype(jnp.float32)
    lf = jax.nn.log_sigmoid(fg.astype(jnp.float32).reshape(B, S, 2, MLSTM_HEADS)
                            + f_bias.astype(jnp.float32))
    h_f = _mlstm_scan(q, k, v, li[:, :, 0], lf[:, :, 0])
    h_b = _flip(_mlstm_scan(_flip(q), _flip(k), _flip(v), _flip(li[:, :, 1]), _flip(lf[:, :, 1])))
    h = _rmsnorm(h_f + h_b, norm_g.reshape(MLSTM_HEADS, HEAD_DIM)).reshape(B, S, MLSTM_WIDTH)
    return (jax.nn.sigmoid(o.astype(jnp.float32)) * h).astype(o.dtype)

def _expert_choice_ffn(x, router, w_gate, w_up, w_down):
    B, S, D = x.shape
    T = B * S
    cap = EC_CAPACITY * T // N_EXPERTS
    xf = x.reshape(T, D)
    aff = jax.nn.softmax((xf @ router).astype(jnp.float32), axis=-1)
    gate, idx = lax.top_k(aff.T, cap)
    xs = xf[idx]
    hid = jax.nn.silu(jnp.einsum('ecd,edf->ecf', xs, w_gate)) * jnp.einsum('ecd,edf->ecf', xs, w_up)
    ye = jnp.einsum('ecf,efd->ecd', hid, w_down) * gate[..., None].astype(x.dtype)
    out = jnp.zeros((T, D), x.dtype).at[idx.reshape(-1)].add(ye.reshape(-1, D))
    return out.reshape(B, S, D)

def _trunk(x, mix_norm, w_in, attn_q_norm, attn_k_norm, attn_sink, rel_bias,
           ssd_conv_w, ssd_conv_b, ssd_dt_bias, ssd_a_log, ssd_d, ssd_norm,
           mlstm_i_bias, mlstm_f_bias, mlstm_norm, w_out, ffn_norm, router, w_gate, w_up, w_down):
    B, S = x.shape[0], x.shape[1]
    offsets = [int(o) for o in np.cumsum(IN_SPLITS)[:-1]]
    for l in range(DEPTH):
        h = _rmsnorm(x, mix_norm[l])
        aq, ak, av, sz, sxbc, sdt, mq, mk, mv, mo, mi, mf = jnp.split(h @ w_in[l], offsets, axis=-1)
        ya = _window_attention(aq.reshape(B, S, ATT_HEADS, HEAD_DIM),
                               ak.reshape(B, S, ATT_KV_HEADS, HEAD_DIM),
                               av.reshape(B, S, ATT_KV_HEADS, HEAD_DIM),
                               attn_q_norm[l], attn_k_norm[l], attn_sink[l], rel_bias)
        yb = _ssd_mixer(sz, sxbc, sdt, ssd_conv_w[l], ssd_conv_b[l], ssd_dt_bias[l],
                        ssd_a_log[l], ssd_d[l], ssd_norm[l])
        yc = _mlstm_mixer(mq, mk, mv, mo, mi, mf, mlstm_i_bias[l], mlstm_f_bias[l], mlstm_norm[l])
        x = x + jnp.concatenate([ya, yb, yc], axis=-1) @ w_out[l]
        x = x + _expert_choice_ffn(_rmsnorm(x, ffn_norm[l]), router[l], w_gate[l], w_up[l], w_down[l])
    return x

def setup_inputs(seed: int = 0) -> dict:
    key = jax.random.key(seed)
    ks = jax.random.split(key, 26)

    def nrm(k, shape, scale):
        return jax.random.normal(k, shape, jnp.float32) * scale

    dt0 = jnp.exp(jax.random.uniform(ks[10], (DEPTH, 2, SSD_HEADS), jnp.float32,
                                     minval=float(np.log(1e-3)), maxval=float(np.log(1e-1))))
    return {
        'x_prompt': nrm(ks[0], (BATCH, SEQ, D_MODEL), 1.0),
        'x_sample': nrm(ks[1], (DEC_BATCH, DEC_SEQ, D_MODEL), 1.0),
        'mix_norm': 1.0 + nrm(ks[2], (DEPTH, D_MODEL), 0.02),
        'w_in': nrm(ks[3], (DEPTH, D_MODEL, D_IN), D_MODEL ** -0.5),
        'attn_q_norm': 1.0 + nrm(ks[4], (DEPTH, HEAD_DIM), 0.02),
        'attn_k_norm': 1.0 + nrm(ks[5], (DEPTH, HEAD_DIM), 0.02),
        'attn_sink': nrm(ks[6], (DEPTH, ATT_HEADS), 0.5),
        'rel_bias': nrm(ks[7], (REL_BUCKETS, ATT_HEADS), 0.5),
        'ssd_conv_w': nrm(ks[8], (DEPTH, SSD_CONV, SSD_CONV_DIM), SSD_CONV ** -0.5),
        'ssd_conv_b': nrm(ks[9], (DEPTH, SSD_CONV_DIM), 0.02),
        'ssd_dt_bias': dt0 + jnp.log(-jnp.expm1(-dt0)),
        'ssd_a_log': jnp.log(jax.random.uniform(ks[11], (DEPTH, 2, SSD_HEADS), jnp.float32,
                                                minval=1.0, maxval=16.0)),
        'ssd_d': 1.0 + nrm(ks[12], (DEPTH, SSD_HEADS), 0.1),
        'ssd_norm': 1.0 + nrm(ks[13], (DEPTH, SSD_WIDTH), 0.02),
        'mlstm_i_bias': nrm(ks[14], (DEPTH, 2, MLSTM_HEADS), 0.1),
        'mlstm_f_bias': jnp.linspace(3.0, 6.0, MLSTM_HEADS, dtype=jnp.float32)
                        + nrm(ks[15], (DEPTH, 2, MLSTM_HEADS), 0.1),
        'mlstm_norm': 1.0 + nrm(ks[16], (DEPTH, MLSTM_WIDTH), 0.02),
        'w_out': nrm(ks[17], (DEPTH, D_MIX, D_MODEL), D_MIX ** -0.5),
        'ffn_norm': 1.0 + nrm(ks[18], (DEPTH, D_MODEL), 0.02),
        'router': nrm(ks[19], (DEPTH, D_MODEL, N_EXPERTS), D_MODEL ** -0.5),
        'w_gate': nrm(ks[20], (DEPTH, N_EXPERTS, D_MODEL, EXPERT_FF), D_MODEL ** -0.5),
        'w_up': nrm(ks[21], (DEPTH, N_EXPERTS, D_MODEL, EXPERT_FF), D_MODEL ** -0.5),
        'w_down': nrm(ks[22], (DEPTH, N_EXPERTS, EXPERT_FF, D_MODEL), EXPERT_FF ** -0.5),
    }

def reference(x_prompt, x_sample, mix_norm, w_in, attn_q_norm, attn_k_norm, attn_sink, rel_bias,
              ssd_conv_w, ssd_conv_b, ssd_dt_bias, ssd_a_log, ssd_d, ssd_norm,
              mlstm_i_bias, mlstm_f_bias, mlstm_norm, w_out, ffn_norm, router, w_gate, w_up, w_down):
    y_prompt = _trunk(x_prompt, mix_norm, w_in, attn_q_norm, attn_k_norm, attn_sink, rel_bias,
                      ssd_conv_w, ssd_conv_b, ssd_dt_bias, ssd_a_log, ssd_d, ssd_norm,
                      mlstm_i_bias, mlstm_f_bias, mlstm_norm, w_out, ffn_norm, router, w_gate, w_up, w_down)
    y_sample = _trunk(x_sample, mix_norm, w_in, attn_q_norm, attn_k_norm, attn_sink, rel_bias,
                      ssd_conv_w, ssd_conv_b, ssd_dt_bias, ssd_a_log, ssd_d, ssd_norm,
                      mlstm_i_bias, mlstm_f_bias, mlstm_norm, w_out, ffn_norm, router, w_gate, w_up, w_down)
    return (y_prompt, y_sample)


_drawn_inputs = setup_inputs


def setup_inputs(seed=0):
    import zlib

    import numpy as np

    out = dict(_drawn_inputs(seed))
    spreads = {}
    factors = {'attn_q_norm': 8.0,
     'attn_k_norm': 7.252,
     'attn_sink': 8.0,
     'mlstm_i_bias': 6.803,
     'mlstm_norm': 4.892,
     'ffn_norm': 2.877}
    for name, (base, spread) in spreads.items():
        noise = np.random.default_rng([zlib.crc32(name.encode()), seed]).standard_normal(out[name].shape)
        drawn = base * np.exp(spread * noise) if base else spread * noise
        out[name] = __import__('jax').numpy.asarray(drawn.astype(out[name].dtype))
    for name, factor in factors.items():
        out[name] = (out[name] * factor).astype(out[name].dtype)
    return out
```

```python
import concourse.bass as bass
from concourse import mybir
from contextlib import ExitStack
import numpy as np

DEPTH, D = 2, 1024
SEQS = (256, 1024)
T = sum(SEQS)
P = 128
NC = T // P
NP = SEQS[0] // P
KD = D // P
HD = 64
SH, MH, AH = 8, 4, 4
E, CAPS, CAPP, FF = 16, 128, 32, 512
TOK = CAPS + CAPP
KF = FF // P
D_IN = 2848
NEG = -1e30
EPS = 1e-6

PAR = {}
_n = 0
for _name, _w in (("gmix", 8), ("gffn", 8), ("gy", 8), ("convw", 30), ("convb", 6), ("qg", 1), ("kg", 1),
                  ("sink", 4), ("gbias", 32), ("alog", 16), ("dskip", 8), ("router", 128)):
    PAR[_name] = (_n, _n + _w)
    _n += _w
NPAR = _n
NCST = 3 * P + 1
NREL = 511

SLICES = [("xbc", 1024), ("xbc", 1280), ("xbc", 1536), ("z", 512), ("z", 768), ("qk", 1808), ("qk", 2064),
          ("v", 2320), ("o", 2576), ("att", 0), ("att", 256)]
GROUPS = [(0, 512), (512, 512), (1024, 256)]
UNITS = []
for _s, (_k, _c) in enumerate(SLICES):
    _i = [k for k, _ in SLICES[:_s]].count(_k)
    if _k in ("xbc", "qk"):
        UNITS += [(_s, _k, 2 * _i + h, g) for h in range(2) for g in range(3)]
    else:
        UNITS += [(_s, _k, _i, c) for c in range(NC)]
U_XBC, U_Z, U_QK, U_VO, U_ATT = 0, 18, 38, 50, 70
LAST_UNIT = [max(u for u, x in enumerate(UNITS) if x[0] == s) for s in range(len(SLICES))]


def in_seq(c):
    return (0, NP) if c < NP else (NP, NC)


def scan_chunk(d, i):
    if d == 0:
        return i
    lo, hi = in_seq(i)
    return lo + hi - 1 - i


def has_next(i):
    return i not in (NP - 1, NC - 1)


def tcol(c):
    return P * c + (2 if c >= NP else 0)



def attn_keys(c):
    lo, hi = in_seq(c)
    c0 = max(c - 1, lo)
    return min(c + 1, hi - 1) - c0 + 1, c0


def program(nc, wi, wo, wga, wup, wdn, par, cst, onehot, xp, xs_in, yp, ys, btab, h2p, h2s, flip):
    F32, U32 = mybir.dt.float32, mybir.dt.uint32
    ALU, ACT = mybir.AluOpType, mybir.ActivationFunctionType
    AX = mybir.AxisListType.X
    ctx = ExitStack()
    with ctx:
        def sb(name, cols, dt=F32, parts=P):
            return ctx.enter_context(nc.sbuf_tensor(name, [parts, cols], dt))

        HT = sb("HT", KD * T)
        MID = sb("MID", 2 * NC * 512 + 2 * 1284 + 2 * NC * 256 + 5120 + NC * 516)
        RING = sb("RING", 2 * KD * 256)
        SCR = sb("SCR", 4096)
        TMP = sb("TMP", 1536)
        cstt = sb("cstt", NCST)
        part = sb("part", NPAR)
        bias = sb("bias", AH * 384)
        small = sb("small", 1980)
        idxs = sb("idxs", E, U32)
        idxp = sb("idxp", E, U32, CAPP)
        idxu = sb("idxu", TOK, U32, E)
        ps = ctx.enter_context(nc.psum_tensor("ps", [P, 8, 512], F32))

        o = 0

        def take(n):
            nonlocal o
            o += n
            return MID[:, o - n:o]

        hT = HT[:, :].rearrange("p (k t) -> p k t", k=KD)
        ZF = take(NC * 512)
        Z = ZF.rearrange("p (c n) -> p c n", c=NC)
        XSF = take(NC * 512)
        XS = XSF.rearrange("p (c n) -> p c n", c=NC)
        bc_at = o
        BC = take(2 * 1284).rearrange("p (w t) -> p w t", w=2)
        pv_at = o
        PREV = take(2 * NC * 256).rearrange("p (d c n) -> p d c n", d=2, c=NC)
        qk_at = o
        QK = take(5120).rearrange("p (f t) -> p f t", f=4)
        VO = take(NC * 516)
        V = VO[:, 0:NC * 260].rearrange("p (c h e) -> p c h e", c=NC, h=MH)
        O = VO[:, NC * 260:NC * 516].rearrange("p (c n) -> p c n", c=NC)
        XF = [MID[:, qk_at + 1284 * j:qk_at + 1284 * (j + 1)] for j in range(2)]
        UROW = VO[0:4, 0:2 * T].rearrange("p (d t) -> p d t", d=2)
        MROW = VO[0:4, 2 * T:4 * T].rearrange("p (d t) -> p d t", d=2)
        PREVM = MID[:, pv_at:pv_at + 2 * NC * 130].rearrange("p (d c h e) -> p d c h e", d=2, c=NC, h=2)
        KT = MID[:, pv_at + 2 * NC * 130:pv_at + 2 * NC * 130 + T]
        QT = MID[:, bc_at:bc_at + 2 * T].rearrange("p (j t) -> p j t", j=2)
        WO = MID[:, pv_at:pv_at + KD * D].rearrange("p (k n) -> p k n", k=KD)
        ring = [RING[:, j * 2048:(j + 1) * 2048].rearrange("p (k n) -> p k n", k=KD) for j in range(2)]
        RAW = [SCR[:, 1288 * j:1288 * (j + 1)] for j in range(2)]
        ACC = [SCR[:, 2576:2576 + 1284], TMP[:, 0:1284]]
        BT = SCR[:, 0:NC * P].rearrange("p (c n) -> p c n", c=NC)
        DXS = SCR[:, 1280:1280 + 2048].rearrange("p (b d n) -> p b d n", b=2, d=2)
        DM = SCR[:, :].rearrange("p (b d n) -> p b d n", b=2, d=2)
        DMM = SCR[:, 0:2048].rearrange("p (b d h t) -> p b d h t", b=2, d=2, h=MH)
        PSC = [SCR[:, 1536 * b:1536 * (b + 1)].rearrange("p (h k) -> p h k", h=AH) for b in range(2)]
        ident, tri = cstt[:, 0:P], [cstt[:, P:2 * P], cstt[:, 2 * P:3 * P]]
        ones1 = cstt[:, 3 * P:3 * P + 1]
        bia = bias[:, :].rearrange("p (h k) -> p h k", h=AH)
        EW = [MID[:, j * 12288:(j + 1) * 12288] for j in range(2)]
        EG = [w[:, 0:4096].rearrange("p (k f) -> p k f", k=KD) for w in EW]
        EU = [w[:, 4096:8192].rearrange("p (k f) -> p k f", k=KD) for w in EW]
        ED = [w[:, 8192:12288].rearrange("p (k n) -> p k n", k=KF) for w in EW]
        XG = [HT[:, j * D:(j + 1) * D] for j in range(2)]
        XGP = [HT[0:CAPP, (2 + j) * D:(3 + j) * D] for j in range(2)]
        XT = [HT[:, 4096 + 1280 * j:4096 + 1280 * (j + 1)].rearrange("p (k t) -> p k t", k=KD) for j in range(2)]
        HID = HT[:, 6656:6656 + KF * TOK].rearrange("p (f t) -> p f t", f=KF)
        THG = HT[:, 7296:7296 + TOK]
        YO = HT[:, 7936:7936 + D]
        YOP = HT[0:CAPP, 8960:8960 + D]
        XO = [SCR[:, j * D:(j + 1) * D] for j in range(2)]
        H2 = [SCR[:, (2 + j) * D:(3 + j) * D] for j in range(2)]
        H2T = RING[:, 0:D].rearrange("p (k t) -> p k t", k=KD)
        JUNK = RING[:, D:2 * D]
        AFF = TMP[0:E, 0:T]
        AFT = RING[:, 2 * D:2 * D + E]
        VAL = RING[0:E, 2 * D + 64:2 * D + 64 + TOK]
        IDF = RING[0:E, 2 * D + 256:2 * D + 256 + TOK]

        def pr(name):
            return part[:, PAR[name][0]:PAR[name][1]]

        z_at = 0

        def early(n):
            nonlocal z_at
            z_at += n
            return ZF[:, z_at - n:z_at]

        small_at = 0

        def tiny(n, parts=P):
            nonlocal small_at
            small_at += n
            return small[0:parts, small_at - n:small_at]

        def per(a, n):
            return a.rearrange("p (c d n) -> p c d n", c=NC, d=2)

        wg = early(KD * 32).rearrange("p (k n) -> p k n", k=KD)
        G = early(NC * 32).rearrange("p (c n) -> p c n", c=NC)
        SPV = early(NC * 24).rearrange("p (c n) -> p c n", c=NC)
        SPE = early(NC * 24).rearrange("p (c n) -> p c n", c=NC)
        SPT = early(NC * 24).rearrange("p (c n) -> p c n", c=NC)
        SP2 = early(NC * 24).rearrange("p (c n) -> p c n", c=NC)
        SPP = early(NC * 24).rearrange("p (c n) -> p c n", c=NC)
        TOT = per(early(NC * 24), 12)
        TMC = per(early(NC * 16), 8)
        LND = early(NC * 16).rearrange("p (c n) -> p c n", c=NC)
        DRC = per(early(NC * 8), 4)
        BM = per(early(NC * 8), 4)
        WMX = per(early(NC * 8), 4)
        AL = per(tiny(NC * 24), 12)
        CS = per(tiny(NC * 24), 12)
        ECS = per(tiny(NC * 24), 12)
        WS = per(tiny(NC * 16), 8)
        DECG = per(tiny(NC * 8), 4)
        U = per(tiny(NC * 8), 4)
        MCOL = per(tiny(NC * 8), 4)
        SC = per(tiny(NC * 8), 4)
        EML = per(tiny(NC * 8), 4)
        WM = per(tiny(NC * 8), 4)
        SOLD = tiny(NC * 4).rearrange("p (d c n) -> p d c n", d=2, c=NC)
        NEGA = tiny(16)
        MPREV = tiny(2 * NC, 4).rearrange("p (d c) -> p d c", d=2)
        GROW = tiny(2 * NC, 4).rearrange("p (d c) -> p d c", d=2)
        ss, rs = tiny(NC), tiny(NC)
        ssb, rsb, halfn, den, rec, mx, esk, nmx = (tiny(8) for _ in range(8))
        mr8 = [tiny(P, 8) for _ in range(2)]
        gts, gtp = tiny(E), tiny(E, CAPP)
        assert small_at <= 1980, small_at

        def sem(name):
            return ctx.enter_context(nc.semaphore(name))

        setup = sem("setup")
        layer_sems = []

        def layer_sem(name):
            layer_sems.append(sem(name))
            return layer_sems[-1]

        par_loaded = layer_sem("par_loaded")
        wg_loaded = layer_sem("wg_loaded")
        slice_used = layer_sem("slice_used")
        ring_loaded0 = layer_sem("ring_loaded0")
        ring_loaded1 = layer_sem("ring_loaded1")
        ht_made = layer_sem("ht_made")
        x_loaded0 = layer_sem("x_loaded0")
        x_loaded1 = layer_sem("x_loaded1")
        o_made = layer_sem("o_made")
        wo_loaded = layer_sem("wo_loaded")
        a_done = layer_sem("a_done")
        x_stored = layer_sem("x_stored")
        xo_loaded0 = layer_sem("xo_loaded0")
        xo_loaded1 = layer_sem("xo_loaded1")
        op_added = layer_sem("op_added")
        n2_scaled = layer_sem("n2_scaled")
        h2_stored = layer_sem("h2_stored")
        ew_loaded0 = layer_sem("ew_loaded0")
        ew_loaded1 = layer_sem("ew_loaded1")
        down_made = layer_sem("down_made")
        pool_chain = layer_sem("pool_chain")
        squared = layer_sem("squared")
        rooted = layer_sem("rooted")
        pads_ready = layer_sem("pads_ready")
        xbc_made = layer_sem("xbc_made")
        xs_kept = layer_sem("xs_kept")
        ws_made = layer_sem("ws_made")
        state_made = layer_sem("state_made")
        dxs_made = layer_sem("dxs_made")
        csb_read = layer_sem("csb_read")
        d_masked = layer_sem("d_masked")
        y_gated = layer_sem("y_gated")
        xsd_made = layer_sem("xsd_made")
        y_squared = layer_sem("y_squared")
        y_rooted = layer_sem("y_rooted")
        mcol_made = layer_sem("mcol_made")
        v_ones = layer_sem("v_ones")
        mb_read = layer_sem("mb_read")
        md_masked = layer_sem("md_masked")
        h_summed = layer_sem("h_summed")
        h_rooted = layer_sem("h_rooted")
        a_squared = layer_sem("a_squared")
        a_rooted = layer_sem("a_rooted")
        n2_squared = layer_sem("n2_squared")
        n2_rooted = layer_sem("n2_rooted")
        idx_ready = layer_sem("idx_ready")
        g_turned = layer_sem("g_turned")
        gathered = layer_sem("gathered")
        down_scaled = layer_sem("down_scaled")
        scattered = layer_sem("scattered")
        act_chain = layer_sem("act_chain")
        scaled = layer_sem("scaled")
        softplus_exp = layer_sem("softplus_exp")
        softplus_in = layer_sem("softplus_in")
        proj_made = layer_sem("proj_made")
        conv_done = layer_sem("conv_done")
        proj_read = layer_sem("proj_read")
        wm_ready = layer_sem("wm_ready")
        xs_turned = layer_sem("xs_turned")
        tanh_done = layer_sem("tanh_done")
        dt_made = layer_sem("dt_made")
        ln_done = layer_sem("ln_done")
        cs_read = layer_sem("cs_read")
        state_exps = layer_sem("state_exps")
        mcol_read = layer_sem("mcol_read")
        m_exps = layer_sem("m_exps")
        wm_diff = layer_sem("wm_diff")
        b_turned = layer_sem("b_turned")
        b_kept = layer_sem("b_kept")
        d_exp = layer_sem("d_exp")
        z_tanh = layer_sem("z_tanh")
        y_done = layer_sem("y_done")
        mlast_row = layer_sem("mlast_row")
        mst_kept = layer_sem("mst_kept")
        md_exp = layer_sem("md_exp")
        h_done = layer_sem("h_done")
        o_tanh = layer_sem("o_tanh")
        s_shift = layer_sem("s_shift")
        p_exp = layer_sem("p_exp")
        sink_exp = layer_sem("sink_exp")
        p_turned = layer_sem("p_turned")
        p_kept = layer_sem("p_kept")
        h2t_made = layer_sem("h2t_made")
        lg_shift = layer_sem("lg_shift")
        lg_exp = layer_sem("lg_exp")
        gu_made = layer_sem("gu_made")
        hid_made = layer_sem("hid_made")
        gate_tanh = layer_sem("gate_tanh")
        down_part = layer_sem("down_part")
        dve_chain = layer_sem("dve_chain")
        ht_copied = layer_sem("ht_copied")
        gates_made = layer_sem("gates_made")
        gates_read = layer_sem("gates_read")
        al_made = layer_sem("al_made")
        cs_made = layer_sem("cs_made")
        urow_made = layer_sem("urow_made")
        rows_read = layer_sem("rows_read")
        rows_made = layer_sem("rows_made")
        mcol_kept = layer_sem("mcol_kept")
        mlast_made = layer_sem("mlast_made")
        state_kept = layer_sem("state_kept")
        csb_made = layer_sem("csb_made")
        y_made = layer_sem("y_made")
        cb_made = layer_sem("cb_made")
        w_made = layer_sem("w_made")
        kt_turned = layer_sem("kt_turned")
        mstate_made = layer_sem("mstate_made")
        wk_made = layer_sem("wk_made")
        mstate_kept = layer_sem("mstate_kept")
        mb_made = layer_sem("mb_made")
        nd_made = layer_sem("nd_made")
        mw_made = layer_sem("mw_made")
        nd_read = layer_sem("nd_read")
        a_turned = layer_sem("a_turned")
        a_normed = layer_sem("a_normed")
        a_kept = layer_sem("a_kept")
        s_made = layer_sem("s_made")
        s_read = layer_sem("s_read")
        yt_made = layer_sem("yt_made")
        yt_copied = layer_sem("yt_copied")
        op_made = layer_sem("op_made")
        lg_made = layer_sem("lg_made")
        h2t_copied = layer_sem("h2t_copied")
        aff_turned = layer_sem("aff_turned")
        aff_made = layer_sem("aff_made")
        aff_kept = layer_sem("aff_kept")
        top_done = layer_sem("top_done")
        topt_made = layer_sem("topt_made")
        g_copied = layer_sem("g_copied")
        pe_fence = layer_sem("pe_fence")
        rng = range(min(x.num for x in layer_sems), max(x.num for x in layer_sems) + 1)
        assert len(rng) == len(layer_sems)

        cbank = ps[0:AH, 0, 0:NREL]
        with nc.Block() as block:
            @block.sync
            def _(sp):
                sp.dma_start(cstt[:, :], cst[:, :]).then_inc(setup, 16)
                sp.dma_start(SCR[0:33, 0:NREL + AH], onehot[:, :]).then_inc(setup, 16)
                sp.dma_start(HT[:, 0:P], flip[:, :]).then_inc(setup, 16)
                sp.dma_start(yp[:, :], xp[:, :]).then_inc(setup, 16)
                sp.dma_start(ys[:, :], xs_in[:, :]).then_inc(setup, 16)
                sp.wait_ge(setup, 82)
                sp.dma_start(btab[:, 0:NREL], SCR[0:AH, 1024:1024 + NREL]).then_inc(setup, 16)
                sp.wait_ge(setup, 98)
                sp.dma_start(HT[:, P:P + AH * 384].rearrange("p (h k) -> p h k", h=AH),
                             bass.AP(tensor=btab.tensor, offset=0, ap=[[1, P], [512, AH], [1, 384]])).then_inc(setup, 16)
                sp.wait_ge(setup, 114)

            @block.tensor
            def _(pe):
                pe.wait_ge(setup, 80)
                pe.matmul(cbank, SCR[0:33, NREL:NREL + AH], SCR[0:33, 0:NREL],
                          start=True, stop=True).then_inc(setup, 1)
                pe.wait_ge(setup, 114)
                for h in range(AH):
                    last = pe.matmul(ps[:, 1 + h, 0:384], HT[:, 0:P], HT[:, P + 384 * h:P + 384 * (h + 1)], start=True, stop=True)
                last.then_inc(setup, 1)

            @block.vector
            def _(dve):
                dve.wait_ge(setup, 81)
                dve.tensor_copy(SCR[0:AH, 1024:1024 + NREL], cbank).then_inc(setup, 1)
                dve.wait_ge(setup, 115)
                dve.tensor_copy(bia, ps[:, 1:5, 0:384]).then_inc(setup, 1)

        def counter(eng, own):
            n = {}

            def link(ins, to=own):
                n[to.num] = n.get(to.num, 0) + 1
                ins.then_inc(to, 1)
                eng.wait_ge(to, n[to.num])

            return link

        def last_of(d):
            return P - 1 if d == 0 else 0

        with nc.Fori(0, DEPTH) as layer:
          with nc.Block() as block:
            @block.sync
            def _(sp):
                sp.dma_start(part[:, :], par[bass.ds(layer * P, P), :]).then_inc(par_loaded, 16)
                with nc.allow_non_contiguous_dma(reason="gate columns"):
                    for at, c0, w in ((0, 1792, 16), (16, 2832, 16)):
                        sp.dma_start(wg[:, :, at:at + w], wi[bass.ds(layer * D, D), c0:c0 + w]
                                     .rearrange("(k p) n -> p k n", p=P)).then_inc(wg_loaded, 16)

                def x_rows(c):
                    return yp[c * P:(c + 1) * P, :] if c < NP else ys[(c - NP) * P:(c - NP + 1) * P, :]

                def h2_rows(c):
                    return h2p[c * P:(c + 1) * P, :] if c < NP else h2s[(c - NP) * P:(c - NP + 1) * P, :]

                def ring_load(i):
                    if i >= 2:
                        sp.wait_ge(slice_used, i - 1)
                    c0 = SLICES[i][1]
                    sp.dma_start(ring[i % 2], wi[bass.ds(layer * D, D), c0:c0 + 256]
                                 .rearrange("(k p) n -> p k n", p=P)).then_inc([ring_loaded0, ring_loaded1][i % 2], 16)

                for c in range(NC):
                    if c >= 2:
                        sp.wait_ge(ht_made, 2 * (c - 1))
                    sp.dma_start(SCR[:, (c % 2) * D:(c % 2 + 1) * D], x_rows(c)).then_inc([x_loaded0, x_loaded1][c % 2], 16)
                    if c < 2:
                        ring_load(c)
                for i in range(2, len(SLICES)):
                    ring_load(i)
                sp.wait_ge(o_made, NC)
                sp.dma_start(WO, wo[bass.ds(layer * D, D), :].rearrange("(k p) n -> p k n", p=P)).then_inc(wo_loaded, 16)
                sp.wait_ge(a_done, NC)
                for c in range(NC + 1):
                    if c < NC:
                        if c >= 2:
                            sp.wait_ge(x_stored, 16 * (c - 1))
                        sp.dma_start(XO[c % 2], x_rows(c)).then_inc([xo_loaded0, xo_loaded1][c % 2], 16)
                    if c >= 1:
                        sp.wait_ge(op_added, 2 * c)
                        if c >= 2:
                            sp.wait_ge(x_stored, 16 * (c - 1))
                        sp.dma_start(x_rows(c - 1), XO[(c - 1) % 2]).then_inc(x_stored, 16)
                        sp.wait_ge(n2_scaled, c)
                        if c >= 2:
                            sp.wait_ge(h2_stored, 16 * (c - 1))
                        sp.dma_start(h2_rows(c - 1), H2[(c - 1) % 2]).then_inc(h2_stored, 16)
                sp.wait_ge(x_stored, 16 * NC)
                sp.wait_ge(h2_stored, 16 * NC)

                def expert_load(e):
                    done = [ew_loaded0, ew_loaded1][e % 2]
                    for dst, src, rows in ((EG, wga, D), (EU, wup, D), (ED, wdn, FF)):
                        sp.dma_start(dst[e % 2], src[bass.ds(layer * (E * rows) + e * rows, rows), :]
                                     .rearrange("(k p) n -> p k n", p=P)).then_inc(done, 16)

                for e in range(E):
                    if e >= 2:
                        sp.wait_ge(down_made, e - 1)
                    expert_load(e)

            @block.gpsimd
            def _(pool):
                link = counter(pool, pool_chain)

                def rroot(out, src, n, mul, eps, wait, to):
                    link(pool.tensor_scalar(out[:, 0:n], src[:, 0:n], mul, eps, ALU.mult, ALU.add))
                    link(pool.tensor_tensor(out[:, 0:n], out[:, 0:n], halfn[:, 0:n], ALU.pow), to)

                link(pool.memset(halfn, -0.5))
                for c in range(NC):
                    pool.wait_ge(squared, c + 1)
                    rroot(rs[:, c:c + 1], ss[:, c:c + 1], 1, 1.0 / D, EPS, None, rooted)
                pool.wait_ge(ht_made, 2 * NC)
                for r in RAW:
                    for a, b in ((0, 2), (258, 260), (1284, 1286)):
                        link(pool.memset(r[:, a:b], 0.0), pads_ready)
                pool.wait_ge(xbc_made, 6)
                pool.wait_ge(xs_kept, 12)
                pool.wait_ge(ws_made, 1)
                for i in range(NC):
                    if i >= 2:
                        pool.wait_ge(state_made, i - 1)
                    for d in range(2):
                        c = scan_chunk(d, i)
                        link(pool.tensor_tensor(DXS[:, i % 2, d, :].rearrange("p (h e) -> p h e", h=SH),
                                                XS[:, c, :].rearrange("p (h e) -> p h e", h=SH),
                                                WS[:, c, d, :].unsqueeze(2).to_broadcast([P, SH, HD]), ALU.mult), dxs_made)
                for c in range(NC):
                    for d in range(2):
                        pool.wait_ge(csb_read, 2 * c + d + 1)
                        v = DM[:, c % 2, d, :].rearrange("p (h t) -> p h t", h=SH)
                        sgn = 1 if d == 0 else -1
                        link(pool.affine_select(out=v, in_=v, compare_op=ALU.is_ge, fill=NEG, base=0,
                                                pattern=[[0, SH], [sgn, P]], channel_multiplier=-sgn), d_masked)
                    if c >= 1:
                        pool.wait_ge(y_gated, c)
                    link(pool.tensor_tensor(TMP[:, 0:512].rearrange("p (h e) -> p h e", h=SH),
                                            XS[:, c, :].rearrange("p (h e) -> p h e", h=SH),
                                            pr("dskip").unsqueeze(2).to_broadcast([P, SH, HD]), ALU.mult), xsd_made)
                    pool.wait_ge(y_squared, c + 1)
                    rroot(rsb, ssb, 1, 1.0 / 512, 4 * EPS, None, y_rooted)
                pool.wait_ge(mcol_made, 1)
                link(pool.memset(V[:, :, :, HD:HD + 1], 1.0), v_ones)
                for c in range(NC):
                    for d in range(2):
                        pool.wait_ge(mb_read, 2 * c + d + 1)
                        v = DMM[:, c % 2, d]
                        sgn = 1 if d == 0 else -1
                        link(pool.affine_select(out=v, in_=v, compare_op=ALU.is_ge, fill=NEG, base=0,
                                                pattern=[[0, MH], [sgn, P]], channel_multiplier=-sgn), md_masked)
                    pool.wait_ge(h_summed, c + 1)
                    rroot(rsb, ssb, MH, 4.0 / HD, 4 * EPS, None, h_rooted)
                for c in range(NC):
                    pool.wait_ge(a_squared, c + 1)
                    rroot(rsb, ssb, 6, 1.0 / HD, EPS, None, a_rooted)
                for c in range(NC):
                    pool.wait_ge(n2_squared, c + 1)
                    rroot(rsb, ssb, 1, 1.0 / D, EPS, None, n2_rooted)
                pool.wait_ge(idx_ready, 1)
                pool.wait_ge(h2_stored, 16 * NC)
                pool.wait_ge(x_stored, 16 * NC)

                def gather(e):
                    if e >= 2:
                        pool.wait_ge(g_turned, 3 * (e - 1))
                        pool.wait_ge(gathered, 32 * (e - 1))
                    pool.indirect_dma_start(XG[e % 2], None, h2s[:, :], bass.IndirectOffsetOnAxis(ap=idxs[:, e:e + 1], axis=0)
                                            ).then_inc(gathered, 16)
                    pool.indirect_dma_start(XGP[e % 2], None, h2p[:, :], bass.IndirectOffsetOnAxis(ap=idxp[:, e:e + 1], axis=0)
                                            ).then_inc(gathered, 16)

                gather(0)
                for e in range(E):
                    if e + 1 < E:
                        pool.wait_ge(gathered, 32 * (e + 1))
                        gather(e + 1)
                    pool.wait_ge(down_scaled, 4 * (e + 1))
                    if e >= 1:
                        pool.wait_ge(scattered, 32 * e)
                    pool.indirect_dma_start(ys[:, :], bass.IndirectOffsetOnAxis(ap=idxs[:, e:e + 1], axis=0), YO, None,
                                            compute_op=ALU.add, bounds_check=SEQS[1] - 1).then_inc(scattered, 16)
                    pool.indirect_dma_start(yp[:, :], bass.IndirectOffsetOnAxis(ap=idxp[:, e:e + 1], axis=0), YOP, None,
                                            compute_op=ALU.add, bounds_check=SEQS[0] - 1).then_inc(scattered, 16)
                pool.wait_ge(scattered, 32 * E)

            @block.scalar
            def _(act):
                link = counter(act, act_chain)
                for c in range(NC):
                    x = SCR[:, (c % 2) * D:(c % 2 + 1) * D]
                    act.wait_ge([x_loaded0, x_loaded1][c % 2], 16 * (c // 2 + 1))
                    link(act.activation(XSF[:, 0:D], x, ACT.Square, accum_out=ss[:, c:c + 1]), squared)
                    act.wait_ge(rooted, c + 1)
                    link(act.mul(x, x, rs[:, c:c + 1]), scaled)
                act.wait_ge(par_loaded, 16)
                link(act.activation(NEGA, pr("alog"), ACT.Exp), softplus_exp)
                act.wait_ge(softplus_in, 1)
                link(act.activation(SPE, SPE, ACT.Exp, scale=-1.0), softplus_exp)

                def evac(u):
                    sl, kind, f, g = UNITS[u]
                    act.wait_ge(proj_made, u + 1)
                    src = ps[:, u % 2, :]
                    if kind == "xbc":
                        t0, n = GROUPS[g]
                        if g == 0 and f >= 2:
                            act.wait_ge(conv_done, f - 1)
                        if g == 0 and f < 2:
                            act.wait_ge(pads_ready, 6)
                        if g == 0:
                            link(act.copy(RAW[f % 2][:, 2:258], src[:, 0:256]))
                            link(act.copy(RAW[f % 2][:, 260:516], src[:, 256:512]), proj_read)
                        else:
                            link(act.copy(RAW[f % 2][:, t0 + 4:t0 + 4 + n], src[:, 0:n]), proj_read)
                    elif kind == "z":
                        if u == U_Z:
                            act.wait_ge(wm_ready, 1)
                        link(act.copy(Z[:, g, f * 256:(f + 1) * 256], src[:, 0:256]), proj_read)
                    elif kind == "qk":
                        t0, n = GROUPS[g]
                        link(act.mul(QK[:, f, t0:t0 + n], src[:, 0:n], 1.0 if f < 2 else HD ** -0.5), proj_read)
                    elif kind == "v":
                        link(act.copy(V[:, g, :, 0:HD], src[:, 0:256].rearrange("p (h e) -> p h e", h=MH)), proj_read)
                    elif kind == "o":
                        link(act.copy(O[:, g, :], src[:, 0:256]), proj_read)
                    else:
                        link(act.copy(Z[:, g, f * 256:(f + 1) * 256], src[:, 0:256]), proj_read)

                def conv_tanh(f):
                    act.wait_ge(conv_done, f + 1)
                    if f >= 2:
                        act.wait_ge(xs_turned, 3 * min(f - 1, 4))
                        if f >= 2:
                            act.wait_ge(xbc_made, f - 1)
                    link(act.activation(XF[f % 2][:, 0:1282], ACC[f % 2][:, 0:1282], ACT.Tanh, scale=0.5), tanh_done)

                def keep_xs(f):
                    for j, (c0, n) in enumerate(((0, 4), (4, 4), (8, 2))):
                        act.wait_ge(xs_turned, 3 * f + j + 1)
                        link(act.copy(XS[:, c0:c0 + n, f * P:(f + 1) * P],
                                      ps[:, 2 + j % 2, 0:n * P].rearrange("p (c n) -> p c n", c=n)), xs_kept)

                for u in range(0, 3):
                    evac(u)
                act.wait_ge(dt_made, 1)
                link(act.activation(LND, LND, ACT.Ln), ln_done)
                for u in range(3, 6):
                    evac(u)
                conv_tanh(0)
                act.wait_ge(cs_read, 1)
                link(act.activation(ECS, CS, ACT.Exp))
                link(act.activation(TMC, TMC, ACT.Exp))
                for g in range(2):
                    link(act.activation(DECG[64 * g:64 * g + 64], TOT[64 * g:64 * g + 64, :, :, 4 * g:4 * g + 4], ACT.Exp),
                         state_exps)
                for u in range(6, 9):
                    evac(u)
                conv_tanh(1)
                keep_xs(0)
                for u in range(9, 12):
                    evac(u)
                conv_tanh(2)
                act.wait_ge(mcol_read, 1)
                link(act.activation(SC, DRC, ACT.Exp, scale=-1.0))
                link(act.activation(EML, BM, ACT.Exp, scale=-1.0), m_exps)
                keep_xs(1)
                for u in range(12, 15):
                    evac(u)
                conv_tanh(3)
                act.wait_ge(wm_diff, 1)
                link(act.activation(WM, WMX, ACT.Exp), wm_ready)
                keep_xs(2)
                for u in range(15, 18):
                    evac(u)
                conv_tanh(4)
                keep_xs(3)
                conv_tanh(5)
                act.wait_ge(xbc_made, 6)
                for j, (c0, n) in enumerate(((0, 4), (4, 4), (8, 2))):
                    act.wait_ge(b_turned, j + 1)
                    link(act.copy(BT[:, c0:c0 + n, :], ps[:, 2 + j % 2, 0:n * P].rearrange("p (c n) -> p c n", c=n)), b_kept)
                for i in range(NC):
                    evac(U_Z + 2 * i)
                    evac(U_Z + 2 * i + 1)
                for c in range(NC):
                    for d in range(2):
                        act.wait_ge(d_masked, 2 * c + d + 1)
                        link(act.activation(DM[:, c % 2, d, :], DM[:, c % 2, d, :], ACT.Exp), d_exp)
                    if c >= 1:
                        act.wait_ge(y_gated, c)
                    link(act.activation(TMP[:, 1024:1536], Z[:, c, :], ACT.Tanh, scale=0.5), z_tanh)
                    for u in range(U_QK + 3 * c, U_QK + 3 * c + 3):
                        evac(u)
                    act.wait_ge(y_gated, c + 1)
                    link(act.activation(ZF[:, c * 512:(c + 1) * 512], XS[:, c, :], ACT.Square,
                                        accum_out=ssb[:, 0:1]), y_squared)
                    act.wait_ge(y_rooted, c + 1)
                    link(act.mul(XS[:, c, :], XS[:, c, :], rsb[:, 0:1]), y_done)
                evac(U_ATT - 2)
                evac(U_ATT - 1)
                for i in range(NC):
                    evac(U_ATT + 2 * i)
                    evac(U_ATT + 2 * i + 1)
                for c in range(NC):
                    act.wait_ge(mlast_row, c + 1)
                    link(act.copy(mr8[c % 2], ps[0:8, 0, 0:P]), mst_kept)
                    for d in range(2):
                        act.wait_ge(md_masked, 2 * c + d + 1)
                        link(act.activation(DMM[:, c % 2, d], DMM[:, c % 2, d], ACT.Exp), md_exp)
                    if c >= 1:
                        act.wait_ge(h_done, c)
                    link(act.activation(TMP[:, 1280:1536], O[:, c, :], ACT.Tanh, scale=0.5), o_tanh)
                for c in range(NC):
                    nk, c0 = attn_keys(c)
                    act.wait_ge(s_shift, c + 1)
                    for h in range(AH):
                        v = PSC[c % 2][:, h, 0:nk * P]
                        link(act.activation(v, v, ACT.Exp, bias=nmx[:, h:h + 1], accum_out=den[:, h:h + 1]), p_exp)
                    link(act.activation(esk[:, 0:4], esk[:, 0:4], ACT.Exp), sink_exp)
                    for h in range(AH):
                        act.wait_ge(p_turned, AH * c + h + 1)
                        link(act.copy(TMP[:, h * 384:h * 384 + nk * P], ps[:, 6 + h % 2, 0:nk * P]), p_kept)
                for c in range(NC):
                    act.wait_ge(op_added, 2 * c + 2)
                    link(act.activation(JUNK, XO[c % 2], ACT.Square, accum_out=ssb[:, 0:1]), n2_squared)
                    act.wait_ge(n2_rooted, c + 1)
                    if c >= 2:
                        act.wait_ge(h2_stored, 16 * (c - 1))
                        act.wait_ge(h2t_made, 2 * (c - 1))
                    link(act.mul(H2[c % 2], XO[c % 2], rsb[:, 0:1]), n2_scaled)
                    act.wait_ge(lg_shift, c + 1)
                    link(act.activation(AFT, AFT, ACT.Exp, accum_out=den[:, 0:1]), lg_exp)
                for e in range(E):
                    for f in range(KF):
                        act.wait_ge(gu_made, KF * e + f + 1)
                        act.wait_ge(hid_made, KF * e + f) if e + f else None
                        link(act.activation(THG, ps[:, 2 + f % 2, 0:TOK], ACT.Tanh, scale=0.5), gate_tanh)
                    if e >= 1:
                        act.wait_ge(scattered, 32 * e)
                    for j in range(4):
                        act.wait_ge(down_part, 4 * e + j + 1)
                        hf = j % 2
                        if j < 2:
                            link(act.mul(YO[:, hf * 512:(hf + 1) * 512], ps[:, 4 + j, :], gts[:, e:e + 1]), down_scaled)
                        else:
                            link(act.mul(YOP[:, hf * 512:(hf + 1) * 512], ps[0:CAPP, 4 + j, :], gtp[:, e:e + 1]), down_scaled)

            @block.vector
            def _(dve):
                link = counter(dve, dve_chain)

                def tt(out, a, b, op, to=dve_chain):
                    link(dve.tensor_tensor(out, a, b, op), to)

                def ts(out, a, x, y, op0, op1=None, to=dve_chain):
                    if op1 is None:
                        link(dve.tensor_scalar(out, a, x, None, op0), to)
                    else:
                        link(dve.tensor_scalar(out, a, x, y, op0, op1), to)

                def stt(out, a, x, b, op0, op1, to=dve_chain):
                    link(dve.scalar_tensor_tensor(out=out, in0=a, scalar=x, in1=b, op0=op0, op1=op1), to)

                def wide(a, n):
                    return a.unsqueeze(2).to_broadcast([a.shape[0], a.shape[1], n])

                def quarter(b):
                    return ps[:, b, :].rearrange("p (k t) -> p k t", k=4)

                dve.wait_ge(par_loaded, 16)
                for c in range(NC):
                    for j in range(2):
                        dve.wait_ge(ht_made, 2 * c + j + 1)
                        tt(hT[:, 4 * j:4 * j + 4, c * P:(c + 1) * P], quarter(2 + j), wide(pr("gmix")[:, 4 * j:4 * j + 4], P),
                           ALU.mult, ht_copied)
                dve.wait_ge(gates_made, 1)
                tt(G, ps[:, 4, 0:NC * 32].rearrange("p (c n) -> p c n", c=NC),
                   pr("gbias").unsqueeze(1).to_broadcast([P, NC, 32]), ALU.add, gates_read)
                link(dve.tensor_copy(SPV[:, :, 0:16], G[:, :, 0:16]))
                ts(SPV[:, :, 16:24], G[:, :, 24:32], -1.0, None, ALU.mult)
                ts(SPT, SPV, -1.0, None, ALU.mult)
                tt(SPE, SPV, SPT, ALU.max, softplus_in)
                dve.wait_ge(softplus_exp, 2)
                ts(SPT, SPE, 2.0, None, ALU.add)
                link(dve.reciprocal(SPT, SPT))
                tt(SPT, SPE, SPT, ALU.mult)
                tt(SP2, SPT, SPT, ALU.mult)
                ts(SPP, SP2, 1.0 / 17, None, ALU.mult)
                for k in (15, 13, 11, 9, 7, 5, 3):
                    stt(SPP, SPP, 1.0 / k, SP2, ALU.add, ALU.mult)
                stt(SPP, SPP, 1.0, SPT, ALU.add, ALU.mult)
                ts(SPP, SPP, 2.0, None, ALU.mult)
                stt(SPV, SPV, 0.0, SPP, ALU.max, ALU.add)
                ts(LND, SPV[:, :, 0:16], 1e-19, None, ALU.max, to=dt_made)
                ts(NEGA, NEGA, -1.0, None, ALU.mult)
                for d in range(2):
                    tt(AL[:, :, d, 0:8], SPV[:, :, 8 * d:8 * d + 8], NEGA[:, 8 * d:8 * d + 8].unsqueeze(1).to_broadcast([P, NC, 8]),
                       ALU.mult)
                    ts(AL[:, :, d, 8:12], SPV[:, :, 16 + 4 * d:20 + 4 * d], -1.0, None, ALU.mult, to=al_made)

                def conv(f):
                    dve.wait_ge(proj_read, 3 * f + 3)
                    if f >= 2:
                        dve.wait_ge(tanh_done, f - 1)
                    w = pr("convw")[:, 5 * f:5 * f + 5]
                    raw, acc = RAW[f % 2], ACC[f % 2][:, 0:1282]
                    ts(acc, raw[:, 0:1282], w[:, 0:1], pr("convb")[:, f:f + 1], ALU.mult, ALU.add)
                    for j in range(1, 5):
                        stt(acc, raw[:, j:j + 1282], w[:, j:j + 1], acc, ALU.mult, ALU.add,
                            conv_done if j == 4 else dve_chain)

                def silu(f):
                    dve.wait_ge(tanh_done, f + 1)
                    th = XF[f % 2][:, 0:1282]
                    ts(th, th, 0.5, 0.5, ALU.mult, ALU.add)
                    out = th if f < 4 else BC[:, f - 4, 0:1282]
                    tt(out, th, ACC[f % 2][:, 0:1282], ALU.mult, xbc_made)

                conv(0)
                dve.wait_ge(cs_made, 1)
                link(dve.tensor_copy(CS, ps[:, 5, 0:240].rearrange("p (c d n) -> p c d n", c=NC, d=2)))
                link(dve.tensor_copy(TOT, ps[:, 6, 0:240].rearrange("p (c d n) -> p c d n", c=NC, d=2)))
                tt(TMC, TOT[:, :, :, 0:8], CS[:, :, :, 0:8], ALU.subtract)
                for d in range(2):
                    tt(U[:, :, d, :], G[:, :, 16 + 4 * d:20 + 4 * d], CS[:, :, d, 8:12], ALU.subtract,
                       cs_read if d == 1 else dve_chain)
                conv(1)
                silu(0)
                dve.wait_ge(state_exps, 2)
                for d in range(2):
                    tt(WS[:, :, d, :], TMC[:, :, d, :], SPV[:, :, 8 * d:8 * d + 8], ALU.mult, ws_made if d == 1 else dve_chain)
                dve.wait_ge(ln_done, 1)
                for d in range(2):
                    tt(CS[:, :, d, 0:8], CS[:, :, d, 0:8], LND[:, :, 8 * d:8 * d + 8], ALU.subtract)
                dve.wait_ge(urow_made, 1)
                for d in range(2):
                    for j, (t0, n) in enumerate(GROUPS):
                        link(dve.tensor_copy(UROW[:, d, t0:t0 + n], ps[0:4, 2 + 3 * d + j, 0:n]))
                link(dve.tensor_copy(GROW, ps[0:4, 4, 256:276].rearrange("p (d c) -> p d c", d=2)), rows_read)
                for d in range(2):
                    for i in range(NC):
                        c = scan_chunk(d, i)
                        u, m = UROW[:, d, c * P:(c + 1) * P], MROW[:, d, c * P:(c + 1) * P]
                        if i in (0, NP):
                            link(dve.memset(MPREV[:, d, c:c + 1], NEG))
                        if d == 1:
                            u, m = u[:, ::-1], m[:, ::-1]
                        link(dve.tensor_tensor_scan(m, u, u, MPREV[:, d, c:c + 1], ALU.max, ALU.max))
                        if has_next(i):
                            cn = scan_chunk(d, i + 1)
                            tt(MPREV[:, d, cn:cn + 1], GROW[:, d, c:c + 1], m[:, P - 1:P], ALU.add)
                for d in range(2):
                    tt(UROW[:, d, :].rearrange("p (c t) -> p c t", c=NC), MROW[:, d, :].rearrange("p (c t) -> p c t", c=NC),
                       MPREV[:, d, :].unsqueeze(2).to_broadcast([4, NC, P]), ALU.subtract, rows_made)
                conv(2)
                silu(1)
                dve.wait_ge(mcol_made, 1)
                link(dve.tensor_copy(MCOL, ps[:, 5, 0:80].rearrange("p (c d n) -> p c d n", c=NC, d=2)), mcol_kept)
                link(dve.tensor_copy(DRC, ps[:, 5, 80:160].rearrange("p (c d n) -> p c d n", c=NC, d=2)))
                tt(BM, MCOL, CS[:, :, :, 8:12], ALU.add, mcol_read)
                conv(3)
                silu(2)
                dve.wait_ge(mlast_made, 1)
                tt(WMX, U, ps[:, 6, 0:80].rearrange("p (c d n) -> p c d n", c=NC, d=2), ALU.subtract, wm_diff)
                link(dve.tensor_copy(SOLD, ps[:, 6, 256:296].rearrange("p (d c n) -> p d c n", d=2, c=NC)))
                conv(4)
                silu(3)
                conv(5)
                silu(4)
                silu(5)
                link(dve.memset(PREV[:, 0, 0, :], 0.0))
                link(dve.memset(PREV[:, 0, NP, :], 0.0))
                link(dve.memset(PREV[:, 1, NP - 1, :], 0.0))
                link(dve.memset(PREV[:, 1, NC - 1, :], 0.0))
                for i in range(NC):
                    dve.wait_ge(state_made, i + 1)
                    if has_next(i):
                        for d in range(2):
                            c, cn = scan_chunk(d, i), scan_chunk(d, i + 1)
                            tt(TMP[:, 0:256].rearrange("p (h e) -> p h e", h=4), PREV[:, d, c, :].rearrange("p (h e) -> p h e", h=4),
                               wide(DECG[:, c, d, :], HD), ALU.mult)
                            tt(PREV[:, d, cn, :], ps[:, 4, 256 * d:256 * d + 256], TMP[:, 0:256], ALU.add,
                               state_kept if d == 1 else dve_chain)
                    else:
                        ts(TMP[:, 256:257], ones1, 1.0, None, ALU.mult, to=state_kept)

                def heads(a, h=SH):
                    return a.rearrange("p (h e) -> p h e", h=h)

                def ssd_exponents(c):
                    for d in range(2):
                        dve.wait_ge(csb_made, 2 * c + d + 1)
                        if c >= 2:
                            dve.wait_ge(y_made, c - 1)
                        tt(DM[:, c % 2, d, :].rearrange("p (h t) -> p h t", h=SH),
                           ps[:, 2:4, :].rearrange("p b (h t) -> p (b h) t", h=4),
                           wide(CS[:, c, d, 0:8], P), ALU.subtract, csb_read)

                def ssd_weights(c):
                    dve.wait_ge(cb_made, c + 1)
                    for d in range(2):
                        dve.wait_ge(d_exp, 2 * c + d + 1)
                        cb = ps[:, 4, 0:256].rearrange("p (g t) -> p g t", g=2)
                        for g in range(2):
                            v = DM[:, c % 2, d, g * 512:(g + 1) * 512].rearrange("p (h t) -> p h t", h=4)
                            tt(v, v, cb[:, g, :].unsqueeze(1).to_broadcast([P, 4, P]), ALU.mult, w_made)

                def ssd_output(c):
                    dve.wait_ge(y_made, c + 1)
                    dve.wait_ge(xsd_made, c + 1)
                    dve.wait_ge(z_tanh, c + 1)
                    y, t, zt = TMP[:, 0:512], TMP[:, 512:1024], TMP[:, 1024:1536]
                    tt(y, ps[:, 5, :], y, ALU.add)
                    for d in range(2):
                        tt(t.rearrange("p (g h e) -> p g h e", g=2, h=4),
                           ps[:, 6:8, 256 * d:256 * d + 256].rearrange("p g (h e) -> p g h e", h=4),
                           ECS[:, c, d, 0:8].rearrange("p (g h) -> p g h", g=2).unsqueeze(3).to_broadcast([P, 2, 4, HD]), ALU.mult)
                        tt(y, y, t, ALU.add)
                    stt(zt, zt, 1.0, Z[:, c, :], ALU.add, ALU.mult)
                    tt(XS[:, c, :], y, zt, ALU.mult, y_gated)

                ssd_exponents(0)
                for c in range(NC):
                    ssd_weights(c)
                    if c + 1 < NC:
                        ssd_exponents(c + 1)
                    ssd_output(c)
                dve.wait_ge(y_done, NC)
                for d, c in ((0, 0), (0, NP), (1, NP - 1), (1, NC - 1)):
                    link(dve.memset(PREVM[:, d, c], 0.0))
                for i in range(NC):
                    for d in range(2):
                        c = scan_chunk(d, i)
                        dve.wait_ge(kt_turned, i + 1)
                        if i >= 1 and d == 0:
                            dve.wait_ge(mstate_made, i)
                        tt(TMP[:, 256 * d:256 * d + 256].rearrange("p (h e) -> p h e", h=4),
                           ps[:, 4, 256 * d:256 * d + 256].rearrange("p (h e) -> p h e", h=4),
                           wide(WM[:, c, d, :], HD), ALU.mult, wk_made)
                    dve.wait_ge(mstate_made, i + 1)
                    if has_next(i):
                        for d in range(2):
                            c, cn = scan_chunk(d, i), scan_chunk(d, i + 1)
                            tmp = TMP[:, 512:642].rearrange("p (h e) -> p h e", h=2)
                            tt(tmp, PREVM[:, d, c], wide(SOLD[:, d, c, :], 65), ALU.mult)
                            tt(PREVM[:, d, cn], ps[:, 5, 256 * d:256 * d + 130].rearrange("p (h e) -> p h e", h=2), tmp, ALU.add,
                               mstate_kept)

                def ml_exponents(c):
                    for d in range(2):
                        dve.wait_ge(mb_made, 2 * c + d + 1)
                        if c >= 2:
                            dve.wait_ge(nd_made, c - 1)
                        tt(DMM[:, c % 2, d], wide(U[:, c, d, :], P), quarter(3), ALU.subtract, mb_read)

                def ml_weights(c):
                    for d in range(2):
                        dve.wait_ge(md_exp, 2 * c + d + 1)
                        tt(DMM[:, c % 2, d], DMM[:, c % 2, d], quarter(2), ALU.mult, mw_made)

                def ml_output(c):
                    dve.wait_ge(nd_made, c + 1)
                    nd, t = heads(TMP[:, 0:260], 4), heads(TMP[:, 260:520], 4)
                    hs, hd = heads(TMP[:, 520:776], 4), heads(TMP[:, 776:1032], 4)
                    for d in range(2):
                        tt(t.rearrange("p (j q) e -> p q j e", q=2),
                           ps[:, 4:8:3, 130 * d:130 * d + 130].rearrange("p q (j e) -> p q j e", j=2),
                           SC[:, c, d, :].rearrange("p (j q) -> p q j", q=2).unsqueeze(3).to_broadcast([P, 2, 2, 65]), ALU.mult)
                        tt(nd, heads(ps[:, 5 + d, 0:260], 4), t, ALU.add, nd_read)
                        dn = den[:, 0:4]
                        ts(dn, nd[:, :, HD:HD + 1].rearrange("p h e -> p (h e)"), -1.0, None, ALU.mult)
                        tt(dn, dn, nd[:, :, HD:HD + 1].rearrange("p h e -> p (h e)"), ALU.max)
                        tt(dn, dn, EML[:, c, d, :], ALU.max)
                        link(dve.reciprocal(rec[:, 0:4], dn))
                        tt(hd if d else hs, nd[:, :, 0:HD], wide(rec[:, 0:4], HD), ALU.mult)
                    tt(hs, hs, hd, ALU.add)
                    tt(hd, hs, hs, ALU.mult)
                    link(dve.tensor_reduce(out=ssb[:, 0:4], in_=hd, axis=AX, op=ALU.add), h_summed)
                    dve.wait_ge(h_rooted, c + 1)
                    tt(hs, hs, wide(rsb[:, 0:4], HD), ALU.mult)
                    dve.wait_ge(o_tanh, c + 1)
                    stt(O[:, c, :], TMP[:, 1280:1536], 1.0, TMP[:, 520:776], ALU.add, ALU.mult, h_done)

                ml_exponents(0)
                for c in range(NC):
                    ml_weights(c)
                    if c + 1 < NC:
                        ml_exponents(c + 1)
                    ml_output(c)
                dve.wait_ge(proj_read, len(UNITS))
                dve.wait_ge(h_done, NC)
                for c in range(NC):
                    qk, sq = Z[:, c, 0:384], TMP[:, 0:384]
                    if c >= 1:
                        dve.wait_ge(a_turned, c)
                    tt(sq, qk, qk, ALU.mult)
                    link(dve.tensor_reduce(out=ssb[:, 0:6], in_=heads(sq, 6), axis=AX, op=ALU.add), a_squared)
                    dve.wait_ge(a_rooted, c + 1)
                    tt(TMP[:, 0:256].rearrange("p (j g e) -> p g j e", j=2, g=2),
                       Z[:, c, 0:256].rearrange("p (g j e) -> p g j e", j=2, g=2),
                       rsb[:, 0:4].rearrange("p (g j) -> p g j", g=2).unsqueeze(3).to_broadcast([P, 2, 2, HD]), ALU.mult)
                    tt(heads(TMP[:, 256:384], 2), heads(Z[:, c, 256:384], 2), wide(rsb[:, 4:6], HD), ALU.mult, a_normed)
                    dve.wait_ge(a_turned, c + 1)
                    ts(QT[:, :, c * P:(c + 1) * P], ps[:, 7, 0:256].rearrange("p (j t) -> p j t", j=2), pr("qg"), HD ** -0.5,
                       ALU.mult, ALU.mult)
                    ts(KT[:, c * P:(c + 1) * P], ps[:, 7, 256:384], pr("kg"), None, ALU.mult, to=a_kept)
                for c in range(NC):
                    nk, c0 = attn_keys(c)
                    b0 = (c0 - c + 1) * P
                    dve.wait_ge(s_made, c + 1)
                    v = PSC[c % 2][:, :, 0:nk * P]
                    if c >= 2:
                        dve.wait_ge(p_turned, AH * (c - 1))
                    tt(v, ps[:, 2:6, 0:nk * P], bia[:, :, b0:b0 + nk * P], ALU.add, s_read)
                    link(dve.tensor_reduce(out=mx[:, 0:4], in_=v, axis=AX, op=ALU.max))
                    tt(mx[:, 0:4], mx[:, 0:4], pr("sink"), ALU.max)
                    tt(esk[:, 0:4], pr("sink"), mx[:, 0:4], ALU.subtract)
                    ts(nmx[:, 0:4], mx[:, 0:4], -1.0, None, ALU.mult, to=s_shift)
                    dve.wait_ge(sink_exp, c + 1)
                    tt(rec[:, 0:4], den[:, 0:4], esk[:, 0:4], ALU.add)
                    link(dve.reciprocal(rec[:, 0:4], rec[:, 0:4]))
                    dve.wait_ge(o_made, c + 1)
                    tt(heads(Z[:, c, 0:256], 4), heads(ps[:, c % 2, 0:256], 4), wide(rec[:, 0:4], HD), ALU.mult, a_done)
                for c in range(NC):
                    for j in range(2):
                        dve.wait_ge(yt_made, 2 * c + j + 1)
                        tt(hT[:, 4 * j:4 * j + 4, c * P:(c + 1) * P], quarter(2 + j), wide(pr("gy")[:, 4 * j:4 * j + 4], P),
                           ALU.mult, yt_copied)
                for c in range(NC):
                    dve.wait_ge([xo_loaded0, xo_loaded1][c % 2], 16 * (c // 2 + 1))
                    for hf in range(2):
                        dve.wait_ge(op_made, 2 * c + hf + 1)
                        tt(XO[c % 2][:, hf * 512:(hf + 1) * 512], ps[:, hf, :], XO[c % 2][:, hf * 512:(hf + 1) * 512], ALU.add,
                           op_added)
                    if c >= 1:
                        dve.wait_ge(lg_made, c)
                    for j in range(2):
                        dve.wait_ge(h2t_made, 2 * c + j + 1)
                        tt(H2T[:, 4 * j:4 * j + 4, :], quarter(4 + j), wide(pr("gffn")[:, 4 * j:4 * j + 4], P), ALU.mult, h2t_copied)
                    dve.wait_ge(lg_made, c + 1)
                    if c >= 1:
                        dve.wait_ge(aff_turned, c)
                    link(dve.tensor_reduce(out=mx[:, 0:1], in_=ps[:, 6, 0:E], axis=AX, op=ALU.max))
                    ts(AFT, ps[:, 6, 0:E], mx[:, 0:1], None, ALU.subtract, to=lg_shift)
                    dve.wait_ge(lg_exp, c + 1)
                    link(dve.reciprocal(rec[:, 0:1], den[:, 0:1]))
                    ts(AFT, AFT, rec[:, 0:1], None, ALU.mult, to=aff_made)
                    dve.wait_ge(aff_turned, c + 1)
                    link(dve.tensor_copy(AFF[:, c * P:(c + 1) * P], ps[0:E, 7, 0:P]), aff_kept)
                for a, w, v0, n in ((0, SEQS[0], CAPS, CAPP), (SEQS[0], SEQS[1], 0, CAPS)):
                    row = AFF[:, a:a + w]
                    for r in range(n // 8):
                        v8 = VAL[:, v0 + 8 * r:v0 + 8 * r + 8]
                        link(dve.max(v8, row))
                        link(dve.max_index(idxu[:, v0 + 8 * r:v0 + 8 * r + 8], v8, row))
                        if r + 1 < n // 8:
                            link(dve.match_replace(row, v8, row, -1.0))
                link(dve.tensor_copy(IDF, idxu[:, :]), top_done)
                dve.wait_ge(topt_made, 1)
                link(dve.tensor_copy(idxs[:, :], ps[:, 7, 0:E]))
                link(dve.tensor_copy(idxp[:, :], ps[0:CAPP, 7, E:2 * E]))
                ts(gts, ps[:, 7, 2 * E:3 * E], 0.5, None, ALU.mult)
                ts(gtp, ps[0:CAPP, 7, 3 * E:4 * E], 0.5, None, ALU.mult, to=idx_ready)

                def copy_tokens(e):
                    for j, (k0, n) in enumerate(((0, 3), (3, 3), (6, 2))):
                        dve.wait_ge(g_turned, 3 * e + j + 1)
                        tt(XT[e % 2][:, k0:k0 + n, :], ps[:, j % 2, 0:n * TOK].rearrange("p (k t) -> p k t", k=n),
                           wide(pr("gffn")[:, k0:k0 + n], TOK), ALU.mult, g_copied)

                copy_tokens(0)
                for e in range(E):
                    for f in range(KF):
                        dve.wait_ge(gate_tanh, KF * e + f + 1)
                        if f == 0 and e >= 1:
                            dve.wait_ge(down_made, e)
                        stt(HID[:, f, :], THG, 1.0, ps[:, 2 + f % 2, 0:TOK], ALU.add, ALU.mult)
                        tt(HID[:, f, :], HID[:, f, :], ps[:, 2 + f % 2, TOK:2 * TOK], ALU.mult, hid_made)
                    if e + 1 < E:
                        copy_tokens(e + 1)

            @block.tensor
            def _(pe):
                fence = counter(pe, pe_fence)

                def mm(out, a, b, start=True, stop=True):
                    return pe.matmul(out, a, b, start=start, stop=stop)

                for c in range(NC):
                    pe.wait_ge(scaled, c + 1)
                    for j in range(2):
                        if c >= 1:
                            pe.wait_ge(ht_copied, 2 * c - 1 + j)
                        for k in range(4):
                            last = pe.transpose(ps[:, 2 + j, k * P:(k + 1) * P],
                                                SCR[:, (c % 2) * D + (4 * j + k) * P:(c % 2) * D + (4 * j + k + 1) * P], ident)
                        last.then_inc(ht_made, 1)
                pe.wait_ge(wg_loaded, 32)
                pe.wait_ge(ht_copied, 2 * NC)
                for c in range(NC):
                    for k in range(KD):
                        last = mm(ps[:, 4, c * 32:(c + 1) * 32], hT[:, k, c * P:(c + 1) * P], wg[:, k, :], k == 0, k == KD - 1)
                last.then_inc(gates_made, 1)

                def unit(u):
                    sl, kind, f, g = UNITS[u]
                    pe.wait_ge([ring_loaded0, ring_loaded1][sl % 2], 16 * (sl // 2 + 1))
                    if u >= 2:
                        pe.wait_ge(proj_read, u - 1)
                    for k in range(KD):
                        if kind in ("xbc", "qk"):
                            t0, n = GROUPS[g]
                            last = mm(ps[:, u % 2, 0:n], ring[sl % 2][:, k, (f % 2) * P:(f % 2 + 1) * P], hT[:, k, t0:t0 + n],
                                      k == 0, k == KD - 1)
                        else:
                            last = mm(ps[:, u % 2, 0:256], hT[:, k, g * P:(g + 1) * P], ring[sl % 2][:, k, :], k == 0, k == KD - 1)
                    last.then_inc(proj_made, 1)
                    if u in LAST_UNIT:
                        pe.wait_ge(proj_made, u + 1)
                        pe.sem_inc(slice_used, 1)

                def turn_xs(f):
                    pe.wait_ge(xbc_made, f + 1)
                    for j, (c0, n) in enumerate(((0, 4), (4, 4), (8, 2))):
                        g = 3 * f + j
                        if g >= 1:
                            pe.wait_ge(xs_kept, g - 1) if g >= 2 else None
                        for c in range(c0, c0 + n):
                            last = pe.transpose(ps[:, 2 + j % 2, (c - c0) * P:(c - c0 + 1) * P],
                                                XF[f % 2][:, tcol(c):tcol(c) + P], ident)
                        last.then_inc(xs_turned, 1)
                        if j == 2:
                            pe.wait_ge(xs_kept, g + 1)

                for u in range(0, 6):
                    unit(u)
                pe.wait_ge(al_made, 2)
                csp = ps[:, 5, 0:240].rearrange("p (c d n) -> p c d n", c=NC, d=2)
                for d in range(2):
                    mm(csp[:, :, d, :], tri[d], AL[:, :, d, :])
                last = mm(ps[:, 6, 0:240], ones1.to_broadcast([P, P]), AL)
                last.then_inc(cs_made, 1)
                for u in range(6, 9):
                    unit(u)
                pe.wait_ge(cs_read, 1)
                for d in range(2):
                    for c in range(NC):
                        pe.transpose(ps[0:4, 2 + 3 * d + c // 4, (c % 4) * P:(c % 4 + 1) * P], U[:, c, d, :], ident)
                for d in range(2):
                    for c in range(NC):
                        last = mm(ps[0:4, 4, 256 + d * NC + c:257 + d * NC + c], AL[:, c, d, 8:12], ones1)
                last.then_inc(urow_made, 1)
                pe.wait_ge(rows_read, 1)
                turn_xs(0)
                for u in range(9, 12):
                    unit(u)
                pe.wait_ge(rows_made, 2)
                for d in range(2):
                    for c in range(NC):
                        for row, at in ((MROW, 0), (UROW, 80)):
                            last = mm(ps[:, 5, at + c * 8 + d * 4:at + c * 8 + d * 4 + 4], row[:, d, c * P:(c + 1) * P], ident[0:4, 0:4])
                last.then_inc(mcol_made, 1)
                turn_xs(1)
                for u in range(12, 15):
                    unit(u)
                pe.wait_ge(mcol_kept, 1)
                pe.wait_ge(m_exps, 1)
                mlp = ps[:, 6, 0:80].rearrange("p (c d n) -> p c d n", c=NC, d=2)
                sop = ps[:, 6, 256:296].rearrange("p (d c n) -> p d c n", d=2, c=NC)
                for d in range(2):
                    at = ident[:, last_of(d):last_of(d) + 1]
                    mm(mlp[:, :, d, :], at.to_broadcast([P, P]), MCOL[:, :, d, :])
                    for q in range(2):
                        last = mm(sop[64 * q:64 * q + 64, d], at.to_broadcast([P, HD]),
                                  SC[:, :, d, :].rearrange("p c (j q) -> p c j q", q=2)[:, :, :, q])
                last.then_inc(mlast_made, 1)
                turn_xs(2)
                for u in range(15, 18):
                    unit(u)
                turn_xs(3)
                pe.wait_ge(xbc_made, 6)
                for j, (c0, n) in enumerate(((0, 4), (4, 4), (8, 2))):
                    if j == 2:
                        pe.wait_ge(b_kept, 1)
                    for c in range(c0, c0 + n):
                        last = pe.transpose(ps[:, 2 + j % 2, (c - c0) * P:(c - c0 + 1) * P], BC[:, 0, tcol(c):tcol(c) + P], ident)
                    last.then_inc(b_turned, 1)
                pe.wait_ge(b_kept, 3)
                for i in range(NC):
                    unit(U_Z + 2 * i)
                    unit(U_Z + 2 * i + 1)
                    pe.wait_ge(dxs_made, 2 * i + 2)
                    if i >= 1:
                        pe.wait_ge(state_kept, i)
                    for d in range(2):
                        for g in range(2):
                            last = mm(ps[64 * g:64 * g + 64, 4, 256 * d:256 * d + 256], BT[:, scan_chunk(d, i), 64 * g:64 * g + 64],
                                      DXS[:, i % 2, d, 256 * g:256 * g + 256])
                    last.then_inc(state_made, 1)
                pe.wait_ge(state_kept, NC)

                def ssd_pairs(c):
                    t = tcol(c)
                    for d in range(2):
                        if 2 * c + d >= 1:
                            pe.wait_ge(csb_read, 2 * c + d)
                        for h in range(SH):
                            last = mm(ps[:, 2 + h // 4, (h % 4) * P:(h % 4 + 1) * P],
                                      AL[:, c, d, h:h + 1].to_broadcast([P, P]), tri[d])
                        last.then_inc(csb_made, 1)
                    if c >= 1:
                        pe.wait_ge(w_made, 4 * c)
                    for g in range(2):
                        fence(mm(ps[:, 4, g * P:(g + 1) * P], BC[64 * g:64 * g + 64, 0, t:t + P], BC[64 * g:64 * g + 64, 1, t:t + P]))
                    pe.sem_inc(cb_made, 1)

                def ssd_sum(c):
                    t = tcol(c)
                    pe.wait_ge(w_made, 4 * (c + 1))
                    if c >= 1:
                        pe.wait_ge(y_gated, c)
                    for h in range(SH):
                        for d in range(2):
                            mm(ps[:, 5, h * HD:(h + 1) * HD], DM[:, c % 2, d, h * P:(h + 1) * P], XS[:, c, h * HD:(h + 1) * HD],
                               d == 0, d == 1)
                    for d in range(2):
                        for g in range(2):
                            last = mm(ps[:, 6 + g, 256 * d:256 * d + 256], BC[64 * g:64 * g + 64, 1, t:t + P],
                                      PREV[64 * g:64 * g + 64, d, c, :])
                    last.then_inc(y_made, 1)

                ssd_pairs(0)
                for c in range(NC):
                    for u in range(U_QK + 3 * c, U_QK + 3 * c + 2):
                        unit(u)
                    if c + 1 < NC:
                        ssd_pairs(c + 1)
                    unit(U_QK + 3 * c + 2)
                    ssd_sum(c)
                unit(U_ATT - 2)
                unit(U_ATT - 1)
                pe.wait_ge(y_gated, NC)
                pe.wait_ge(v_ones, 1)
                pe.wait_ge(proj_read, U_ATT)
                for i in range(NC):
                    unit(U_ATT + 2 * i)
                    if i >= 1:
                        pe.wait_ge(wk_made, 2 * i)
                    for d in range(2):
                        c = scan_chunk(d, i)
                        for q in range(2):
                            last = pe.transpose(ps[:, 4, 256 * d + q * P:256 * d + (q + 1) * P], QK[:, 2 + q, c * P:(c + 1) * P], ident)
                    last.then_inc(kt_turned, 1)
                    unit(U_ATT + 2 * i + 1)
                    pe.wait_ge(wk_made, 2 * i + 2)
                    if i >= 1:
                        n = 2 * sum(has_next(j) for j in range(i))
                        pe.wait_ge(mstate_kept, n)
                    for d in range(2):
                        c = scan_chunk(d, i)
                        for h in range(MH):
                            q = h % 2
                            last = mm(ps[64 * q:64 * q + 64, 5, 256 * d + 65 * (h // 2):256 * d + 65 * (h // 2) + 65],
                                      TMP[:, 256 * d + HD * h:256 * d + HD * (h + 1)], V[:, c, h, :])
                    last.then_inc(mstate_made, 1)
                pe.wait_ge(mstate_kept, 2 * sum(has_next(j) for j in range(NC)))

                def ml_pairs(c):
                    if c >= 1:
                        pe.wait_ge(mst_kept, c)
                    pe.transpose(ps[0:8, 0, 0:P], MCOL[:, c].rearrange("p d n -> p (d n)"), ident).then_inc(mlast_row, 1)
                    if c >= 1:
                        pe.wait_ge(mw_made, 2 * c)
                    for h in (0, 2, 1, 3):
                        if h == 1:
                            fence(last)
                        b = 64 * (h % 2)
                        last = mm(ps[:, 2, h * P:(h + 1) * P], QK[b:b + 64, 2 + h // 2, c * P:(c + 1) * P],
                                  QK[b:b + 64, h // 2, c * P:(c + 1) * P])
                    fence(last)
                    pe.wait_ge(mst_kept, c + 1)
                    for d in range(2):
                        if 2 * c + d >= 1:
                            pe.wait_ge(mb_read, 2 * c + d)
                        for h in range(MH):
                            last = mm(ps[:, 3, h * P:(h + 1) * P], ident[0:8, 4 * d + h:4 * d + h + 1].to_broadcast([8, P]), mr8[c % 2])
                        last.then_inc(mb_made, 1)

                def ml_sum(c):
                    pe.wait_ge(mw_made, 2 * c + 2)
                    if c >= 1:
                        pe.wait_ge(nd_read, 2 * c)
                    for d in range(2):
                        for h in range(MH):
                            b = 64 * (h % 2)
                            mm(ps[:, 5 + d, 65 * h:65 * h + 65], DMM[:, c % 2, d, h, :], V[:, c, h, :])
                            last = mm(ps[:, 4 + 3 * (h % 2), 130 * d + 65 * (h // 2):130 * d + 65 * (h // 2) + 65], QK[b:b + 64, h // 2, c * P:(c + 1) * P],
                                      PREVM[b:b + 64, d, c, h // 2, :])
                    last.then_inc(nd_made, 1)

                pe.wait_ge(proj_read, len(UNITS))
                ml_pairs(0)
                for c in range(NC):
                    if c + 1 < NC:
                        ml_pairs(c + 1)
                    ml_sum(c)
                for c in range(NC):
                    pe.wait_ge(a_normed, c + 1)
                    if c == 0:
                        pe.wait_ge(nd_read, 2 * NC)
                    else:
                        pe.wait_ge(a_kept, c)
                    for j in range(3):
                        last = pe.transpose(ps[:, 7, j * P:(j + 1) * P], TMP[:, j * P:(j + 1) * P], ident)
                    last.then_inc(a_turned, 1)
                pe.wait_ge(a_kept, NC)

                def scores(c):
                    nk, c0 = attn_keys(c)
                    if c >= 1:
                        pe.wait_ge(s_read, c)
                    for h in range(AH):
                        g, j = h // 2, h % 2
                        last = mm(ps[:, 2 + h, 0:nk * P], QT[64 * g:64 * g + 64, j, c * P:(c + 1) * P],
                                  KT[64 * g:64 * g + 64, c0 * P:(c0 + nk) * P])
                    last.then_inc(s_made, 1)

                scores(0)
                for c in range(NC):
                    nk, c0 = attn_keys(c)
                    if c + 1 < NC:
                        scores(c + 1)
                    pe.wait_ge(sink_exp, c + 1)
                    if c >= 1:
                        pe.wait_ge(a_done, c)
                    for h in range(AH):
                        if h >= 2:
                            pe.wait_ge(p_kept, AH * c + h - 1)
                        for b in range(nk):
                            last = pe.transpose(ps[:, 6 + h % 2, b * P:(b + 1) * P], PSC[c % 2][:, h, b * P:(b + 1) * P], ident)
                        last.then_inc(p_turned, 1)
                    for h in range(AH):
                        pe.wait_ge(p_kept, AH * c + h + 1)
                        g = h // 2
                        for b in range(nk):
                            last = mm(ps[:, c % 2, HD * h:HD * h + HD],
                                      TMP[:, h * 384 + b * P:h * 384 + (b + 1) * P],
                                      Z[:, c0 + b, 384 + 64 * g:448 + 64 * g], b == 0, b == nk - 1)
                    last.then_inc(o_made, 1)
                pe.wait_ge(a_done, NC)
                pe.wait_ge(y_done, NC)
                for c in range(NC):
                    tiles = [Z[:, c, 0:P], Z[:, c, P:2 * P]] + [XS[:, c, k * P:(k + 1) * P] for k in range(4)] \
                        + [O[:, c, 0:P], O[:, c, P:2 * P]]
                    for j in range(2):
                        if c >= 1:
                            pe.wait_ge(yt_copied, 2 * c - 1 + j)
                        for k in range(4):
                            last = pe.transpose(ps[:, 2 + j, k * P:(k + 1) * P], tiles[4 * j + k], ident)
                        last.then_inc(yt_made, 1)
                pe.wait_ge(wo_loaded, 16)
                pe.wait_ge(yt_copied, 2 * NC)

                def out_proj(c):
                    for hf in range(2):
                        if c >= 1:
                            pe.wait_ge(op_added, 2 * c - 1 + hf)
                        for k in range(KD):
                            last = mm(ps[:, hf, :], hT[:, k, c * P:(c + 1) * P], WO[:, k, hf * 512:(hf + 1) * 512], k == 0, k == KD - 1)
                        last.then_inc(op_made, 1)

                out_proj(0)
                for c in range(NC):
                    if c + 1 < NC:
                        out_proj(c + 1)
                    pe.wait_ge(n2_scaled, c + 1)
                    for j in range(2):
                        if c >= 1:
                            pe.wait_ge(h2t_copied, 2 * c - 1 + j)
                        for k in range(4):
                            last = pe.transpose(ps[:, 4 + j, k * P:(k + 1) * P], H2[c % 2][:, (4 * j + k) * P:(4 * j + k + 1) * P], ident)
                        last.then_inc(h2t_made, 1)
                    pe.wait_ge(h2t_copied, 2 * c + 2)
                    if c >= 1:
                        pe.wait_ge(lg_shift, c)
                    for k in range(KD):
                        last = mm(ps[:, 6, 0:E], H2T[:, k, :], pr("router")[:, k * E:(k + 1) * E], k == 0, k == KD - 1)
                    last.then_inc(lg_made, 1)
                    pe.wait_ge(aff_made, c + 1)
                    if c >= 1:
                        pe.wait_ge(aff_kept, c)
                    pe.transpose(ps[0:E, 7, 0:P], AFT, ident).then_inc(aff_turned, 1)
                pe.wait_ge(top_done, 1)
                pe.transpose(ps[:, 7, 0:E], IDF[:, 0:CAPS], ident[0:E, 0:E])
                pe.transpose(ps[0:CAPP, 7, E:2 * E], IDF[:, CAPS:TOK], ident[0:E, 0:E])
                pe.transpose(ps[:, 7, 2 * E:3 * E], VAL[:, 0:CAPS], ident[0:E, 0:E])
                pe.transpose(ps[0:CAPP, 7, 3 * E:4 * E], VAL[:, CAPS:TOK], ident[0:E, 0:E]).then_inc(topt_made, 1)
                pe.wait_ge(idx_ready, 1)

                def turn_tokens(e):
                    pe.wait_ge(gathered, 32 * (e + 1))
                    for j, (k0, n) in enumerate(((0, 3), (3, 3), (6, 2))):
                        g = 3 * e + j
                        if g >= 1:
                            pe.wait_ge(g_copied, g - 1 if j == 2 else 3 * e) if (j == 2 or e >= 1) else None
                        for k in range(n):
                            src = slice((k0 + k) * P, (k0 + k + 1) * P)
                            pe.transpose(ps[:, j % 2, k * TOK:k * TOK + CAPS], XG[e % 2][:, src], ident)
                            last = pe.transpose(ps[:, j % 2, k * TOK + CAPS:(k + 1) * TOK], XGP[e % 2][:, src], ident[0:CAPP, 0:CAPP])
                        last.then_inc(g_turned, 1)

                turn_tokens(0)
                for e in range(E):
                    pe.wait_ge([ew_loaded0, ew_loaded1][e % 2], 48 * (e // 2 + 1))
                    pe.wait_ge(g_copied, 3 * e + 3)
                    for f in range(KF):
                        n = KF * e + f
                        if n >= 2:
                            pe.wait_ge(hid_made, n - 1)
                        for w, at in ((EG, 0), (EU, TOK)):
                            for k in range(KD):
                                last = mm(ps[:, 2 + f % 2, at:at + TOK], w[e % 2][:, k, f * P:(f + 1) * P], XT[e % 2][:, k, :],
                                          k == 0, k == KD - 1)
                        last.then_inc(gu_made, 1)
                    if e + 1 < E:
                        turn_tokens(e + 1)
                    pe.wait_ge(hid_made, KF * e + KF)
                    if e >= 1:
                        pe.wait_ge(down_scaled, 4 * e)
                    for j in range(4):
                        hf = j % 2
                        m = CAPS if j < 2 else CAPP
                        t0 = 0 if j < 2 else CAPS
                        for f in range(KF):
                            last = mm(ps[0:m, 4 + j, :], HID[:, f, t0:t0 + m], ED[e % 2][:, f, hf * 512:(hf + 1) * 512],
                                      f == 0, f == KF - 1)
                        last.then_inc(down_part, 1)
                    pe.wait_ge(down_part, 4 * e + 4)
                    pe.sem_inc(down_made, 1)
          nc.gpsimd.dma_reset(rng)
          nc.all_engine_barrier()
          nc.sync.sem_clear(rng)
          nc.all_engine_barrier()


_BIG = [("w_in", D_IN), ("w_out", D), ("w_gate", FF), ("w_up", FF), ("w_down", D)]


def constants():
    i = np.arange(P)
    eye = np.eye(P, dtype=np.float32)
    le = (i[:, None] <= i[None, :]).astype(np.float32)
    cst = np.concatenate([eye, le, le.T, np.ones((P, 1), np.float32)], axis=1)
    rel = np.arange(-(NREL // 2), NREL // 2 + 1)
    half, exact = 16, 8
    n = np.abs(rel)
    large = exact + (np.log(np.maximum(n, 1) / exact) / np.log(128 / exact) * (half - exact)).astype(np.int32)
    bucket = (rel > 0).astype(np.int32) * half + np.where(n < exact, n, np.minimum(large, half - 1))
    hot = np.zeros((33, NREL), np.float32)
    hot[bucket, np.arange(NREL)] = 1.0
    hot[32] = np.where(n <= 128, 0.0, NEG)
    return np.ascontiguousarray(cst), hot


def parameters(x):
    def col(a, k):
        return a.reshape(DEPTH, k, P).transpose(0, 2, 1)

    def row(a):
        a = a.reshape(DEPTH, 1, -1)
        return np.broadcast_to(a, (DEPTH, P, a.shape[2]))

    def twice(a):
        return np.concatenate([a, a], axis=1)[:, :, None]

    cw = x["ssd_conv_w"].reshape(DEPTH, 5, 6, P).transpose(0, 3, 2, 1).reshape(DEPTH, P, 30)
    rt = x["router"].reshape(DEPTH, KD, P, E).transpose(0, 2, 1, 3).reshape(DEPTH, P, KD * E)
    parts = dict(gmix=col(x["mix_norm"], 8), gffn=col(x["ffn_norm"], 8),
                 gy=np.concatenate([np.ones((DEPTH, P, 2), np.float32), col(x["ssd_norm"], 4), col(x["mlstm_norm"], 2)], axis=2),
                 convw=cw, convb=col(x["ssd_conv_b"], 6), qg=twice(x["attn_q_norm"]), kg=twice(x["attn_k_norm"]),
                 sink=row(x["attn_sink"]),
                 gbias=np.concatenate([row(x["ssd_dt_bias"]), row(x["mlstm_i_bias"]), row(x["mlstm_f_bias"])], axis=2),
                 alog=row(x["ssd_a_log"]), dskip=row(x["ssd_d"]), router=rt)
    return np.ascontiguousarray(np.concatenate([parts[n] for n in PAR], axis=2)).reshape(DEPTH * P, NPAR)


def kernel(**inputs):
    import concourse.bacc as bacc
    from concourse.bass_utils import run_bass_kernel_spmd

    x = {k: np.asarray(v) for k, v in inputs.items()}
    cst, hot = constants()
    table = np.concatenate([x["rel_bias"], np.ones((1, AH), np.float32)], axis=0)
    arrays = {n: np.ascontiguousarray(x[n]).reshape(-1, w) for n, w in _BIG}
    arrays.update(flip=np.ascontiguousarray(np.eye(P, dtype=np.float32)[::-1]), par=parameters(x), cst=cst, onehot=np.concatenate([hot, table], axis=1),
                  x_prompt=np.ascontiguousarray(x["x_prompt"][0]), x_sample=np.ascontiguousarray(x["x_sample"][0]))
    nc = bacc.Bacc("TRN2", target_bir_lowering=False, num_devices=1)
    f32 = mybir.dt.float32
    ap = {n: nc.dram_tensor(n, a.shape, f32, kind="ExternalInput").ap() for n, a in arrays.items()}
    yp = nc.dram_tensor("y_prompt", (SEQS[0], D), f32, kind="ExternalOutput").ap()
    ys = nc.dram_tensor("y_sample", (SEQS[1], D), f32, kind="ExternalOutput").ap()
    btab = nc.dram_tensor("bias_table", (AH, 512), f32, kind="Internal").ap()
    h2p = nc.dram_tensor("h2_prompt", (SEQS[0], D), f32, kind="Internal").ap()
    h2s = nc.dram_tensor("h2_sample", (SEQS[1], D), f32, kind="Internal").ap()
    program(nc, ap["w_in"], ap["w_out"], ap["w_gate"], ap["w_up"], ap["w_down"], ap["par"], ap["cst"], ap["onehot"],
            ap["x_prompt"], ap["x_sample"], yp, ys, btab, h2p, h2s, ap["flip"])
    r = run_bass_kernel_spmd(nc, [arrays], core_ids=[0]).results[0]
    return r["y_prompt"][None], r["y_sample"][None]
```

```python
import concourse.bass as bass
from concourse import mybir
from contextlib import ExitStack
import numpy as np

DEPTH, D = 2, 1024
SEQS = (256, 1024)
T = sum(SEQS)
P = 128
NC = T // P
NP = SEQS[0] // P
KD = D // P
HD = 64
SH, MH, AH = 8, 4, 4
E, CAPS, CAPP, FF = 16, 128, 32, 512
TOK = CAPS + CAPP
KF = FF // P
D_IN = 2848
NEG = -1e30
EPS = 1e-6

PAR = {}
_n = 0
for _name, _w in (("gmix", 8), ("gffn", 8), ("gy", 8), ("convw", 30), ("convb", 6), ("qg", 1), ("kg", 1),
                  ("sink", 4), ("gbias", 32), ("alog", 16), ("dskip", 8), ("router", 128)):
    PAR[_name] = (_n, _n + _w)
    _n += _w
NPAR = _n
NCST = 3 * P + 1
NREL = 511

SLICES = [("xbc", 1024), ("xbc", 1280), ("xbc", 1536), ("z", 512), ("z", 768), ("qk", 1808), ("qk", 2064),
          ("v", 2320), ("o", 2576), ("att", 0), ("att", 256)]
GROUPS = [(0, 512), (512, 512), (1024, 256)]
UNITS = []
for _s, (_k, _c) in enumerate(SLICES):
    _i = [k for k, _ in SLICES[:_s]].count(_k)
    if _k in ("xbc", "qk"):
        UNITS += [(_s, _k, 2 * _i + h, g) for h in range(2) for g in range(3)]
    else:
        UNITS += [(_s, _k, _i, c) for c in range(NC)]
U_XBC, U_Z, U_QK, U_VO, U_ATT = 0, 18, 38, 50, 70
LAST_UNIT = [max(u for u, x in enumerate(UNITS) if x[0] == s) for s in range(len(SLICES))]


def in_seq(c):
    return (0, NP) if c < NP else (NP, NC)


def scan_chunk(d, i):
    if d == 0:
        return i
    lo, hi = in_seq(i)
    return lo + hi - 1 - i


def has_next(i):
    return i not in (NP - 1, NC - 1)


def tcol(c):
    return P * c + (2 if c >= NP else 0)



def attn_keys(c):
    lo, hi = in_seq(c)
    c0 = max(c - 1, lo)
    return min(c + 1, hi - 1) - c0 + 1, c0


def program(nc, wi, wo, wga, wup, wdn, par, cst, onehot, xp, xs_in, yp, ys, btab, h2p, h2s, flip):
    F32, U32 = mybir.dt.float32, mybir.dt.uint32
    ALU, ACT = mybir.AluOpType, mybir.ActivationFunctionType
    AX = mybir.AxisListType.X
    ctx = ExitStack()
    with ctx:
        def sb(name, cols, dt=F32, parts=P):
            return ctx.enter_context(nc.sbuf_tensor(name, [parts, cols], dt))

        HT = sb("HT", KD * T)
        MID = sb("MID", 2 * NC * 512 + 2 * 1284 + 2 * NC * 256 + 5120 + NC * 516)
        RING = sb("RING", 2 * KD * 256)
        SCR = sb("SCR", 4096)
        TMP = sb("TMP", 1536)
        cstt = sb("cstt", NCST)
        part = sb("part", NPAR)
        bias = sb("bias", AH * 384)
        small = sb("small", 1980)
        idxs = sb("idxs", E, U32)
        idxp = sb("idxp", E, U32, CAPP)
        idxu = sb("idxu", CAPS, U32, 3 * E)
        ps = ctx.enter_context(nc.psum_tensor("ps", [P, 8, 512], F32))

        o = 0

        def take(n):
            nonlocal o
            o += n
            return MID[:, o - n:o]

        hT = HT[:, :].rearrange("p (k t) -> p k t", k=KD)
        ZF = take(NC * 512)
        Z = ZF.rearrange("p (c n) -> p c n", c=NC)
        XSF = take(NC * 512)
        XS = XSF.rearrange("p (c n) -> p c n", c=NC)
        bc_at = o
        BC = take(2 * 1284).rearrange("p (w t) -> p w t", w=2)
        pv_at = o
        PREV = take(2 * NC * 256).rearrange("p (d c n) -> p d c n", d=2, c=NC)
        qk_at = o
        QK = take(5120).rearrange("p (f t) -> p f t", f=4)
        VO = take(NC * 516)
        V = VO[:, 0:NC * 260].rearrange("p (c h e) -> p c h e", c=NC, h=MH)
        O = VO[:, NC * 260:NC * 516].rearrange("p (c n) -> p c n", c=NC)
        XF = [MID[:, qk_at + 1284 * j:qk_at + 1284 * (j + 1)] for j in range(2)]
        UROW = VO[0:4, 0:2 * T].rearrange("p (d t) -> p d t", d=2)
        MROW = VO[0:4, 2 * T:4 * T].rearrange("p (d t) -> p d t", d=2)
        PREVM = MID[:, pv_at:pv_at + 2 * NC * 130].rearrange("p (d c h e) -> p d c h e", d=2, c=NC, h=2)
        QT = MID[:, bc_at:bc_at + 2 * T].rearrange("p (j t) -> p j t", j=2)
        WO = MID[:, pv_at:pv_at + KD * D].rearrange("p (k n) -> p k n", k=KD)
        ring = [RING[:, j * 2048:(j + 1) * 2048].rearrange("p (k n) -> p k n", k=KD) for j in range(2)]
        XN = [SCR[:, j * D:(j + 1) * D] for j in range(4)]
        RAW = [SCR[:, 1288 * j:1288 * (j + 1)] for j in range(2)]
        ACC = [SCR[:, 2576:2576 + 1284], TMP[:, 0:1284]]
        BT = SCR[:, 0:NC * P].rearrange("p (c n) -> p c n", c=NC)
        DXS = SCR[:, 1280:1280 + 2048].rearrange("p (b d n) -> p b d n", b=2, d=2)
        DM = SCR[:, :].rearrange("p (b d n) -> p b d n", b=2, d=2)
        OTH = [SCR[:, 2304:2560], SCR[:, 2048:2304]]
        QKN = [RING[:, 3328 + 384 * j:3328 + 384 * (j + 1)] for j in range(2)]
        QKS = SCR[:, 3328:3328 + 6 * NC].rearrange("p (c n) -> p c n", c=NC)
        WK = [TMP[:, 512 * j:512 * (j + 1)] for j in range(2)]
        DMM = SCR[:, 0:2048].rearrange("p (b d h t) -> p b d h t", b=2, d=2, h=MH)
        KT = RING[:, 0:T]
        PSC = [SCR[:, 1536 * b:1536 * (b + 1)].rearrange("p (h k) -> p h k", h=AH) for b in range(2)]
        ident, tri = cstt[:, 0:P], [cstt[:, P:2 * P], cstt[:, 2 * P:3 * P]]
        ones1 = cstt[:, 3 * P:3 * P + 1]
        bia = bias[:, :].rearrange("p (h k) -> p h k", h=AH)
        EW = [MID[:, j * 12288:(j + 1) * 12288] for j in range(2)]
        EG = [w[:, 0:4096].rearrange("p (k f) -> p k f", k=KD) for w in EW]
        EU = [w[:, 4096:8192].rearrange("p (k f) -> p k f", k=KD) for w in EW]
        ED = [w[:, 8192:12288].rearrange("p (k n) -> p k n", k=KF) for w in EW]
        XG = [HT[:, j * D:(j + 1) * D] for j in range(3)]
        XGP = [HT[0:CAPP, (3 + j) * D:(4 + j) * D] for j in range(3)]
        XT = [HT[:, 6 * D + 1280 * j:6 * D + 1280 * (j + 1)].rearrange("p (k t) -> p k t", k=KD) for j in range(2)]
        HID = HT[:, 8704:8704 + KF * TOK].rearrange("p (f t) -> p f t", f=KF)
        THG = HT[:, 9344:9344 + TOK]
        YO = [SCR[:, j * D:(j + 1) * D] for j in range(2)]
        YOP = [SCR[0:CAPP, (2 + j) * D:(3 + j) * D] for j in range(2)]
        XO = [RING[:, 1280 + j * D:1280 + (j + 1) * D] for j in range(2)]
        H2 = [SCR[:, (2 + j) * D:(3 + j) * D] for j in range(2)]
        H2T = RING[:, 0:D].rearrange("p (k t) -> p k t", k=KD)
        JUNK = SCR[:, 0:D]
        AFF = TMP[0:3 * E, 0:512]
        VAL3 = TMP[0:3 * E, 512:512 + CAPS]
        IDF3 = TMP[0:3 * E, 640:640 + CAPS]
        REV = TMP[0:3 * E, 1088:1088 + 2 * CAPS]
        TC = TMP[:, 768:768 + 7 * E]
        AFTM = TMP[:, 896:896 + 12 * E].rearrange("p (j n) -> p j n", j=4)
        AFT = RING[:, 3328:3328 + E]

        def pr(name):
            return part[:, PAR[name][0]:PAR[name][1]]

        z_at = 0

        def early(n):
            nonlocal z_at
            z_at += n
            return ZF[:, z_at - n:z_at]

        small_at = 0

        def tiny(n, parts=P):
            nonlocal small_at
            small_at += n
            return small[0:parts, small_at - n:small_at]

        def per(a, n):
            return a.rearrange("p (c d n) -> p c d n", c=NC, d=2)

        wg = early(KD * 32).rearrange("p (k n) -> p k n", k=KD)
        G = early(NC * 32).rearrange("p (c n) -> p c n", c=NC)
        SPV = early(NC * 24).rearrange("p (c n) -> p c n", c=NC)
        SPE = early(NC * 24).rearrange("p (c n) -> p c n", c=NC)
        SPT = early(NC * 24).rearrange("p (c n) -> p c n", c=NC)
        SP2 = early(NC * 24).rearrange("p (c n) -> p c n", c=NC)
        SPP = early(NC * 24).rearrange("p (c n) -> p c n", c=NC)
        TOT = per(early(NC * 24), 12)
        TMC = per(early(NC * 16), 8)
        LND = early(NC * 16).rearrange("p (c n) -> p c n", c=NC)
        DRC = per(early(NC * 8), 4)
        BM = per(early(NC * 8), 4)
        WMX = per(early(NC * 8), 4)
        AL = per(tiny(NC * 24), 12)
        CS = per(tiny(NC * 24), 12)
        ECS = per(tiny(NC * 24), 12)
        WS = per(tiny(NC * 16), 8)
        DECG = per(tiny(NC * 8), 4)
        U = per(tiny(NC * 8), 4)
        MCOL = per(tiny(NC * 8), 4)
        SC = per(tiny(NC * 8), 4)
        EML = per(tiny(NC * 8), 4)
        WM = per(tiny(NC * 8), 4)
        SOLD = tiny(NC * 4).rearrange("p (d c n) -> p d c n", d=2, c=NC)
        NEGA = tiny(16)
        MPREV = tiny(2 * NC, 4).rearrange("p (d c) -> p d c", d=2)
        GROW = tiny(2 * NC, 4).rearrange("p (d c) -> p d c", d=2)
        ss, rs = tiny(NC), tiny(NC)
        ssb, rsb, halfn, den, rec, mx, esk, nmx = (tiny(8) for _ in range(8))
        MR = tiny(P, 8 * NC)
        AMX, AESK, ANMX, ADEN = ([tiny(AH) for _ in range(2)] for _ in range(4))
        gts, gtp = tiny(E), tiny(E, CAPP)
        assert small_at <= 1980, small_at

        def sem(name):
            return ctx.enter_context(nc.semaphore(name))

        setup = sem("setup")
        layer_sems = []

        def layer_sem(name):
            layer_sems.append(sem(name))
            return layer_sems[-1]

        par_loaded = layer_sem("par_loaded")
        wg_loaded = layer_sem("wg_loaded")
        slice_used = layer_sem("slice_used")
        ring_loaded0 = layer_sem("ring_loaded0")
        ring_loaded1 = layer_sem("ring_loaded1")
        ht_made = layer_sem("ht_made")
        x_loaded = [layer_sem(f"x_loaded{j}") for j in range(4)]
        o_made = layer_sem("o_made")
        wo_loaded = layer_sem("wo_loaded")
        a_done = layer_sem("a_done")
        x_stored = [layer_sem(f"x_stored{j}") for j in range(2)]
        xo_loaded0 = layer_sem("xo_loaded0")
        xo_loaded1 = layer_sem("xo_loaded1")
        op_added = layer_sem("op_added")
        n2_scaled = layer_sem("n2_scaled")
        h2_stored = [layer_sem(f"h2_stored{j}") for j in range(2)]
        ew_loaded0 = layer_sem("ew_loaded0")
        ew_loaded1 = layer_sem("ew_loaded1")
        down_made = layer_sem("down_made")
        pool_chain = layer_sem("pool_chain")
        squared = layer_sem("squared")
        rooted = layer_sem("rooted")
        pads_ready = layer_sem("pads_ready")
        xbc_made = layer_sem("xbc_made")
        xs_kept = layer_sem("xs_kept")
        ws_made = layer_sem("ws_made")
        state_made = layer_sem("state_made")
        dxs_made = layer_sem("dxs_made")
        csb_read = layer_sem("csb_read")
        d_masked = layer_sem("d_masked")
        y_gated = layer_sem("y_gated")
        y_read = layer_sem("y_read")
        xsd_made = layer_sem("xsd_made")
        y_squared = layer_sem("y_squared")
        y_rooted = layer_sem("y_rooted")
        mcol_made = layer_sem("mcol_made")
        v_ones = layer_sem("v_ones")
        mb_read = layer_sem("mb_read")
        st_made = layer_sem("st_made")
        mrow_made = layer_sem("mrow_made")
        mrow_kept = layer_sem("mrow_kept")
        md_masked = layer_sem("md_masked")
        h_summed = layer_sem("h_summed")
        h_rooted = layer_sem("h_rooted")
        a_squared = layer_sem("a_squared")
        a_rooted = layer_sem("a_rooted")
        n2_squared = layer_sem("n2_squared")
        n2_rooted = layer_sem("n2_rooted")
        idx_ready = layer_sem("idx_ready")
        g_turned = layer_sem("g_turned")
        gathered = [layer_sem(f"gathered{j}") for j in range(3)]
        down_scaled = layer_sem("down_scaled")
        scattered = layer_sem("scattered")
        act_chain = layer_sem("act_chain")
        scaled = layer_sem("scaled")
        softplus_exp = layer_sem("softplus_exp")
        softplus_in = layer_sem("softplus_in")
        proj_made = layer_sem("proj_made")
        conv_done = layer_sem("conv_done")
        proj_read = layer_sem("proj_read")
        wm_ready = layer_sem("wm_ready")
        xs_turned = layer_sem("xs_turned")
        tanh_done = layer_sem("tanh_done")
        dt_made = layer_sem("dt_made")
        ln_done = layer_sem("ln_done")
        cs_read = layer_sem("cs_read")
        state_exps = layer_sem("state_exps")
        mcol_read = layer_sem("mcol_read")
        m_exps = layer_sem("m_exps")
        wm_diff = layer_sem("wm_diff")
        b_turned = layer_sem("b_turned")
        b_kept = layer_sem("b_kept")
        d_exp = layer_sem("d_exp")
        z_tanh = layer_sem("z_tanh")
        y_done = layer_sem("y_done")
        md_exp = layer_sem("md_exp")
        h_done = layer_sem("h_done")
        o_tanh = layer_sem("o_tanh")
        s_shift = layer_sem("s_shift")
        sink_exp = layer_sem("sink_exp")
        p_turned = layer_sem("p_turned")
        p_kept = layer_sem("p_kept")
        h2t_made = layer_sem("h2t_made")
        lg_shift = layer_sem("lg_shift")
        lg_exp = layer_sem("lg_exp")
        gu_made = layer_sem("gu_made")
        hid_made = layer_sem("hid_made")
        gate_tanh = layer_sem("gate_tanh")
        down_part = layer_sem("down_part")
        dve_chain = layer_sem("dve_chain")
        ht_copied = layer_sem("ht_copied")
        gates_made = layer_sem("gates_made")
        gates_read = layer_sem("gates_read")
        al_made = layer_sem("al_made")
        cs_made = layer_sem("cs_made")
        urow_made = layer_sem("urow_made")
        rows_read = layer_sem("rows_read")
        rows_made = layer_sem("rows_made")
        mcol_kept = layer_sem("mcol_kept")
        mlast_made = layer_sem("mlast_made")
        state_kept = layer_sem("state_kept")
        csb_made = layer_sem("csb_made")
        y_made = layer_sem("y_made")
        cb_made = layer_sem("cb_made")
        w_made = layer_sem("w_made")
        kt_turned = layer_sem("kt_turned")
        mstate_made = layer_sem("mstate_made")
        wk_made = layer_sem("wk_made")
        mstate_kept = layer_sem("mstate_kept")
        mb_made = layer_sem("mb_made")
        nd_made = layer_sem("nd_made")
        mw_made = layer_sem("mw_made")
        nd_read = layer_sem("nd_read")
        a_turned = layer_sem("a_turned")
        a_normed = layer_sem("a_normed")
        a_kept = layer_sem("a_kept")
        s_made = layer_sem("s_made")
        s_read = layer_sem("s_read")
        yt_made = layer_sem("yt_made")
        yt_copied = layer_sem("yt_copied")
        op_made = layer_sem("op_made")
        lg_made = layer_sem("lg_made")
        h2t_copied = layer_sem("h2t_copied")
        aff_turned = layer_sem("aff_turned")
        aff_made = layer_sem("aff_made")
        top_done = layer_sem("top_done")
        topt_made = layer_sem("topt_made")
        g_copied = layer_sem("g_copied")
        pe_fence = layer_sem("pe_fence")
        rng = range(min(x.num for x in layer_sems), max(x.num for x in layer_sems) + 1)
        assert len(rng) == len(layer_sems)

        cbank = ps[0:AH, 0, 0:NREL]
        with nc.Block() as block:
            @block.sync
            def _(sp):
                sp.dma_start(cstt[:, :], cst[:, :]).then_inc(setup, 16)
                sp.dma_start(SCR[0:33, 0:NREL + AH], onehot[:, :]).then_inc(setup, 16)
                sp.dma_start(HT[:, 0:P], flip[:, :]).then_inc(setup, 16)
                sp.dma_start(yp[:, :], xp[:, :]).then_inc(setup, 16)
                sp.dma_start(ys[:, :], xs_in[:, :]).then_inc(setup, 16)
                sp.wait_ge(setup, 82)
                sp.dma_start(btab[:, 0:NREL], SCR[0:AH, 1024:1024 + NREL]).then_inc(setup, 16)
                sp.wait_ge(setup, 98)
                sp.dma_start(HT[:, P:P + AH * 384].rearrange("p (h k) -> p h k", h=AH),
                             bass.AP(tensor=btab.tensor, offset=0, ap=[[1, P], [512, AH], [1, 384]])).then_inc(setup, 16)
                sp.wait_ge(setup, 114)

            @block.tensor
            def _(pe):
                pe.wait_ge(setup, 80)
                pe.matmul(cbank, SCR[0:33, NREL:NREL + AH], SCR[0:33, 0:NREL],
                          start=True, stop=True).then_inc(setup, 1)
                pe.wait_ge(setup, 114)
                for h in range(AH):
                    last = pe.matmul(ps[:, 1 + h, 0:384], HT[:, 0:P], HT[:, P + 384 * h:P + 384 * (h + 1)], start=True, stop=True)
                last.then_inc(setup, 1)

            @block.vector
            def _(dve):
                dve.wait_ge(setup, 81)
                dve.tensor_copy(SCR[0:AH, 1024:1024 + NREL], cbank).then_inc(setup, 1)
                dve.wait_ge(setup, 115)
                dve.tensor_copy(bia, ps[:, 1:5, 0:384]).then_inc(setup, 1)

        def counter(eng, own):
            n = {}

            def link(ins, to=own):
                n[to.num] = n.get(to.num, 0) + 1
                ins.then_inc(to, 1)
                eng.wait_ge(to, n[to.num])

            return link

        def last_of(d):
            return P - 1 if d == 0 else 0

        with nc.Fori(0, DEPTH) as layer:
          with nc.Block() as block:
            @block.sync
            def _(sp):
                sp.dma_start(part[:, :], par[bass.ds(layer * P, P), :]).then_inc(par_loaded, 16)
                with nc.allow_non_contiguous_dma(reason="gate columns"):
                    for at, c0, w in ((0, 1792, 16), (16, 2832, 16)):
                        sp.dma_start(wg[:, :, at:at + w], wi[bass.ds(layer * D, D), c0:c0 + w]
                                     .rearrange("(k p) n -> p k n", p=P)).then_inc(wg_loaded, 16)

                def x_rows(c):
                    return yp[c * P:(c + 1) * P, :] if c < NP else ys[(c - NP) * P:(c - NP + 1) * P, :]

                def h2_rows(c):
                    return h2p[c * P:(c + 1) * P, :] if c < NP else h2s[(c - NP) * P:(c - NP + 1) * P, :]

                def ring_load(i):
                    if i >= 2:
                        sp.wait_ge(slice_used, i - 1)
                    c0 = SLICES[i][1]
                    sp.dma_start(ring[i % 2], wi[bass.ds(layer * D, D), c0:c0 + 256]
                                 .rearrange("(k p) n -> p k n", p=P)).then_inc([ring_loaded0, ring_loaded1][i % 2], 16)

                def expert_load(e):
                    done = [ew_loaded0, ew_loaded1][e % 2]
                    for dst, src, rows in ((EG, wga, D), (EU, wup, D), (ED, wdn, FF)):
                        sp.dma_start(dst[e % 2], src[bass.ds(layer * (E * rows) + e * rows, rows), :]
                                     .rearrange("(k p) n -> p k n", p=P)).then_inc(done, 16)

                for c in range(NC):
                    if c >= 4:
                        sp.wait_ge(ht_made, 2 * (c - 3))
                    sp.dma_start(XN[c % 4], x_rows(c)).then_inc(x_loaded[c % 4], 16)
                    if c in (3, 5):
                        ring_load(c // 2 - 1)
                for i in range(2, len(SLICES)):
                    ring_load(i)
                sp.wait_ge(nd_made, NC)
                sp.dma_start(WO, wo[bass.ds(layer * D, D), :].rearrange("(k p) n -> p k n", p=P)).then_inc(wo_loaded, 16)
                sp.wait_ge(slice_used, len(SLICES))
                for c in range(2):
                    sp.dma_start(XO[c], x_rows(c)).then_inc([xo_loaded0, xo_loaded1][c], 16)
                for c in range(NC):
                    sp.wait_ge(op_added, 2 * c + 2)
                    sp.dma_start(x_rows(c), XO[c % 2]).then_inc(x_stored[c % 2], 16)
                    sp.wait_ge(n2_scaled, c + 1)
                    sp.dma_start(h2_rows(c), H2[c % 2]).then_inc(h2_stored[c % 2], 16)
                    if c + 2 < NC:
                        sp.wait_ge(x_stored[c % 2], 16 * (c // 2 + 1))
                        sp.dma_start(XO[c % 2], x_rows(c + 2)).then_inc([xo_loaded0, xo_loaded1][c % 2], 16)
                    if c == NC - 2:
                        sp.wait_ge(yt_made, 2 * NC)
                        expert_load(0)
                sp.wait_ge(op_made, 2 * NC)

                for e in range(1, E):
                    if e >= 2:
                        sp.wait_ge(down_made, e - 1)
                    expert_load(e)

            @block.gpsimd
            def _(pool):
                link = counter(pool, pool_chain)

                def rroot(out, src, n, mul, eps, to):
                    link(pool.tensor_scalar(out[:, 0:n], src[:, 0:n], mul, eps, ALU.mult, ALU.add))
                    link(pool.tensor_tensor(out[:, 0:n], out[:, 0:n], halfn[:, 0:n], ALU.pow), to)

                link(pool.memset(halfn, -0.5))
                for c in range(NC):
                    pool.wait_ge(squared, c + 1)
                    rroot(rs[:, c:c + 1], ss[:, c:c + 1], 1, 1.0 / D, EPS, rooted)
                pool.wait_ge(ht_made, 2 * NC)
                for r in RAW:
                    for a, b in ((0, 2), (258, 260), (1284, 1286)):
                        link(pool.memset(r[:, a:b], 0.0), pads_ready)
                pool.wait_ge(xbc_made, 6)
                pool.wait_ge(xs_kept, 12)
                pool.wait_ge(ws_made, 1)
                for i in range(NC):
                    if i >= 2:
                        pool.wait_ge(state_made, i - 1)
                    for d in range(2):
                        c = scan_chunk(d, i)
                        link(pool.tensor_tensor(DXS[:, i % 2, d, :].rearrange("p (h e) -> p h e", h=SH),
                                                XS[:, c, :].rearrange("p (h e) -> p h e", h=SH),
                                                WS[:, c, d, :].unsqueeze(2).to_broadcast([P, SH, HD]), ALU.mult), dxs_made)
                def ssd_mask(c, d):
                    pool.wait_ge(csb_read, 2 * c + d + 1)
                    v = DM[:, c % 2, d, :].rearrange("p (h t) -> p h t", h=SH)
                    sgn = 1 if d == 0 else -1
                    link(pool.affine_select(out=v, in_=v, compare_op=ALU.is_ge, fill=NEG, base=0,
                                            pattern=[[0, SH], [sgn, P]], channel_multiplier=-sgn), d_masked)

                ssd_mask(0, 0)
                ssd_mask(0, 1)
                for c in range(NC + 1):
                    if c < NC:
                        if c >= 1:
                            pool.wait_ge(y_gated, c)
                        link(pool.tensor_tensor(TMP[:, 0:512].rearrange("p (h e) -> p h e", h=SH),
                                                XS[:, c, :].rearrange("p (h e) -> p h e", h=SH),
                                                pr("dskip").unsqueeze(2).to_broadcast([P, SH, HD]), ALU.mult), xsd_made)
                    if c >= 1:
                        pool.wait_ge(y_squared, c)
                        rroot(rsb, ssb, 1, 1.0 / 512, 4 * EPS, y_rooted)
                    if c + 1 < NC:
                        ssd_mask(c + 1, 0)
                        ssd_mask(c + 1, 1)
                pool.wait_ge(mcol_made, 1)
                link(pool.memset(V[:, :, :, HD:HD + 1], 1.0), v_ones)

                def ml_mask(c, d):
                    pool.wait_ge(mb_read, 2 * c + d + 1)
                    v = DMM[:, c % 2, d]
                    sgn = 1 if d == 0 else -1
                    link(pool.affine_select(out=v, in_=v, compare_op=ALU.is_ge, fill=NEG, base=0,
                                            pattern=[[0, MH], [sgn, P]], channel_multiplier=-sgn), md_masked)

                def attn_root(c):
                    pool.wait_ge(a_squared, c + 1)
                    rroot(QKS[:, c, :], QKS[:, c, :], 6, 1.0 / HD, EPS, a_rooted)

                ml_mask(0, 0)
                ml_mask(0, 1)
                for c in range(NC + 1):
                    if c + 1 < NC:
                        ml_mask(c + 1, 0)
                        ml_mask(c + 1, 1)
                    if c >= 1:
                        pool.wait_ge(h_summed, c)
                        rroot(rsb, ssb, MH, 4.0 / HD, 4 * EPS, h_rooted)
                    if c >= 2:
                        attn_root(c - 2)
                attn_root(NC - 1)
                for c in range(NC):
                    pool.wait_ge(n2_squared, c + 1)
                    rroot(rsb, ssb, 1, 1.0 / D, EPS, n2_rooted)
                pool.wait_ge(idx_ready, 1)
                for j in range(2):
                    pool.wait_ge(h2_stored[j], 8 * NC)
                    pool.wait_ge(x_stored[j], 8 * NC)

                def gather(e):
                    if e >= 3:
                        pool.wait_ge(g_turned, 3 * (e - 2))
                    for dst, src, at in ((XG, h2s, idxs), (XGP, h2p, idxp)):
                        pool.indirect_dma_start(dst[e % 3], None, src[:, :], bass.IndirectOffsetOnAxis(ap=at[:, e:e + 1], axis=0)
                                                ).then_inc(gathered[e % 3], 16)

                gather(0)
                gather(1)
                for e in range(E):
                    if e + 2 < E:
                        gather(e + 2)
                    pool.wait_ge(down_scaled, 4 * (e + 1))
                    if e >= 1:
                        pool.wait_ge(scattered, 32 * e)
                    pool.indirect_dma_start(ys[:, :], bass.IndirectOffsetOnAxis(ap=idxs[:, e:e + 1], axis=0), YO[e % 2], None,
                                            compute_op=ALU.add, bounds_check=SEQS[1] - 1).then_inc(scattered, 16)
                    pool.indirect_dma_start(yp[:, :], bass.IndirectOffsetOnAxis(ap=idxp[:, e:e + 1], axis=0), YOP[e % 2], None,
                                            compute_op=ALU.add, bounds_check=SEQS[0] - 1).then_inc(scattered, 16)
                pool.wait_ge(scattered, 32 * E)

            @block.scalar
            def _(act):
                link = counter(act, act_chain)
                def square(c):
                    act.wait_ge(x_loaded[c % 4], 16 * (c // 4 + 1))
                    link(act.activation(XSF[:, 0:D], XN[c % 4], ACT.Square, accum_out=ss[:, c:c + 1]), squared)

                square(0)
                for c in range(NC):
                    if c + 1 < NC:
                        square(c + 1)
                    act.wait_ge(rooted, c + 1)
                    link(act.mul(XN[c % 4], XN[c % 4], rs[:, c:c + 1]), scaled)
                act.wait_ge(par_loaded, 16)
                link(act.activation(NEGA, pr("alog"), ACT.Exp), softplus_exp)
                act.wait_ge(softplus_in, 1)
                link(act.activation(SPE, SPE, ACT.Exp, scale=-1.0), softplus_exp)

                def evac(u):
                    sl, kind, f, g = UNITS[u]
                    act.wait_ge(proj_made, u + 1)
                    src = ps[:, u % 2, :]
                    if kind == "xbc":
                        t0, n = GROUPS[g]
                        if g == 0 and f >= 2:
                            act.wait_ge(conv_done, f - 1)
                        if g == 0 and f < 2:
                            act.wait_ge(pads_ready, 6)
                        if g == 0:
                            link(act.copy(RAW[f % 2][:, 2:258], src[:, 0:256]))
                            link(act.copy(RAW[f % 2][:, 260:516], src[:, 256:512]), proj_read)
                        else:
                            link(act.copy(RAW[f % 2][:, t0 + 4:t0 + 4 + n], src[:, 0:n]), proj_read)
                    elif kind == "z":
                        if u == U_Z:
                            act.wait_ge(wm_ready, 1)
                        link(act.copy(Z[:, g, f * 256:(f + 1) * 256], src[:, 0:256]), proj_read)
                    elif kind == "qk":
                        t0, n = GROUPS[g]
                        link(act.mul(QK[:, f, t0:t0 + n], src[:, 0:n], 1.0 if f < 2 else HD ** -0.5), proj_read)
                    elif kind == "v":
                        link(act.copy(V[:, g, :, 0:HD], src[:, 0:256].rearrange("p (h e) -> p h e", h=MH)), proj_read)
                    elif kind == "o":
                        link(act.copy(O[:, g, :], src[:, 0:256]), proj_read)
                    else:
                        link(act.copy(Z[:, g, f * 256:(f + 1) * 256], src[:, 0:256]), proj_read)

                def conv_tanh(f):
                    act.wait_ge(conv_done, f + 1)
                    if f >= 2:
                        act.wait_ge(xs_turned, 3 * min(f - 1, 4))
                        if f >= 2:
                            act.wait_ge(xbc_made, f - 1)
                    link(act.activation(XF[f % 2][:, 0:1282], ACC[f % 2][:, 0:1282], ACT.Tanh, scale=0.5), tanh_done)

                def keep_xs(f):
                    for j, (c0, n) in enumerate(((0, 4), (4, 4), (8, 2))):
                        act.wait_ge(xs_turned, 3 * f + j + 1)
                        link(act.copy(XS[:, c0:c0 + n, f * P:(f + 1) * P],
                                      ps[:, 2 + j % 2, 0:n * P].rearrange("p (c n) -> p c n", c=n)), xs_kept)

                for u in range(0, 3):
                    evac(u)
                act.wait_ge(dt_made, 1)
                link(act.activation(LND, LND, ACT.Ln), ln_done)
                for u in range(3, 6):
                    evac(u)
                conv_tanh(0)
                act.wait_ge(cs_read, 1)
                link(act.activation(ECS, CS, ACT.Exp))
                link(act.activation(TMC, TMC, ACT.Exp))
                for g in range(2):
                    link(act.activation(DECG[64 * g:64 * g + 64], TOT[64 * g:64 * g + 64, :, :, 4 * g:4 * g + 4], ACT.Exp),
                         state_exps)
                for u in range(6, 9):
                    evac(u)
                conv_tanh(1)
                keep_xs(0)
                for u in range(9, 12):
                    evac(u)
                conv_tanh(2)
                act.wait_ge(mcol_read, 1)
                link(act.activation(SC, DRC, ACT.Exp, scale=-1.0))
                link(act.activation(EML, BM, ACT.Exp, scale=-1.0), m_exps)
                keep_xs(1)
                for u in range(12, 15):
                    evac(u)
                conv_tanh(3)
                act.wait_ge(wm_diff, 1)
                link(act.activation(WM, WMX, ACT.Exp), wm_ready)
                keep_xs(2)
                for u in range(15, 18):
                    evac(u)
                conv_tanh(4)
                keep_xs(3)
                conv_tanh(5)
                act.wait_ge(xbc_made, 6)
                for j, (c0, n) in enumerate(((0, 4), (4, 4), (8, 2))):
                    act.wait_ge(b_turned, j + 1)
                    link(act.copy(BT[:, c0:c0 + n, :], ps[:, 2 + j % 2, 0:n * P].rearrange("p (c n) -> p c n", c=n)), b_kept)
                for i in range(NC):
                    evac(U_Z + 2 * i)
                    evac(U_Z + 2 * i + 1)
                def ssd_exp(c, d):
                    act.wait_ge(d_masked, 2 * c + d + 1)
                    link(act.activation(DM[:, c % 2, d, :], DM[:, c % 2, d, :], ACT.Exp), d_exp)

                ssd_exp(0, 0)
                ssd_exp(0, 1)
                for c in range(NC + 1):
                    if c >= 1:
                        act.wait_ge(y_gated, c)
                        link(act.activation(ZF[:, (c - 1) * 512:c * 512], XS[:, c - 1, :], ACT.Square,
                                            accum_out=ssb[:, 0:1]), y_squared)
                    if c < NC:
                        link(act.activation(TMP[:, 1024:1536], Z[:, c, :], ACT.Tanh, scale=0.5), z_tanh)
                    if c >= 1:
                        act.wait_ge(y_rooted, c)
                        link(act.mul(XS[:, c - 1, :], XS[:, c - 1, :], rsb[:, 0:1]), y_done)
                    if c < NC:
                        if c + 1 < NC:
                            ssd_exp(c + 1, 0)
                        evac(U_QK + 3 * c)
                        if c + 1 < NC:
                            ssd_exp(c + 1, 1)
                        evac(U_QK + 3 * c + 1)
                        evac(U_QK + 3 * c + 2)
                evac(U_ATT - 2)
                evac(U_ATT - 1)
                for i in range(NC):
                    evac(U_ATT + i)
                act.wait_ge(mrow_made, 1)
                link(act.copy(MR, ps[0:8 * NC, 3, 0:P]), mrow_kept)
                def ml_exp(c, d):
                    act.wait_ge(md_masked, 2 * c + d + 1)
                    link(act.activation(DMM[:, c % 2, d], DMM[:, c % 2, d], ACT.Exp), md_exp)

                ml_exp(0, 0)
                ml_exp(0, 1)
                for c in range(NC):
                    if c + 1 < NC:
                        ml_exp(c + 1, 0)
                    if c >= 2:
                        act.wait_ge(h_done, c - 1)
                    link(act.activation(OTH[c % 2], O[:, c, :], ACT.Tanh, scale=0.5), o_tanh)
                    evac(U_ATT + NC + c)
                    if c + 1 < NC:
                        ml_exp(c + 1, 1)
                def attn_exps(c):
                    nk, c0 = attn_keys(c)
                    act.wait_ge(s_shift, c + 1)
                    if c >= 2:
                        act.wait_ge(a_done, c - 1)
                    for h in range(AH):
                        v = PSC[c % 2][:, h, 0:nk * P]
                        link(act.activation(v, v, ACT.Exp, bias=ANMX[c % 2][:, h:h + 1], accum_out=ADEN[c % 2][:, h:h + 1]))
                    link(act.activation(AESK[c % 2], AESK[c % 2], ACT.Exp), sink_exp)

                attn_exps(0)
                for c in range(NC):
                    nk, c0 = attn_keys(c)
                    for h in range(AH):
                        act.wait_ge(p_turned, AH * c + h + 1)
                        if h == 0 and c >= 1:
                            act.wait_ge(o_made, c)
                        link(act.copy(TMP[:, h * 384:h * 384 + nk * P], ps[:, 6 + h % 2, 0:nk * P]), p_kept)
                    if c + 1 < NC:
                        attn_exps(c + 1)
                def route_exp(c):
                    act.wait_ge(lg_shift, c + 1)
                    link(act.activation(AFT, AFT, ACT.Exp, accum_out=den[:, 0:1]), lg_exp)

                for c in range(NC):
                    act.wait_ge(op_added, 2 * c + 2)
                    link(act.activation(JUNK, XO[c % 2], ACT.Square, accum_out=ssb[:, 0:1]), n2_squared)
                    act.wait_ge(n2_rooted, c + 1)
                    if c >= 2:
                        act.wait_ge(h2_stored[c % 2], 16 * (c // 2))
                        act.wait_ge(h2t_made, 2 * (c - 1))
                    link(act.mul(H2[c % 2], XO[c % 2], rsb[:, 0:1]), n2_scaled)
                    if c >= 1:
                        route_exp(c - 1)
                route_exp(NC - 1)
                for e in range(E):
                    for f in range(KF):
                        act.wait_ge(gu_made, KF * e + f + 1)
                        act.wait_ge(hid_made, KF * e + f) if e + f else None
                        link(act.activation(THG, ps[:, 2 + f % 2, 0:TOK], ACT.Tanh, scale=0.5), gate_tanh)
                    if e >= 2:
                        act.wait_ge(scattered, 32 * (e - 1))
                    for j in range(4):
                        act.wait_ge(down_part, 4 * e + j + 1)
                        hf = j % 2
                        if j < 2:
                            link(act.mul(YO[e % 2][:, hf * 512:(hf + 1) * 512], ps[:, 4 + j, :], gts[:, e:e + 1]), down_scaled)
                        else:
                            link(act.mul(YOP[e % 2][:, hf * 512:(hf + 1) * 512], ps[0:CAPP, 4 + j, :], gtp[:, e:e + 1]), down_scaled)

            @block.vector
            def _(dve):
                link = counter(dve, dve_chain)

                def tt(out, a, b, op, to=dve_chain):
                    link(dve.tensor_tensor(out, a, b, op), to)

                def ts(out, a, x, y, op0, op1=None, to=dve_chain):
                    if op1 is None:
                        link(dve.tensor_scalar(out, a, x, None, op0), to)
                    else:
                        link(dve.tensor_scalar(out, a, x, y, op0, op1), to)

                def stt(out, a, x, b, op0, op1, to=dve_chain):
                    link(dve.scalar_tensor_tensor(out=out, in0=a, scalar=x, in1=b, op0=op0, op1=op1), to)

                def wide(a, n):
                    return a.unsqueeze(2).to_broadcast([a.shape[0], a.shape[1], n])

                def quarter(b):
                    return ps[:, b, :].rearrange("p (k t) -> p k t", k=4)

                dve.wait_ge(par_loaded, 16)
                for c in range(NC):
                    for j in range(2):
                        dve.wait_ge(ht_made, 2 * c + j + 1)
                        tt(hT[:, 4 * j:4 * j + 4, c * P:(c + 1) * P], quarter(4 + 2 * (c % 2) + j), wide(pr("gmix")[:, 4 * j:4 * j + 4], P),
                           ALU.mult, ht_copied)
                dve.wait_ge(gates_made, 1)
                tt(G, ps[:, 2, 0:NC * 32].rearrange("p (c n) -> p c n", c=NC),
                   pr("gbias").unsqueeze(1).to_broadcast([P, NC, 32]), ALU.add, gates_read)
                link(dve.tensor_copy(SPV[:, :, 0:16], G[:, :, 0:16]))
                ts(SPV[:, :, 16:24], G[:, :, 24:32], -1.0, None, ALU.mult)
                ts(SPT, SPV, -1.0, None, ALU.mult)
                tt(SPE, SPV, SPT, ALU.max, softplus_in)
                dve.wait_ge(softplus_exp, 2)
                ts(SPT, SPE, 2.0, None, ALU.add)
                link(dve.reciprocal(SPT, SPT))
                tt(SPT, SPE, SPT, ALU.mult)
                tt(SP2, SPT, SPT, ALU.mult)
                ts(SPP, SP2, 1.0 / 17, None, ALU.mult)
                for k in (15, 13, 11, 9, 7, 5, 3):
                    stt(SPP, SPP, 1.0 / k, SP2, ALU.add, ALU.mult)
                stt(SPP, SPP, 1.0, SPT, ALU.add, ALU.mult)
                ts(SPP, SPP, 2.0, None, ALU.mult)
                stt(SPV, SPV, 0.0, SPP, ALU.max, ALU.add)
                ts(LND, SPV[:, :, 0:16], 1e-19, None, ALU.max, to=dt_made)
                ts(NEGA, NEGA, -1.0, None, ALU.mult)
                for d in range(2):
                    tt(AL[:, :, d, 0:8], SPV[:, :, 8 * d:8 * d + 8], NEGA[:, 8 * d:8 * d + 8].unsqueeze(1).to_broadcast([P, NC, 8]),
                       ALU.mult)
                    ts(AL[:, :, d, 8:12], SPV[:, :, 16 + 4 * d:20 + 4 * d], -1.0, None, ALU.mult, to=al_made)

                def conv(f):
                    dve.wait_ge(proj_read, 3 * f + 3)
                    if f >= 2:
                        dve.wait_ge(tanh_done, f - 1)
                    w = pr("convw")[:, 5 * f:5 * f + 5]
                    raw, acc = RAW[f % 2], ACC[f % 2][:, 0:1282]
                    ts(acc, raw[:, 0:1282], w[:, 0:1], pr("convb")[:, f:f + 1], ALU.mult, ALU.add)
                    for j in range(1, 5):
                        stt(acc, raw[:, j:j + 1282], w[:, j:j + 1], acc, ALU.mult, ALU.add,
                            conv_done if j == 4 else dve_chain)

                def silu(f):
                    dve.wait_ge(tanh_done, f + 1)
                    th = XF[f % 2][:, 0:1282]
                    ts(th, th, 0.5, 0.5, ALU.mult, ALU.add)
                    out = th if f < 4 else BC[:, f - 4, 0:1282]
                    tt(out, th, ACC[f % 2][:, 0:1282], ALU.mult, xbc_made)

                conv(0)
                dve.wait_ge(cs_made, 1)
                link(dve.tensor_copy(CS, ps[:, 5, 0:240].rearrange("p (c d n) -> p c d n", c=NC, d=2)))
                link(dve.tensor_copy(TOT, ps[:, 6, 0:240].rearrange("p (c d n) -> p c d n", c=NC, d=2)))
                tt(TMC, TOT[:, :, :, 0:8], CS[:, :, :, 0:8], ALU.subtract)
                for d in range(2):
                    tt(U[:, :, d, :], G[:, :, 16 + 4 * d:20 + 4 * d], CS[:, :, d, 8:12], ALU.subtract,
                       cs_read if d == 1 else dve_chain)
                conv(1)
                silu(0)
                dve.wait_ge(state_exps, 2)
                for d in range(2):
                    tt(WS[:, :, d, :], TMC[:, :, d, :], SPV[:, :, 8 * d:8 * d + 8], ALU.mult, ws_made if d == 1 else dve_chain)
                dve.wait_ge(ln_done, 1)
                for d in range(2):
                    tt(CS[:, :, d, 0:8], CS[:, :, d, 0:8], LND[:, :, 8 * d:8 * d + 8], ALU.subtract)
                dve.wait_ge(urow_made, 1)
                for d in range(2):
                    for j, (t0, n) in enumerate(GROUPS):
                        link(dve.tensor_copy(UROW[:, d, t0:t0 + n], ps[0:4, 2 + 3 * d + j, 0:n]))
                link(dve.tensor_copy(GROW, ps[0:4, 4, 256:276].rearrange("p (d c) -> p d c", d=2)), rows_read)
                for d in range(2):
                    for i in range(NC):
                        c = scan_chunk(d, i)
                        u, m = UROW[:, d, c * P:(c + 1) * P], MROW[:, d, c * P:(c + 1) * P]
                        if i in (0, NP):
                            link(dve.memset(MPREV[:, d, c:c + 1], NEG))
                        if d == 1:
                            u, m = u[:, ::-1], m[:, ::-1]
                        link(dve.tensor_tensor_scan(m, u, u, MPREV[:, d, c:c + 1], ALU.max, ALU.max))
                        if has_next(i):
                            cn = scan_chunk(d, i + 1)
                            tt(MPREV[:, d, cn:cn + 1], GROW[:, d, c:c + 1], m[:, P - 1:P], ALU.add)
                for d in range(2):
                    tt(UROW[:, d, :].rearrange("p (c t) -> p c t", c=NC), MROW[:, d, :].rearrange("p (c t) -> p c t", c=NC),
                       MPREV[:, d, :].unsqueeze(2).to_broadcast([4, NC, P]), ALU.subtract, rows_made)
                conv(2)
                silu(1)
                dve.wait_ge(mcol_made, 1)
                link(dve.tensor_copy(MCOL, ps[:, 5, 0:80].rearrange("p (c d n) -> p c d n", c=NC, d=2)), mcol_kept)
                link(dve.tensor_copy(DRC, ps[:, 5, 80:160].rearrange("p (c d n) -> p c d n", c=NC, d=2)))
                tt(BM, MCOL, CS[:, :, :, 8:12], ALU.add, mcol_read)
                conv(3)
                silu(2)
                dve.wait_ge(mlast_made, 1)
                tt(WMX, U, ps[:, 6, 0:80].rearrange("p (c d n) -> p c d n", c=NC, d=2), ALU.subtract, wm_diff)
                link(dve.tensor_copy(SOLD, ps[:, 6, 256:296].rearrange("p (d c n) -> p d c n", d=2, c=NC)))
                conv(4)
                silu(3)
                conv(5)
                silu(4)
                silu(5)
                link(dve.memset(PREV[:, 0, 0, :], 0.0))
                link(dve.memset(PREV[:, 0, NP, :], 0.0))
                link(dve.memset(PREV[:, 1, NP - 1, :], 0.0))
                link(dve.memset(PREV[:, 1, NC - 1, :], 0.0))
                for i in range(NC):
                    dve.wait_ge(state_made, i + 1)
                    if has_next(i):
                        for d in range(2):
                            c, cn = scan_chunk(d, i), scan_chunk(d, i + 1)
                            tt(TMP[:, 0:256].rearrange("p (h e) -> p h e", h=4), PREV[:, d, c, :].rearrange("p (h e) -> p h e", h=4),
                               wide(DECG[:, c, d, :], HD), ALU.mult)
                            tt(PREV[:, d, cn, :], ps[:, 4, 256 * d:256 * d + 256], TMP[:, 0:256], ALU.add,
                               state_kept if d == 1 else dve_chain)
                    else:
                        ts(TMP[:, 256:257], ones1, 1.0, None, ALU.mult, to=state_kept)

                def heads(a, h=SH):
                    return a.rearrange("p (h e) -> p h e", h=h)

                def ssd_exponents(c, d):
                    dve.wait_ge(csb_made, 2 * c + d + 1)
                    if c >= 2:
                        dve.wait_ge(y_made, c - 1)
                    tt(DM[:, c % 2, d, :].rearrange("p (h t) -> p h t", h=SH),
                       ps[:, 2:4, :].rearrange("p b (h t) -> p (b h) t", h=4),
                       wide(CS[:, c, d, 0:8], P), ALU.subtract, csb_read)

                def ssd_weights(c):
                    dve.wait_ge(cb_made, c + 1)
                    for d in range(2):
                        dve.wait_ge(d_exp, 2 * c + d + 1)
                        cb = ps[:, 4, 0:256].rearrange("p (g t) -> p g t", g=2)
                        for g in range(2):
                            v = DM[:, c % 2, d, g * 512:(g + 1) * 512].rearrange("p (h t) -> p h t", h=4)
                            tt(v, v, cb[:, g, :].unsqueeze(1).to_broadcast([P, 4, P]), ALU.mult, w_made)

                def ssd_output(c):
                    dve.wait_ge(y_made, c + 1)
                    dve.wait_ge(xsd_made, c + 1)
                    dve.wait_ge(z_tanh, c + 1)
                    y, t, zt = TMP[:, 0:512], TMP[:, 512:1024], TMP[:, 1024:1536]
                    tt(y, ps[:, 5, :], y, ALU.add)
                    for d in range(2):
                        tt(t.rearrange("p (g h e) -> p g h e", g=2, h=4),
                           ps[:, 6:8, 256 * d:256 * d + 256].rearrange("p g (h e) -> p g h e", h=4),
                           ECS[:, c, d, 0:8].rearrange("p (g h) -> p g h", g=2).unsqueeze(3).to_broadcast([P, 2, 4, HD]), ALU.mult, y_read if d == 1 else dve_chain)
                        tt(y, y, t, ALU.add)
                    stt(zt, zt, 1.0, Z[:, c, :], ALU.add, ALU.mult)
                    tt(XS[:, c, :], y, zt, ALU.mult, y_gated)

                ssd_exponents(0, 0)
                ssd_exponents(0, 1)
                ssd_weights(0)
                for c in range(NC + 1):
                    if c >= 1:
                        ssd_output(c - 1)
                    if c + 1 < NC:
                        ssd_exponents(c + 1, 0)
                        ssd_exponents(c + 1, 1)
                        ssd_weights(c + 1)
                dve.wait_ge(y_done, NC)
                for d, c in ((0, 0), (0, NP), (1, NP - 1), (1, NC - 1)):
                    link(dve.memset(PREVM[:, d, c], 0.0))
                def weigh_keys(i):
                    dve.wait_ge(kt_turned, i + 1)
                    if i >= 2:
                        dve.wait_ge(mstate_made, i - 1)
                    for d in range(2):
                        c = scan_chunk(d, i)
                        tt(heads(WK[i % 2][:, 256 * d:256 * d + 256], 4), heads(ps[:, 4 + 2 * (i % 2), 256 * d:256 * d + 256], 4),
                           wide(WM[:, c, d, :], HD), ALU.mult, wk_made)

                weigh_keys(0)
                for i in range(NC):
                    if i + 1 < NC:
                        weigh_keys(i + 1)
                    dve.wait_ge(mstate_made, i + 1)
                    if has_next(i):
                        for d in range(2):
                            c, cn = scan_chunk(d, i), scan_chunk(d, i + 1)
                            tmp = TMP[:, 1024:1154].rearrange("p (h e) -> p h e", h=2)
                            tt(tmp, PREVM[:, d, c], wide(SOLD[:, d, c, :], 65), ALU.mult)
                            tt(PREVM[:, d, cn], ps[:, 5 + 2 * (i % 2), 256 * d:256 * d + 130].rearrange("p (h e) -> p h e", h=2),
                               tmp, ALU.add, mstate_kept)

                def ml_exponents(c, d):
                    dve.wait_ge(mb_made, 2 * c + d + 1)
                    if c >= 2:
                        dve.wait_ge(nd_made, c - 1)
                    tt(DMM[:, c % 2, d], wide(U[:, c, d, :], P), quarter(3), ALU.subtract, mb_read)

                def ml_weights(c):
                    dve.wait_ge(st_made, c + 1)
                    for d in range(2):
                        dve.wait_ge(md_exp, 2 * c + d + 1)
                        tt(DMM[:, c % 2, d], DMM[:, c % 2, d], quarter(2), ALU.mult, mw_made)

                nd = [heads(TMP[:, 260 * d:260 * d + 260], 4) for d in range(2)]
                hs, hd = heads(TMP[:, 780:1036], 4), heads(TMP[:, 1036:1292], 4)
                t4 = heads(TMP[:, 520:780], 4)

                def ml_read(c):
                    dve.wait_ge(nd_made, c + 1)
                    for d in range(2):
                        tt(t4.rearrange("p (j q) e -> p q j e", q=2),
                           ps[:, 4:8:3, 130 * d:130 * d + 130].rearrange("p q (j e) -> p q j e", j=2),
                           SC[:, c, d, :].rearrange("p (j q) -> p q j", q=2).unsqueeze(3).to_broadcast([P, 2, 2, 65]), ALU.mult)
                        tt(nd[d], heads(ps[:, 5 + d, 0:260], 4), t4, ALU.add, nd_read)

                def ml_output(c):
                    for d in range(2):
                        dn = den[:, 4 * d:4 * d + 4]
                        raw = nd[d][:, :, HD:HD + 1].rearrange("p h e -> p (h e)")
                        stt(dn, raw, -1.0, raw, ALU.mult, ALU.max)
                        tt(dn, dn, EML[:, c, d, :], ALU.max)
                    link(dve.reciprocal(rec, den))
                    for d in range(2):
                        tt(hd if d else hs, nd[d][:, :, 0:HD], wide(rec[:, 4 * d:4 * d + 4], HD), ALU.mult)
                    tt(hs, hs, hd, ALU.add)
                    tt(hd, hs, hs, ALU.mult)
                    link(dve.tensor_reduce(out=ssb[:, 0:4], in_=hd, axis=AX, op=ALU.add), h_summed)

                def ml_gate(c):
                    dve.wait_ge(h_rooted, c + 1)
                    tt(hs, hs, wide(rsb[:, 0:4], HD), ALU.mult)
                    dve.wait_ge(o_tanh, c + 1)
                    stt(O[:, c, :], OTH[c % 2], 1.0, TMP[:, 780:1036], ALU.add, ALU.mult, h_done)

                def attn_square(c):
                    dve.wait_ge(proj_read, U_ATT + NC + c + 1)
                    tt(SCR[:, 2560:2944], Z[:, c, 0:384], Z[:, c, 0:384], ALU.mult)
                    link(dve.tensor_reduce(out=QKS[:, c, :], in_=heads(SCR[:, 2560:2944], 6), axis=AX, op=ALU.add), a_squared)

                ml_exponents(0, 0)
                ml_exponents(0, 1)
                ml_weights(0)
                for c in range(NC + 1):
                    if c >= 1:
                        ml_read(c - 1)
                    if c + 1 < NC:
                        ml_exponents(c + 1, 0)
                    if c >= 2:
                        ml_gate(c - 2)
                    if c >= 1:
                        ml_output(c - 1)
                    if c + 1 < NC:
                        ml_exponents(c + 1, 1)
                    if c >= 2:
                        attn_square(c - 2)
                    if c + 1 < NC:
                        ml_weights(c + 1)
                attn_square(NC - 1)
                ml_gate(NC - 1)
                def attn_norm(c):
                    dve.wait_ge(a_rooted, c + 1)
                    if c >= 2:
                        dve.wait_ge(a_turned, c - 1)
                    n = QKN[c % 2]
                    tt(n[:, 0:256].rearrange("p (j g e) -> p g j e", j=2, g=2),
                       Z[:, c, 0:256].rearrange("p (g j e) -> p g j e", j=2, g=2),
                       QKS[:, c, 0:4].rearrange("p (g j) -> p g j", g=2).unsqueeze(3).to_broadcast([P, 2, 2, HD]), ALU.mult)
                    tt(heads(n[:, 256:384], 2), heads(Z[:, c, 256:384], 2), wide(QKS[:, c, 4:6], HD), ALU.mult, a_normed)

                def keep_turned(c):
                    dve.wait_ge(a_turned, c + 1)
                    b = (c + 1) % 2
                    ts(QT[:, :, c * P:(c + 1) * P], ps[:, b, 0:256].rearrange("p (j t) -> p j t", j=2), pr("qg"), HD ** -0.5,
                       ALU.mult, ALU.mult)
                    ts(KT[:, c * P:(c + 1) * P], ps[:, b, 256:384], pr("kg"), None, ALU.mult, to=a_kept)

                def attn_shift(c):
                    nk, c0 = attn_keys(c)
                    b0 = (c0 - c + 1) * P
                    m, e, n = AMX[c % 2], AESK[c % 2], ANMX[c % 2]
                    dve.wait_ge(s_made, c + 1)
                    v = PSC[c % 2][:, :, 0:nk * P]
                    if c >= 2:
                        dve.wait_ge(p_turned, AH * (c - 1))
                    tt(v, ps[:, 2:6, 0:nk * P], bia[:, :, b0:b0 + nk * P], ALU.add, s_read)
                    link(dve.tensor_reduce(out=m, in_=v, axis=AX, op=ALU.max))
                    tt(m, m, pr("sink"), ALU.max)
                    tt(e, pr("sink"), m, ALU.subtract)
                    ts(n, m, -1.0, None, ALU.mult, to=s_shift)

                def attn_output(c):
                    dve.wait_ge(sink_exp, c + 1)
                    r = ADEN[c % 2]
                    tt(r, r, AESK[c % 2], ALU.add)
                    link(dve.reciprocal(r, r))
                    dve.wait_ge(o_made, c + 1)
                    tt(heads(Z[:, c, 0:256], 4), heads(ps[:, c % 2, 0:256], 4), wide(r, HD), ALU.mult, a_done)

                attn_norm(0)
                for c in range(4):
                    attn_norm(c + 1)
                    keep_turned(c)
                attn_shift(0)
                attn_shift(1)
                for c in range(NC):
                    if 5 <= c + 4 < NC:
                        attn_norm(c + 4)
                    attn_output(c)
                    if c + 4 < NC:
                        keep_turned(c + 4)
                    if c + 2 < NC:
                        attn_shift(c + 2)

                def keep_y(c):
                    for j in range(2):
                        dve.wait_ge(yt_made, 2 * c + j + 1)
                        tt(hT[:, 4 * j:4 * j + 4, c * P:(c + 1) * P], quarter(2 + j), wide(pr("gy")[:, 4 * j:4 * j + 4], P),
                           ALU.mult, yt_copied)

                def add_x(c, hf):
                    dve.wait_ge(op_made, 2 * c + hf + 1)
                    tt(XO[c % 2][:, hf * 512:(hf + 1) * 512], ps[:, hf, :], XO[c % 2][:, hf * 512:(hf + 1) * 512], ALU.add, op_added)

                def keep_h2(c):
                    if c >= 1:
                        dve.wait_ge(lg_made, c)
                    for j in range(2):
                        dve.wait_ge(h2t_made, 2 * c + j + 1)
                        tt(H2T[:, 4 * j:4 * j + 4, :], quarter(4 + j), wide(pr("gffn")[:, 4 * j:4 * j + 4], P), ALU.mult, h2t_copied)

                def route(c):
                    dve.wait_ge(lg_made, c + 1)
                    link(dve.tensor_reduce(out=mx[:, 0:1], in_=ps[:, 6, 0:E], axis=AX, op=ALU.max))
                    ts(AFT, ps[:, 6, 0:E], mx[:, 0:1], None, ALU.subtract, to=lg_shift)
                    dve.wait_ge(lg_exp, c + 1)
                    link(dve.reciprocal(rec[:, 0:1], den[:, 0:1]))
                    g, j = (2, c) if c < NP else divmod(c - NP, 4)
                    ts(AFTM[:, j, g * E:(g + 1) * E], AFT, rec[:, 0:1], None, ALU.mult, to=aff_made)

                keep_y(0)
                link(dve.memset(AFTM, -2.0))
                for c in range(NC):
                    dve.wait_ge([xo_loaded0, xo_loaded1][c % 2], 16 * (c // 2 + 1))
                    add_x(c, 0)
                    if c + 1 < NC:
                        keep_y(c + 1)
                    if c >= 1:
                        keep_h2(c - 1)
                    add_x(c, 1)
                    if c >= 1:
                        route(c - 1)
                keep_h2(NC - 1)
                route(NC - 1)
                dve.wait_ge(aff_turned, 1)
                link(dve.tensor_copy(AFF, ps[0:3 * E, 7, :]))
                for r in range(CAPS // 8):
                    n = 3 * E if r < CAPP // 8 else 2 * E
                    v8 = VAL3[0:n, 8 * r:8 * r + 8]
                    link(dve.max(v8, AFF[0:n]))
                    link(dve.max_index(idxu[0:n, 8 * r:8 * r + 8], v8, AFF[0:n]))
                    if r + 1 < CAPS // 8:
                        link(dve.match_replace(AFF[0:n], v8, AFF[0:n], -1.0))
                link(dve.tensor_copy(IDF3[0:2 * E], idxu[0:2 * E, :]))
                link(dve.tensor_copy(REV[0:2 * E, 0:CAPS], VAL3[0:2 * E, ::-1]))
                link(dve.tensor_copy(REV[0:2 * E, CAPS:2 * CAPS], IDF3[0:2 * E, ::-1]))
                link(dve.tensor_copy(IDF3[2 * E:3 * E, 0:CAPP], idxu[2 * E:3 * E, 0:CAPP]), top_done)
                dve.wait_ge(topt_made, 1)
                link(dve.tensor_copy(TC[:, 0:4 * E], ps[:, 7, 0:4 * E]))
                link(dve.tensor_copy(TC[0:CAPP, 4 * E:6 * E], ps[0:CAPP, 7, 4 * E:6 * E]))
                va, vb, ia, ib = TC[:, 0:E], TC[:, E:2 * E], TC[:, 2 * E:3 * E], TC[:, 3 * E:4 * E]
                ts(ib, ib, SEQS[1] / 2, None, ALU.add)
                tt(TC[:, 6 * E:7 * E], va, vb, ALU.is_ge)
                tt(gts, va, vb, ALU.max)
                ts(gts, gts, 0.5, None, ALU.mult)
                tt(ia, ia, ib, ALU.subtract)
                tt(ia, ia, TC[:, 6 * E:7 * E], ALU.mult)
                tt(ia, ia, ib, ALU.add)
                link(dve.tensor_copy(idxs[:, :], ia))
                link(dve.tensor_copy(idxp[:, :], TC[0:CAPP, 5 * E:6 * E]))
                ts(gtp, TC[0:CAPP, 4 * E:5 * E], 0.5, None, ALU.mult, to=idx_ready)

                def copy_tokens(e):
                    for j, (k0, n) in enumerate(((0, 3), (3, 3), (6, 2))):
                        dve.wait_ge(g_turned, 3 * e + j + 1)
                        tt(XT[e % 2][:, k0:k0 + n, :], ps[:, j % 2, 0:n * TOK].rearrange("p (k t) -> p k t", k=n),
                           wide(pr("gffn")[:, k0:k0 + n], TOK), ALU.mult, g_copied)

                copy_tokens(0)
                for e in range(E):
                    for f in range(KF):
                        dve.wait_ge(gate_tanh, KF * e + f + 1)
                        if f == 0 and e >= 1:
                            dve.wait_ge(down_made, e)
                        stt(HID[:, f, :], THG, 1.0, ps[:, 2 + f % 2, 0:TOK], ALU.add, ALU.mult)
                        tt(HID[:, f, :], HID[:, f, :], ps[:, 2 + f % 2, TOK:2 * TOK], ALU.mult, hid_made)
                    if e + 1 < E:
                        copy_tokens(e + 1)

            @block.tensor
            def _(pe):
                fence = counter(pe, pe_fence)

                def mm(out, a, b, start=True, stop=True):
                    return pe.matmul(out, a, b, start=start, stop=stop)

                for c in range(NC):
                    pe.wait_ge(scaled, c + 1)
                    for j in range(2):
                        if c >= 2:
                            pe.wait_ge(ht_copied, 2 * c - 3 + j)
                        for k in range(4):
                            last = pe.transpose(ps[:, 4 + 2 * (c % 2) + j, k * P:(k + 1) * P],
                                                XN[c % 4][:, (4 * j + k) * P:(4 * j + k + 1) * P], ident)
                        last.then_inc(ht_made, 1)
                pe.wait_ge(wg_loaded, 32)
                pe.wait_ge(ht_copied, 2 * NC)
                for c in range(NC):
                    for k in range(KD):
                        last = mm(ps[:, 2, c * 32:(c + 1) * 32], hT[:, k, c * P:(c + 1) * P], wg[:, k, :], k == 0, k == KD - 1)
                last.then_inc(gates_made, 1)

                def unit(u):
                    sl, kind, f, g = UNITS[u]
                    pe.wait_ge([ring_loaded0, ring_loaded1][sl % 2], 16 * (sl // 2 + 1))
                    if u >= 2:
                        pe.wait_ge(proj_read, u - 1)
                    for k in range(KD):
                        if kind in ("xbc", "qk"):
                            t0, n = GROUPS[g]
                            last = mm(ps[:, u % 2, 0:n], ring[sl % 2][:, k, (f % 2) * P:(f % 2 + 1) * P], hT[:, k, t0:t0 + n],
                                      k == 0, k == KD - 1)
                        else:
                            last = mm(ps[:, u % 2, 0:256], hT[:, k, g * P:(g + 1) * P], ring[sl % 2][:, k, :], k == 0, k == KD - 1)
                    last.then_inc(proj_made, 1)
                    if u in LAST_UNIT:
                        pe.wait_ge(proj_made, u + 1)
                        pe.sem_inc(slice_used, 1)

                def turn_xs(f):
                    pe.wait_ge(xbc_made, f + 1)
                    for j, (c0, n) in enumerate(((0, 4), (4, 4), (8, 2))):
                        if f or j == 2:
                            pe.wait_ge(xs_kept, 3 * f + (1 if j == 2 else 0))
                        for c in range(c0, c0 + n):
                            last = pe.transpose(ps[:, 2 + j % 2, (c - c0) * P:(c - c0 + 1) * P],
                                                XF[f % 2][:, tcol(c):tcol(c) + P], ident)
                        last.then_inc(xs_turned, 1)

                for u in range(0, 6):
                    unit(u)
                pe.wait_ge(al_made, 2)
                csp = ps[:, 5, 0:240].rearrange("p (c d n) -> p c d n", c=NC, d=2)
                for d in range(2):
                    mm(csp[:, :, d, :], tri[d], AL[:, :, d, :])
                last = mm(ps[:, 6, 0:240], ones1.to_broadcast([P, P]), AL)
                last.then_inc(cs_made, 1)
                for u in range(6, 9):
                    unit(u)
                pe.wait_ge(cs_read, 1)
                for d in range(2):
                    for c in range(NC):
                        pe.transpose(ps[0:4, 2 + 3 * d + c // 4, (c % 4) * P:(c % 4 + 1) * P], U[:, c, d, :], ident)
                for d in range(2):
                    for c in range(NC):
                        last = mm(ps[0:4, 4, 256 + d * NC + c:257 + d * NC + c], AL[:, c, d, 8:12], ones1)
                last.then_inc(urow_made, 1)
                pe.wait_ge(rows_read, 1)
                turn_xs(0)
                for u in range(9, 12):
                    unit(u)
                pe.wait_ge(rows_made, 2)
                for d in range(2):
                    for c in range(NC):
                        for row, at in ((MROW, 0), (UROW, 80)):
                            last = mm(ps[:, 5, at + c * 8 + d * 4:at + c * 8 + d * 4 + 4], row[:, d, c * P:(c + 1) * P], ident[0:4, 0:4])
                last.then_inc(mcol_made, 1)
                turn_xs(1)
                for u in range(12, 15):
                    unit(u)
                pe.wait_ge(mcol_kept, 1)
                pe.wait_ge(m_exps, 1)
                mlp = ps[:, 6, 0:80].rearrange("p (c d n) -> p c d n", c=NC, d=2)
                sop = ps[:, 6, 256:296].rearrange("p (d c n) -> p d c n", d=2, c=NC)
                for d in range(2):
                    at = ident[:, last_of(d):last_of(d) + 1]
                    mm(mlp[:, :, d, :], at.to_broadcast([P, P]), MCOL[:, :, d, :])
                    for q in range(2):
                        last = mm(sop[64 * q:64 * q + 64, d], at.to_broadcast([P, HD]),
                                  SC[:, :, d, :].rearrange("p c (j q) -> p c j q", q=2)[:, :, :, q])
                last.then_inc(mlast_made, 1)
                turn_xs(2)
                for u in range(15, 18):
                    unit(u)
                turn_xs(3)
                pe.wait_ge(xbc_made, 6)
                pe.wait_ge(xs_kept, 12)
                for j, (c0, n) in enumerate(((0, 4), (4, 4), (8, 2))):
                    if j == 2:
                        pe.wait_ge(b_kept, 1)
                    for c in range(c0, c0 + n):
                        last = pe.transpose(ps[:, 2 + j % 2, (c - c0) * P:(c - c0 + 1) * P], BC[:, 0, tcol(c):tcol(c) + P], ident)
                    last.then_inc(b_turned, 1)
                pe.wait_ge(b_kept, 3)
                for i in range(NC):
                    unit(U_Z + 2 * i)
                    unit(U_Z + 2 * i + 1)
                    pe.wait_ge(dxs_made, 2 * i + 2)
                    if i >= 1:
                        pe.wait_ge(state_kept, i)
                    for d in range(2):
                        for g in range(2):
                            last = mm(ps[64 * g:64 * g + 64, 4, 256 * d:256 * d + 256], BT[:, scan_chunk(d, i), 64 * g:64 * g + 64],
                                      DXS[:, i % 2, d, 256 * g:256 * g + 256])
                    last.then_inc(state_made, 1)
                pe.wait_ge(state_kept, NC)

                def ssd_cumulative(c, d):
                    if 2 * c + d >= 1:
                        pe.wait_ge(csb_read, 2 * c + d)
                    for h in range(SH):
                        last = mm(ps[:, 2 + h // 4, (h % 4) * P:(h % 4 + 1) * P],
                                  AL[:, c, d, h:h + 1].to_broadcast([P, P]), tri[d])
                    last.then_inc(csb_made, 1)

                def ssd_products(c):
                    t = tcol(c)
                    if c >= 1:
                        pe.wait_ge(w_made, 4 * c)
                    fence(mm(ps[:, 4, 0:P], BC[0:64, 0, t:t + P], BC[0:64, 1, t:t + P]))
                    mm(ps[:, 4, P:2 * P], BC[64:P, 0, t:t + P], BC[64:P, 1, t:t + P]).then_inc(cb_made, 1)

                def ssd_sum(c):
                    t = tcol(c)
                    pe.wait_ge(w_made, 4 * (c + 1))
                    if c >= 1:
                        pe.wait_ge(y_read, c)
                    for h in range(SH):
                        for d in range(2):
                            mm(ps[:, 5, h * HD:(h + 1) * HD], DM[:, c % 2, d, h * P:(h + 1) * P], XS[:, c, h * HD:(h + 1) * HD],
                               d == 0, d == 1)
                    for d in range(2):
                        for g in range(2):
                            last = mm(ps[:, 6 + g, 256 * d:256 * d + 256], BC[64 * g:64 * g + 64, 1, t:t + P],
                                      PREV[64 * g:64 * g + 64, d, c, :])
                    last.then_inc(y_made, 1)

                ssd_cumulative(0, 0)
                ssd_cumulative(0, 1)
                ssd_products(0)
                for c in range(NC):
                    if c + 1 < NC:
                        ssd_cumulative(c + 1, 0)
                    unit(U_QK + 3 * c)
                    if c + 1 < NC:
                        ssd_cumulative(c + 1, 1)
                    unit(U_QK + 3 * c + 1)
                    unit(U_QK + 3 * c + 2)
                    if c + 1 < NC:
                        ssd_products(c + 1)
                    ssd_sum(c)
                unit(U_ATT - 2)
                unit(U_ATT - 1)
                pe.wait_ge(y_gated, NC)
                pe.wait_ge(v_ones, 1)
                pe.wait_ge(proj_read, U_ATT)
                def turn_keys(i):
                    if i >= 2:
                        pe.wait_ge(wk_made, 2 * (i - 1))
                    for d in range(2):
                        c = scan_chunk(d, i)
                        for q in range(2):
                            last = pe.transpose(ps[:, 4 + 2 * (i % 2), 256 * d + q * P:256 * d + (q + 1) * P],
                                                QK[:, 2 + q, c * P:(c + 1) * P], ident)
                    last.then_inc(kt_turned, 1)

                turn_keys(0)
                for i in range(NC):
                    if i + 1 < NC:
                        turn_keys(i + 1)
                    unit(U_ATT + i)
                    pe.wait_ge(wk_made, 2 * i + 2)
                    if i >= 2:
                        pe.wait_ge(mstate_kept, 2 * sum(has_next(j) for j in range(i - 1)))
                    for d in range(2):
                        c = scan_chunk(d, i)
                        for h in range(MH):
                            q = h % 2
                            last = mm(ps[64 * q:64 * q + 64, 5 + 2 * (i % 2), 256 * d + 65 * (h // 2):256 * d + 65 * (h // 2) + 65],
                                      WK[i % 2][:, 256 * d + HD * h:256 * d + HD * (h + 1)], V[:, c, h, :])
                    last.then_inc(mstate_made, 1)
                pe.wait_ge(mstate_kept, 2 * sum(has_next(j) for j in range(NC)))
                pe.transpose(ps[0:8 * NC, 3, 0:P], MCOL.rearrange("p c d n -> p (c d n)"), ident).then_inc(mrow_made, 1)
                pe.wait_ge(mrow_kept, 1)

                def ml_rows(c, d):
                    if 2 * c + d >= 1:
                        pe.wait_ge(mb_read, 2 * c + d)
                    for h in range(MH):
                        r = 8 * c + 4 * d + h
                        last = mm(ps[:, 3, h * P:(h + 1) * P], ident[0:8 * NC, r:r + 1].to_broadcast([8 * NC, P]), MR)
                    last.then_inc(mb_made, 1)

                def ml_products(c):
                    if c >= 1:
                        pe.wait_ge(mw_made, 2 * c)
                    for h in (0, 2, 1, 3):
                        if h == 1:
                            fence(last)
                        b = 64 * (h % 2)
                        last = mm(ps[:, 2, h * P:(h + 1) * P], QK[b:b + 64, 2 + h // 2, c * P:(c + 1) * P],
                                  QK[b:b + 64, h // 2, c * P:(c + 1) * P])
                    last.then_inc(st_made, 1)

                def ml_sum(c):
                    pe.wait_ge(mw_made, 2 * c + 2)
                    if c >= 1:
                        pe.wait_ge(nd_read, 2 * c)
                    for d in range(2):
                        for h in range(MH):
                            mm(ps[:, 5 + d, 65 * h:65 * h + 65], DMM[:, c % 2, d, h, :], V[:, c, h, :])
                    for h in (0, 2, 1, 3):
                        b = 64 * (h % 2)
                        for d in range(2):
                            last = mm(ps[:, 4 + 3 * (h % 2), 130 * d + 65 * (h // 2):130 * d + 65 * (h // 2) + 65],
                                      QK[b:b + 64, h // 2, c * P:(c + 1) * P], PREVM[b:b + 64, d, c, h // 2, :])
                    last.then_inc(nd_made, 1)

                ml_rows(0, 0)
                ml_products(0)
                ml_rows(0, 1)
                for c in range(NC):
                    if c + 1 < NC:
                        ml_rows(c + 1, 0)
                    unit(U_ATT + NC + c)
                    if c + 1 < NC:
                        ml_rows(c + 1, 1)
                        ml_products(c + 1)
                    ml_sum(c)
                def turn_qk(c):
                    pe.wait_ge(a_normed, c + 1)
                    if c >= 2:
                        pe.wait_ge(a_kept, c - 1)
                    if c >= 5:
                        pe.wait_ge(a_done, c - 4)
                    for j in range(3):
                        last = pe.transpose(ps[:, (c + 1) % 2, j * P:(j + 1) * P], QKN[c % 2][:, j * P:(j + 1) * P], ident)
                    last.then_inc(a_turned, 1)

                def scores(c):
                    nk, c0 = attn_keys(c)
                    pe.wait_ge(a_kept, min(c + 2, NC))
                    if c >= 1:
                        pe.wait_ge(s_read, c)
                    for h in range(AH):
                        g, j = h // 2, h % 2
                        last = mm(ps[:, 2 + h, 0:nk * P], QT[64 * g:64 * g + 64, j, c * P:(c + 1) * P],
                                  KT[64 * g:64 * g + 64, c0 * P:(c0 + nk) * P])
                    last.then_inc(s_made, 1)

                pe.wait_ge(proj_read, len(UNITS))
                for c in range(4):
                    turn_qk(c)
                pe.wait_ge(nd_read, 2 * NC)
                scores(0)
                scores(1)
                for c in range(NC):
                    nk, c0 = attn_keys(c)
                    pe.wait_ge(sink_exp, c + 1)
                    for h in range(AH):
                        if AH * c + h >= 2:
                            pe.wait_ge(p_kept, AH * c + h - 1)
                        for b in range(nk):
                            last = pe.transpose(ps[:, 6 + h % 2, b * P:(b + 1) * P], PSC[c % 2][:, h, b * P:(b + 1) * P], ident)
                        last.then_inc(p_turned, 1)
                    pe.wait_ge(a_kept, min(c + 4, NC))
                    if c >= 2:
                        pe.wait_ge(a_done, c - 1)
                    for h in range(AH):
                        pe.wait_ge(p_kept, AH * c + h + 1)
                        g = h // 2
                        for b in range(nk):
                            last = mm(ps[:, c % 2, HD * h:HD * h + HD],
                                      TMP[:, h * 384 + b * P:h * 384 + (b + 1) * P],
                                      Z[:, c0 + b, 384 + 64 * g:448 + 64 * g], b == 0, b == nk - 1)
                    last.then_inc(o_made, 1)
                    if c + 4 < NC:
                        turn_qk(c + 4)
                    if c + 2 < NC:
                        scores(c + 2)
                pe.wait_ge(a_done, NC)
                pe.wait_ge(y_done, NC)

                def turn_y(c):
                    tiles = [Z[:, c, 0:P], Z[:, c, P:2 * P]] + [XS[:, c, k * P:(k + 1) * P] for k in range(4)] \
                        + [O[:, c, 0:P], O[:, c, P:2 * P]]
                    for j in range(2):
                        if c >= 1:
                            pe.wait_ge(yt_copied, 2 * c - 1 + j)
                        for k in range(4):
                            last = pe.transpose(ps[:, 2 + j, k * P:(k + 1) * P], tiles[4 * j + k], ident)
                        last.then_inc(yt_made, 1)

                turn_y(0)
                pe.wait_ge(wo_loaded, 16)

                def out_proj(c, hf):
                    pe.wait_ge(yt_copied, 2 * c + 2)
                    if c >= 1:
                        pe.wait_ge(op_added, 2 * c - 1 + hf)
                    for k in range(KD):
                        last = mm(ps[:, hf, :], hT[:, k, c * P:(c + 1) * P], WO[:, k, hf * 512:(hf + 1) * 512], k == 0, k == KD - 1)
                    last.then_inc(op_made, 1)

                for c in range(NC + 1):
                    if c < NC:
                        out_proj(c, 0)
                    if c + 1 < NC:
                        turn_y(c + 1)
                    if c >= 1:
                        pe.wait_ge(n2_scaled, c)
                        for j in range(2):
                            if c >= 2:
                                pe.wait_ge(h2t_copied, 2 * c - 3 + j)
                            for k in range(4):
                                last = pe.transpose(ps[:, 4 + j, k * P:(k + 1) * P],
                                                    H2[(c - 1) % 2][:, (4 * j + k) * P:(4 * j + k + 1) * P], ident)
                            last.then_inc(h2t_made, 1)
                    if c < NC:
                        out_proj(c, 1)
                    if c >= 1:
                        pe.wait_ge(h2t_copied, 2 * c)
                        if c >= 2:
                            pe.wait_ge(lg_shift, c - 1)
                        for k in range(KD):
                            last = mm(ps[:, 6, 0:E], H2T[:, k, :], pr("router")[:, k * E:(k + 1) * E], k == 0, k == KD - 1)
                        last.then_inc(lg_made, 1)
                pe.wait_ge(aff_made, NC)
                for j in range(4):
                    last = pe.transpose(ps[0:3 * E, 7, j * P:(j + 1) * P], AFTM[:, j, :], ident)
                last.then_inc(aff_turned, 1)
                pe.wait_ge(top_done, 1)
                for at, src, rev in ((0, VAL3, REV[0:2 * E, 0:CAPS]), (2 * E, IDF3, REV[0:2 * E, CAPS:2 * CAPS])):
                    mm(ps[:, 7, at:at + E], src[0:E, :], ident[0:E, 0:E])
                    mm(ps[:, 7, at + E:at + 2 * E], rev, ident[0:2 * E, E:2 * E])
                mm(ps[0:CAPP, 7, 4 * E:5 * E], VAL3[:, 0:CAPP], ident[0:3 * E, 2 * E:3 * E])
                mm(ps[0:CAPP, 7, 5 * E:6 * E], IDF3[:, 0:CAPP], ident[0:3 * E, 2 * E:3 * E]).then_inc(topt_made, 1)
                pe.wait_ge(idx_ready, 1)

                def turn_tokens(e):
                    pe.wait_ge(gathered[e % 3], 32 * (e // 3 + 1))
                    for j, (k0, n) in enumerate(((0, 3), (3, 3), (6, 2))):
                        g = 3 * e + j
                        if g >= 1:
                            pe.wait_ge(g_copied, g - 1 if j == 2 else 3 * e) if (j == 2 or e >= 1) else None
                        for k in range(n):
                            src = slice((k0 + k) * P, (k0 + k + 1) * P)
                            pe.transpose(ps[:, j % 2, k * TOK:k * TOK + CAPS], XG[e % 3][:, src], ident)
                            last = pe.transpose(ps[:, j % 2, k * TOK + CAPS:(k + 1) * TOK], XGP[e % 3][:, src], ident[0:CAPP, 0:CAPP])
                        last.then_inc(g_turned, 1)

                turn_tokens(0)
                for e in range(E):
                    pe.wait_ge([ew_loaded0, ew_loaded1][e % 2], 48 * (e // 2 + 1))
                    pe.wait_ge(g_copied, 3 * e + 3)
                    for f in range(KF):
                        n = KF * e + f
                        if n >= 2:
                            pe.wait_ge(hid_made, n - 1)
                        for w, at in ((EG, 0), (EU, TOK)):
                            for k in range(KD):
                                last = mm(ps[:, 2 + f % 2, at:at + TOK], w[e % 2][:, k, f * P:(f + 1) * P], XT[e % 2][:, k, :],
                                          k == 0, k == KD - 1)
                        last.then_inc(gu_made, 1)
                    if e + 1 < E:
                        turn_tokens(e + 1)
                    pe.wait_ge(hid_made, KF * e + KF)
                    if e >= 1:
                        pe.wait_ge(down_scaled, 4 * e)
                    for j in range(4):
                        hf = j % 2
                        m = CAPS if j < 2 else CAPP
                        t0 = 0 if j < 2 else CAPS
                        for f in range(KF):
                            last = mm(ps[0:m, 4 + j, :], HID[:, f, t0:t0 + m], ED[e % 2][:, f, hf * 512:(hf + 1) * 512],
                                      f == 0, f == KF - 1)
                        last.then_inc(down_part, 1)
                    pe.wait_ge(down_part, 4 * e + 4)
                    pe.sem_inc(down_made, 1)
          nc.gpsimd.dma_reset(rng)
          nc.all_engine_barrier()
          nc.sync.sem_clear(rng)
          nc.all_engine_barrier()


_BIG = [("w_in", D_IN), ("w_out", D), ("w_gate", FF), ("w_up", FF), ("w_down", D)]


def constants():
    i = np.arange(P)
    eye = np.eye(P, dtype=np.float32)
    le = (i[:, None] <= i[None, :]).astype(np.float32)
    cst = np.concatenate([eye, le, le.T, np.ones((P, 1), np.float32)], axis=1)
    rel = np.arange(-(NREL // 2), NREL // 2 + 1)
    half, exact = 16, 8
    n = np.abs(rel)
    large = exact + (np.log(np.maximum(n, 1) / exact) / np.log(128 / exact) * (half - exact)).astype(np.int32)
    bucket = (rel > 0).astype(np.int32) * half + np.where(n < exact, n, np.minimum(large, half - 1))
    hot = np.zeros((33, NREL), np.float32)
    hot[bucket, np.arange(NREL)] = 1.0
    hot[32] = np.where(n <= 128, 0.0, NEG)
    return np.ascontiguousarray(cst), hot


def parameters(x):
    def col(a, k):
        return a.reshape(DEPTH, k, P).transpose(0, 2, 1)

    def row(a):
        a = a.reshape(DEPTH, 1, -1)
        return np.broadcast_to(a, (DEPTH, P, a.shape[2]))

    def twice(a):
        return np.concatenate([a, a], axis=1)[:, :, None]

    cw = x["ssd_conv_w"].reshape(DEPTH, 5, 6, P).transpose(0, 3, 2, 1).reshape(DEPTH, P, 30)
    rt = x["router"].reshape(DEPTH, KD, P, E).transpose(0, 2, 1, 3).reshape(DEPTH, P, KD * E)
    parts = dict(gmix=col(x["mix_norm"], 8), gffn=col(x["ffn_norm"], 8),
                 gy=np.concatenate([np.ones((DEPTH, P, 2), np.float32), col(x["ssd_norm"], 4), col(x["mlstm_norm"], 2)], axis=2),
                 convw=cw, convb=col(x["ssd_conv_b"], 6), qg=twice(x["attn_q_norm"]), kg=twice(x["attn_k_norm"]),
                 sink=row(x["attn_sink"]),
                 gbias=np.concatenate([row(x["ssd_dt_bias"]), row(x["mlstm_i_bias"]), row(x["mlstm_f_bias"])], axis=2),
                 alog=row(x["ssd_a_log"]), dskip=row(x["ssd_d"]), router=rt)
    return np.ascontiguousarray(np.concatenate([parts[n] for n in PAR], axis=2)).reshape(DEPTH * P, NPAR)


def kernel(**inputs):
    import concourse.bacc as bacc
    from concourse.bass_utils import run_bass_kernel_spmd

    x = {k: np.asarray(v) for k, v in inputs.items()}
    cst, hot = constants()
    table = np.concatenate([x["rel_bias"], np.ones((1, AH), np.float32)], axis=0)
    arrays = {n: np.ascontiguousarray(x[n]).reshape(-1, w) for n, w in _BIG}
    arrays.update(flip=np.ascontiguousarray(np.eye(P, dtype=np.float32)[::-1]), par=parameters(x), cst=cst, onehot=np.concatenate([hot, table], axis=1),
                  x_prompt=np.ascontiguousarray(x["x_prompt"][0]), x_sample=np.ascontiguousarray(x["x_sample"][0]))
    nc = bacc.Bacc("TRN2", target_bir_lowering=False, num_devices=1)
    f32 = mybir.dt.float32
    ap = {n: nc.dram_tensor(n, a.shape, f32, kind="ExternalInput").ap() for n, a in arrays.items()}
    yp = nc.dram_tensor("y_prompt", (SEQS[0], D), f32, kind="ExternalOutput").ap()
    ys = nc.dram_tensor("y_sample", (SEQS[1], D), f32, kind="ExternalOutput").ap()
    btab = nc.dram_tensor("bias_table", (AH, 512), f32, kind="Internal").ap()
    h2p = nc.dram_tensor("h2_prompt", (SEQS[0], D), f32, kind="Internal").ap()
    h2s = nc.dram_tensor("h2_sample", (SEQS[1], D), f32, kind="Internal").ap()
    program(nc, ap["w_in"], ap["w_out"], ap["w_gate"], ap["w_up"], ap["w_down"], ap["par"], ap["cst"], ap["onehot"],
            ap["x_prompt"], ap["x_sample"], yp, ys, btab, h2p, h2s, ap["flip"])
    r = run_bass_kernel_spmd(nc, [arrays], core_ids=[0]).results[0]
    return r["y_prompt"][None], r["y_sample"][None]
```

```python
import concourse.bass as bass
from concourse import mybir
from contextlib import ExitStack
import numpy as np

DEPTH, D = 2, 1024
SEQS = (256, 1024)
T = sum(SEQS)
P = 128
NC = T // P
NP = SEQS[0] // P
KD = D // P
HD = 64
SH, MH, AH = 8, 4, 4
E, CAPS, CAPP, FF = 16, 128, 32, 512
TOK = CAPS + CAPP
KF = FF // P
THIRDS = ((0, 3), (3, 3), (6, 2))
D_IN = 2848
NEG = -1e30
EPS = 1e-6

PAR = {}
_n = 0
for _name, _w in (("gmix", 8), ("gffn", 8), ("gy", 8), ("convw", 30), ("convb", 6), ("qg", 1), ("kg", 1),
                  ("sink", 4), ("gbias", 32), ("alog", 16), ("dskip", 8), ("router", 128)):
    PAR[_name] = (_n, _n + _w)
    _n += _w
NPAR = _n
NCST = 3 * P + 1
NREL = 511

SLICES = [("xbc", 1024), ("xbc", 1280), ("xbc", 1536), ("z", 512), ("z", 768), ("qk", 1808), ("qk", 2064),
          ("v", 2320), ("o", 2576), ("att", 0), ("att", 256)]
GROUPS = [(0, 512), (512, 512), (1024, 256)]
UNITS = []
for _s, (_k, _c) in enumerate(SLICES):
    _i = [k for k, _ in SLICES[:_s]].count(_k)
    if _k in ("xbc", "qk"):
        UNITS += [(_s, _k, 2 * _i + h, g) for h in range(2) for g in range(3)]
    else:
        UNITS += [(_s, _k, _i, c) for c in range(NC)]
U_XBC, U_Z, U_QK, U_VO, U_ATT = 0, 18, 38, 50, 70
LAST_UNIT = [max(u for u, x in enumerate(UNITS) if x[0] == s) for s in range(len(SLICES))]


ORDER = [*range(NP, NC), *range(NP)]
QK_FIRST = 5
Z_AHEAD = 2


def z_units(n):
    return range(U_Z + Z_AHEAD + 2 * n, U_Z + Z_AHEAD + 2 * n + 2)


def in_seq(c):
    return (0, NP) if c < NP else (NP, NC)


def scan_chunk(d, i):
    if d == 0:
        return i
    lo, hi = in_seq(i)
    return lo + hi - 1 - i


def has_next(i):
    return i not in (NP - 1, NC - 1)


STEPS = [i for i in range(NC) if has_next(i)]


def tcol(c):
    return P * c + (2 if c >= NP else 0)


def attn_keys(c):
    lo, hi = in_seq(c)
    c0 = max(c - 1, lo)
    return min(c + 1, hi - 1) - c0 + 1, c0


def program(nc, wi, wo, wga, wup, wdn, par, cst, onehot, xp, xs_in, yp, ys, btab, h2p, h2s, flip):
    F32, U32 = mybir.dt.float32, mybir.dt.uint32
    ALU, ACT = mybir.AluOpType, mybir.ActivationFunctionType
    AX = mybir.AxisListType.X
    ctx = ExitStack()
    with ctx:
        def sb(name, cols, dt=F32, parts=P):
            return ctx.enter_context(nc.sbuf_tensor(name, [parts, cols], dt))

        HT = sb("HT", KD * T)
        MID = sb("MID", 2 * NC * 512 + 2 * 1284 + 2 * NC * 256 + 5120 + NC * 516)
        RING = sb("RING", 2 * KD * 256)
        SCR = sb("SCR", 4096)
        TMP = sb("TMP", 1536)
        cstt = sb("cstt", NCST)
        part = sb("part", NPAR)
        bias = sb("bias", AH * 384)
        small = sb("small", 1980)
        idxs = sb("idxs", E, U32)
        idxp = sb("idxp", E, U32, CAPP)
        idxus = sb("idxus", CAPS, U32, 2 * E)
        idxup = sb("idxup", CAPP, U32, E)
        ps = ctx.enter_context(nc.psum_tensor("ps", [P, 8, 512], F32))

        o = 0

        def take(n):
            nonlocal o
            o += n
            return MID[:, o - n:o]

        hT = HT[:, :].rearrange("p (k t) -> p k t", k=KD)
        ZF = take(NC * 512)
        Z = ZF.rearrange("p (c n) -> p c n", c=NC)
        XSF = take(NC * 512)
        XS = XSF.rearrange("p (c n) -> p c n", c=NC)
        bc_at = o
        BC = take(2 * 1284).rearrange("p (w t) -> p w t", w=2)
        pv_at = o
        PREV = take(2 * NC * 256).rearrange("p (d c n) -> p d c n", d=2, c=NC)
        qk_at = o
        QK = take(5120).rearrange("p (f t) -> p f t", f=4)
        VO = take(NC * 516)
        V = VO[:, 0:NC * 260].rearrange("p (c h e) -> p c h e", c=NC, h=MH)
        O = VO[:, NC * 260:NC * 516].rearrange("p (c n) -> p c n", c=NC)
        XF = [MID[:, qk_at + 1284 * j:qk_at + 1284 * (j + 1)] for j in range(2)]
        UROW = VO[0:4, 0:2 * T].rearrange("p (d t) -> p d t", d=2)
        MROW = VO[0:4, 2 * T:4 * T].rearrange("p (d t) -> p d t", d=2)
        PREVM = MID[:, pv_at:pv_at + 2 * NC * 130].rearrange("p (d c h e) -> p d c h e", d=2, c=NC, h=2)
        QT = MID[:, bc_at:bc_at + 2 * T].rearrange("p (j t) -> p j t", j=2)
        WO = MID[:, pv_at:pv_at + KD * D].rearrange("p (k n) -> p k n", k=KD)
        ring = [RING[:, j * 2048:(j + 1) * 2048].rearrange("p (k n) -> p k n", k=KD) for j in range(2)]
        XN = [SCR[:, j * D:(j + 1) * D] for j in range(4)]
        RAW = [SCR[:, 1288 * j:1288 * (j + 1)] for j in range(2)]
        ACC = [SCR[:, 2576:2576 + 1284], TMP[:, 0:1284]]
        BT = SCR[:, 0:NC * P].rearrange("p (c n) -> p c n", c=NC)
        DXS = SCR[:, 1280:1280 + 2048].rearrange("p (b d n) -> p b d n", b=2, d=2)
        DM = SCR[:, :].rearrange("p (b d n) -> p b d n", b=2, d=2)
        OTH = [SCR[:, 2304:2560], SCR[:, 3072:3328]]
        QKN = [RING[:, 3328 + 384 * j:3328 + 384 * (j + 1)] for j in range(2)]
        QKS = SCR[:, 3328:3328 + 6 * NC].rearrange("p (c n) -> p c n", c=NC)
        WK = [TMP[:, 512 * j:512 * (j + 1)] for j in range(2)]
        DMM = SCR[:, 0:2048].rearrange("p (b d h t) -> p b d h t", b=2, d=2, h=MH)
        KT = RING[:, 0:T]
        PSC = [SCR[:, 1536 * b:1536 * (b + 1)].rearrange("p (h k) -> p h k", h=AH) for b in range(2)]
        ident, tri = cstt[:, 0:P], [cstt[:, P:2 * P], cstt[:, 2 * P:3 * P]]
        ones1 = cstt[:, 3 * P:3 * P + 1]
        bia = bias[:, :].rearrange("p (h k) -> p h k", h=AH)
        EW = [MID[:, j * 12288:(j + 1) * 12288] for j in range(2)]
        EG = [w[:, 0:4096].rearrange("p (k f) -> p k f", k=KD) for w in EW]
        EU = [w[:, 4096:8192].rearrange("p (k f) -> p k f", k=KD) for w in EW]
        ED = [w[:, 8192:12288].rearrange("p (k n) -> p k n", k=KF) for w in EW]
        XG = [HT[:, j * D:(j + 1) * D] for j in range(3)]
        XGP = [HT[0:CAPP, (3 + j) * D:(4 + j) * D] for j in range(3)]
        XT = [HT[:, 6 * D + 1280 * j:6 * D + 1280 * (j + 1)].rearrange("p (k t) -> p k t", k=KD) for j in range(2)]
        HID = HT[:, 8704:8704 + KF * TOK].rearrange("p (f t) -> p f t", f=KF)
        THG = HT[:, 9344:9344 + TOK]
        YO = [SCR[:, j * D:(j + 1) * D] for j in range(2)]
        YOP = [SCR[0:CAPP, (2 + j) * D:(3 + j) * D] for j in range(2)]
        XO = [RING[:, 1280 + j * D:1280 + (j + 1) * D] for j in range(2)]
        H2 = [SCR[:, (2 + j) * D:(3 + j) * D] for j in range(2)]
        H2T = RING[:, 0:D].rearrange("p (k t) -> p k t", k=KD)
        JUNK = SCR[:, 0:D]
        AFF = TMP[0:2 * E, 0:512]
        VALS = TMP[0:2 * E, 512:512 + CAPS]
        IDFS = TMP[0:2 * E, 640:640 + CAPS]
        REV = TMP[0:2 * E, 1088:1088 + 2 * CAPS]
        AFP = RING[0:E, 3392:3392 + SEQS[0]]
        VALP = RING[0:E, 3648:3648 + CAPP]
        IDFP = RING[0:E, 3680:3680 + CAPP]
        TC = TMP[:, 768:768 + 7 * E]
        AFTM = TMP[:, 896:896 + 12 * E].rearrange("p (j n) -> p j n", j=4)
        AFT = RING[:, 3328:3328 + E]

        def pr(name):
            return part[:, PAR[name][0]:PAR[name][1]]

        z_at = 0

        def early(n):
            nonlocal z_at
            z_at += n
            return ZF[:, z_at - n:z_at]

        small_at = 0

        def tiny(n, parts=P):
            nonlocal small_at
            small_at += n
            return small[0:parts, small_at - n:small_at]

        def per(a, n):
            return a.rearrange("p (c d n) -> p c d n", c=NC, d=2)

        wg = early(KD * 32).rearrange("p (k n) -> p k n", k=KD)
        G = early(NC * 32).rearrange("p (c n) -> p c n", c=NC)
        GT = early(NC * P)[0:32]
        SPV = early(NC * 24).rearrange("p (c n) -> p c n", c=NC)
        SPE = early(NC * 24).rearrange("p (c n) -> p c n", c=NC)
        SPT = early(NC * 24).rearrange("p (c n) -> p c n", c=NC)
        SP2 = early(NC * 24).rearrange("p (c n) -> p c n", c=NC)
        SPP = early(NC * 24).rearrange("p (c n) -> p c n", c=NC)
        TOT = per(early(NC * 24), 12)
        TMC = per(early(NC * 16), 8)
        LND = early(NC * 16).rearrange("p (c n) -> p c n", c=NC)
        DRC = per(early(NC * 8), 4)
        BM = per(early(NC * 8), 4)
        WMX = per(early(NC * 8), 4)
        AL = per(tiny(NC * 24), 12)
        CS = per(tiny(NC * 24), 12)
        ECS = per(tiny(NC * 24), 12)
        WS = per(tiny(NC * 16), 8)
        DECG = per(tiny(NC * 8), 4)
        U = per(tiny(NC * 8), 4)
        MCOL = per(tiny(NC * 8), 4)
        SC = per(tiny(NC * 8), 4)
        EML = per(tiny(NC * 8), 4)
        WM = per(tiny(NC * 8), 4)
        SOLD = tiny(NC * 4).rearrange("p (d c n) -> p d c n", d=2, c=NC)
        NEGA = tiny(16)
        MPREV = tiny(2 * NC, 4).rearrange("p (d c) -> p d c", d=2)
        GROW = tiny(2 * NC, 4).rearrange("p (d c) -> p d c", d=2)
        ss, rs = tiny(NC), tiny(NC)
        ssb, rsb, halfn, den, rec, mx = (tiny(8) for _ in range(6))
        MR = tiny(P, 8 * NC)
        AMX, AESK, ANMX, ADEN = ([tiny(AH) for _ in range(2)] for _ in range(4))
        gts, gtp = tiny(E), tiny(E, CAPP)
        assert small_at <= 1980, small_at

        def sem(name):
            return ctx.enter_context(nc.semaphore(name))

        setup = sem("setup")
        x_copied = [sem(f"x_copied{j}") for j in range(T // 256)]
        layer_sems = []

        def layer_sem(name):
            layer_sems.append(sem(name))
            return layer_sems[-1]

        par_loaded = layer_sem("par_loaded")
        wg_loaded = layer_sem("wg_loaded")
        slice_used = layer_sem("slice_used")
        ring_loaded0 = layer_sem("ring_loaded0")
        ring_loaded1 = layer_sem("ring_loaded1")
        ht_made = layer_sem("ht_made")
        x_loaded = [layer_sem(f"x_loaded{j}") for j in range(4)]
        o_made = layer_sem("o_made")
        wo_loaded = layer_sem("wo_loaded")
        a_done = layer_sem("a_done")
        x_stored = [layer_sem(f"x_stored{j}") for j in range(2)]
        xo_loaded0 = layer_sem("xo_loaded0")
        xo_loaded1 = layer_sem("xo_loaded1")
        op_added = layer_sem("op_added")
        n2_scaled = layer_sem("n2_scaled")
        h2_stored = [layer_sem(f"h2_stored{j}") for j in range(2)]
        ew_loaded0 = layer_sem("ew_loaded0")
        ew_loaded1 = layer_sem("ew_loaded1")
        down_made = layer_sem("down_made")
        pool_chain = layer_sem("pool_chain")
        squared = layer_sem("squared")
        rooted = layer_sem("rooted")
        pads_ready = layer_sem("pads_ready")
        xbc_made = layer_sem("xbc_made")
        xs_kept = layer_sem("xs_kept")
        ws_made = layer_sem("ws_made")
        state_made = layer_sem("state_made")
        dxs_made = layer_sem("dxs_made")
        csb_read = layer_sem("csb_read")
        d_masked = layer_sem("d_masked")
        y_gated = layer_sem("y_gated")
        y_read = layer_sem("y_read")
        xsd_made = layer_sem("xsd_made")
        y_squared = layer_sem("y_squared")
        y_rooted = layer_sem("y_rooted")
        mcol_made = layer_sem("mcol_made")
        v_ones = layer_sem("v_ones")
        mb_read = layer_sem("mb_read")
        st_made = layer_sem("st_made")
        mrow_made = layer_sem("mrow_made")
        mrow_kept = layer_sem("mrow_kept")
        md_masked = layer_sem("md_masked")
        h_summed = layer_sem("h_summed")
        h_rooted = layer_sem("h_rooted")
        a_squared = layer_sem("a_squared")
        a_rooted = layer_sem("a_rooted")
        n2_squared = layer_sem("n2_squared")
        n2_rooted = layer_sem("n2_rooted")
        idx_ready = layer_sem("idx_ready")
        g_turned = layer_sem("g_turned")
        gathered = [layer_sem(f"gathered{j}") for j in range(3)]
        down_scaled = layer_sem("down_scaled")
        scattered = layer_sem("scattered")
        act_chain = layer_sem("act_chain")
        scaled = layer_sem("scaled")
        softplus_exp = layer_sem("softplus_exp")
        softplus_in = layer_sem("softplus_in")
        proj_made = layer_sem("proj_made")
        conv_done = layer_sem("conv_done")
        proj_read = layer_sem("proj_read")
        wm_ready = layer_sem("wm_ready")
        xs_turned = layer_sem("xs_turned")
        tanh_done = layer_sem("tanh_done")
        dt_made = layer_sem("dt_made")
        ln_done = layer_sem("ln_done")
        cs_read = layer_sem("cs_read")
        state_exps = layer_sem("state_exps")
        mcol_read = layer_sem("mcol_read")
        m_exps = layer_sem("m_exps")
        wm_diff = layer_sem("wm_diff")
        b_turned = layer_sem("b_turned")
        b_kept = layer_sem("b_kept")
        d_exp = layer_sem("d_exp")
        z_tanh = layer_sem("z_tanh")
        y_done = layer_sem("y_done")
        md_exp = layer_sem("md_exp")
        h_done = layer_sem("h_done")
        o_tanh = layer_sem("o_tanh")
        s_shift = layer_sem("s_shift")
        sink_exp = layer_sem("sink_exp")
        p_turned = layer_sem("p_turned")
        p_kept = layer_sem("p_kept")
        h2t_made = layer_sem("h2t_made")
        lg_shift = layer_sem("lg_shift")
        lg_exp = layer_sem("lg_exp")
        gu_made = layer_sem("gu_made")
        hid_made = layer_sem("hid_made")
        gate_tanh = layer_sem("gate_tanh")
        down_part = layer_sem("down_part")
        dve_chain = layer_sem("dve_chain")
        ht_copied = layer_sem("ht_copied")
        gates_made = layer_sem("gates_made")
        gate_rows = layer_sem("gate_rows")
        gate_rows_kept = layer_sem("gate_rows_kept")
        al_made = layer_sem("al_made")
        cs_made = layer_sem("cs_made")
        urow_made = layer_sem("urow_made")
        rows_read = layer_sem("rows_read")
        rows_made = layer_sem("rows_made")
        mcol_kept = layer_sem("mcol_kept")
        mlast_made = layer_sem("mlast_made")
        state_kept = layer_sem("state_kept")
        csb_made = layer_sem("csb_made")
        y_made = layer_sem("y_made")
        cb_made = layer_sem("cb_made")
        w_made = layer_sem("w_made")
        kt_turned = layer_sem("kt_turned")
        mstate_made = layer_sem("mstate_made")
        wk_made = layer_sem("wk_made")
        mstate_kept = layer_sem("mstate_kept")
        mb_made = layer_sem("mb_made")
        nd_made = layer_sem("nd_made")
        mw_made = layer_sem("mw_made")
        nd_read = layer_sem("nd_read")
        a_turned = layer_sem("a_turned")
        a_normed = layer_sem("a_normed")
        a_normed_late = layer_sem("a_normed_late")
        a_kept = layer_sem("a_kept")
        s_made = layer_sem("s_made")
        s_read = layer_sem("s_read")
        yt_made = layer_sem("yt_made")
        yt_copied = layer_sem("yt_copied")
        op_made = layer_sem("op_made")
        lg_made = layer_sem("lg_made")
        h2t_copied = layer_sem("h2t_copied")
        aff_turned = layer_sem("aff_turned")
        aff_made = layer_sem("aff_made")
        top_done = layer_sem("top_done")
        topt_made = layer_sem("topt_made")
        g_copied = layer_sem("g_copied")
        pe_fence = layer_sem("pe_fence")
        rng = range(min(x.num for x in layer_sems), max(x.num for x in layer_sems) + 1)
        assert len(rng) == len(layer_sems)

        cbank = ps[0:AH, 0, 0:NREL]
        with nc.Block() as block:
            @block.sync
            def _(sp):
                sp.dma_start(cstt[:, :], cst[:, :]).then_inc(setup, 16)
                sp.dma_start(SCR[0:33, 0:NREL + AH], onehot[:, :]).then_inc(setup, 16)
                sp.dma_start(HT[:, 0:P], flip[:, :]).then_inc(setup, 16)
                sp.dma_start(yp[:, :], xp[:, :]).then_inc(x_copied[0], 16)
                sp.wait_ge(setup, 50)
                sp.dma_start(btab[:, 0:NREL], SCR[0:AH, 1024:1024 + NREL]).then_inc(setup, 16)
                sp.dma_start(ys[0:256, :], xs_in[0:256, :]).then_inc(x_copied[1], 16)
                sp.wait_ge(setup, 66)
                sp.dma_start(HT[:, P:P + AH * 384].rearrange("p (h k) -> p h k", h=AH),
                             bass.AP(tensor=btab.tensor, offset=0, ap=[[1, P], [512, AH], [1, 384]])).then_inc(setup, 16)
                for j in range(1, SEQS[1] // 256):
                    rows = slice(256 * j, 256 * (j + 1))
                    sp.dma_start(ys[rows, :], xs_in[rows, :]).then_inc(x_copied[1 + j], 16)
                sp.wait_ge(setup, 82)

            @block.tensor
            def _(pe):
                pe.wait_ge(setup, 48)
                pe.matmul(cbank, SCR[0:33, NREL:NREL + AH], SCR[0:33, 0:NREL],
                          start=True, stop=True).then_inc(setup, 1)
                pe.wait_ge(setup, 82)
                for h in range(AH):
                    last = pe.matmul(ps[:, 1 + h, 0:384], HT[:, 0:P], HT[:, P + 384 * h:P + 384 * (h + 1)], start=True, stop=True)
                last.then_inc(setup, 1)

            @block.vector
            def _(dve):
                dve.wait_ge(setup, 49)
                dve.tensor_copy(SCR[0:AH, 1024:1024 + NREL], cbank).then_inc(setup, 1)
                dve.wait_ge(setup, 83)
                dve.tensor_copy(bia, ps[:, 1:5, 0:384]).then_inc(setup, 1)

        def counter(eng, own):
            n = {}

            def link(ins, to=own):
                n[to.num] = n.get(to.num, 0) + 1
                ins.then_inc(to, 1)
                eng.wait_ge(to, n[to.num])

            return link

        def last_of(d):
            return P - 1 if d == 0 else 0

        with nc.Fori(0, DEPTH) as layer:
          with nc.Block() as block:
            @block.sync
            def _(sp):
                def load_parameters():
                    sp.dma_start(part[:, :], par[bass.ds(layer * P, P), :]).then_inc(par_loaded, 16)
                    with nc.allow_non_contiguous_dma(reason="gate columns"):
                        for at, c0, w in ((0, 1792, 16), (16, 2832, 16)):
                            sp.dma_start(wg[:, :, at:at + w], wi[bass.ds(layer * D, D), c0:c0 + w]
                                         .rearrange("(k p) n -> p k n", p=P)).then_inc(wg_loaded, 16)

                def x_rows(c):
                    return yp[c * P:(c + 1) * P, :] if c < NP else ys[(c - NP) * P:(c - NP + 1) * P, :]

                def h2_rows(c):
                    return h2p[c * P:(c + 1) * P, :] if c < NP else h2s[(c - NP) * P:(c - NP + 1) * P, :]

                def ring_load(i):
                    if i >= 2:
                        sp.wait_ge(slice_used, i - 1)
                    c0 = SLICES[i][1]
                    sp.dma_start(ring[i % 2], wi[bass.ds(layer * D, D), c0:c0 + 256]
                                 .rearrange("(k p) n -> p k n", p=P)).then_inc([ring_loaded0, ring_loaded1][i % 2], 16)

                def expert_load(e):
                    done = [ew_loaded0, ew_loaded1][e % 2]
                    for dst, src, rows in ((EG, wga, D), (EU, wup, D), (ED, wdn, FF)):
                        sp.dma_start(dst[e % 2], src[bass.ds(layer * (E * rows) + e * rows, rows), :]
                                     .rearrange("(k p) n -> p k n", p=P)).then_inc(done, 16)

                for c in range(NC):
                    if c >= 4:
                        sp.wait_ge(ht_made, 2 * (c - 3))
                    if c % 2 == 0:
                        sp.wait_ge(x_copied[c // 2], 16)
                    sp.dma_start(XN[c % 4], x_rows(c)).then_inc(x_loaded[c % 4], 16)
                    if c == 1:
                        load_parameters()
                    if c in (3, 5):
                        ring_load(c // 2 - 1)
                for i in range(2, len(SLICES)):
                    ring_load(i)
                sp.wait_ge(nd_made, NC)
                sp.dma_start(WO, wo[bass.ds(layer * D, D), :].rearrange("(k p) n -> p k n", p=P)).then_inc(wo_loaded, 16)
                sp.wait_ge(slice_used, len(SLICES))
                for c in range(2):
                    sp.dma_start(XO[c], x_rows(ORDER[c])).then_inc([xo_loaded0, xo_loaded1][c], 16)
                for c in range(NC):
                    sp.wait_ge(op_added, 2 * c + 2)
                    sp.dma_start(x_rows(ORDER[c]), XO[c % 2]).then_inc(x_stored[c % 2], 16)
                    sp.wait_ge(n2_scaled, c + 1)
                    sp.dma_start(h2_rows(ORDER[c]), H2[c % 2]).then_inc(h2_stored[c % 2], 16)
                    if c + 2 < NC:
                        sp.wait_ge(x_stored[c % 2], 16 * (c // 2 + 1))
                        sp.dma_start(XO[c % 2], x_rows(ORDER[c + 2])).then_inc([xo_loaded0, xo_loaded1][c % 2], 16)
                    if c == NC - 2:
                        sp.wait_ge(yt_made, 2 * NC)
                        expert_load(0)
                sp.wait_ge(op_made, 2 * NC)

                for e in range(1, E):
                    if e >= 2:
                        sp.wait_ge(down_made, e - 1)
                    expert_load(e)

            @block.gpsimd
            def _(pool):
                link = counter(pool, pool_chain)

                def rroot(out, src, n, mul, eps, to):
                    link(pool.tensor_scalar(out[:, 0:n], src[:, 0:n], mul, eps, ALU.mult, ALU.add))
                    link(pool.tensor_tensor(out[:, 0:n], out[:, 0:n], halfn[:, 0:n], ALU.pow), to)

                link(pool.memset(halfn, -0.5))
                for c in range(NC):
                    pool.wait_ge(squared, c + 1)
                    rroot(rs[:, c:c + 1], ss[:, c:c + 1], 1, 1.0 / D, EPS, rooted)
                pool.wait_ge(ht_made, 2 * NC)
                for r in RAW:
                    for a, b in ((0, 2), (258, 260), (1284, 1286)):
                        link(pool.memset(r[:, a:b], 0.0), pads_ready)
                pool.wait_ge(xbc_made, 5)
                pool.wait_ge(xs_kept, 12)
                pool.wait_ge(ws_made, 1)
                for n, i in enumerate(STEPS):
                    if n >= 2:
                        pool.wait_ge(state_made, n - 1)
                    for d in range(2):
                        c = scan_chunk(d, i)
                        link(pool.tensor_tensor(DXS[:, n % 2, d, :].rearrange("p (h e) -> p h e", h=SH),
                                                XS[:, c, :].rearrange("p (h e) -> p h e", h=SH),
                                                WS[:, c, d, :].unsqueeze(2).to_broadcast([P, SH, HD]), ALU.mult), dxs_made)
                def ssd_mask(c, d):
                    pool.wait_ge(csb_read, 2 * c + d + 1)
                    v = DM[:, c % 2, d, :].rearrange("p (h t) -> p h t", h=SH)
                    sgn = 1 if d == 0 else -1
                    link(pool.affine_select(out=v, in_=v, compare_op=ALU.is_ge, fill=NEG, base=0,
                                            pattern=[[0, SH], [sgn, P]], channel_multiplier=-sgn), d_masked)

                ssd_mask(0, 0)
                ssd_mask(0, 1)
                for c in range(NC + 1):
                    if c < NC:
                        if c >= 1:
                            pool.wait_ge(y_gated, c)
                        link(pool.tensor_tensor(TMP[:, 0:512].rearrange("p (h e) -> p h e", h=SH),
                                                XS[:, c, :].rearrange("p (h e) -> p h e", h=SH),
                                                pr("dskip").unsqueeze(2).to_broadcast([P, SH, HD]), ALU.mult), xsd_made)
                    if c >= 1:
                        pool.wait_ge(y_squared, c)
                        rroot(rsb, ssb, 1, 1.0 / 512, 4 * EPS, y_rooted)
                    if c + 1 < NC:
                        ssd_mask(c + 1, 0)
                        ssd_mask(c + 1, 1)
                pool.wait_ge(mcol_made, 1)
                link(pool.memset(V[:, :, :, HD:HD + 1], 1.0), v_ones)

                def ml_mask(c, d):
                    pool.wait_ge(mb_read, 2 * c + d + 1)
                    v = DMM[:, c % 2, d]
                    sgn = 1 if d == 0 else -1
                    link(pool.affine_select(out=v, in_=v, compare_op=ALU.is_ge, fill=NEG, base=0,
                                            pattern=[[0, MH], [sgn, P]], channel_multiplier=-sgn), md_masked)

                def attn_root(c):
                    pool.wait_ge(a_squared, c + 1)
                    rroot(QKS[:, c, :], QKS[:, c, :], 6, 1.0 / HD, EPS, a_rooted)

                ml_mask(0, 0)
                ml_mask(0, 1)
                for c in range(NC + 1):
                    if c + 1 < NC:
                        ml_mask(c + 1, 0)
                        ml_mask(c + 1, 1)
                    if c >= 1:
                        pool.wait_ge(h_summed, c)
                        rroot(rsb, ssb, MH, 4.0 / HD, 4 * EPS, h_rooted)
                    if c >= 1:
                        attn_root(c - 1)
                for c in range(QK_FIRST, NC):
                    pool.wait_ge(a_turned, c - 1)
                    n = QKN[c % 2]
                    link(pool.tensor_tensor(n[:, 0:256].rearrange("p (j g e) -> p g j e", j=2, g=2),
                                            Z[:, c, 0:256].rearrange("p (g j e) -> p g j e", j=2, g=2),
                                            QKS[:, c, 0:4].rearrange("p (g j) -> p g j", g=2).unsqueeze(3).to_broadcast([P, 2, 2, HD]),
                                            ALU.mult))
                    link(pool.tensor_tensor(n[:, 256:384].rearrange("p (h e) -> p h e", h=2),
                                            Z[:, c, 256:384].rearrange("p (h e) -> p h e", h=2),
                                            QKS[:, c, 4:6].unsqueeze(2).to_broadcast([P, 2, HD]), ALU.mult), a_normed_late)
                for c in range(NC):
                    pool.wait_ge(n2_squared, c + 1)
                    rroot(rsb, ssb, 1, 1.0 / D, EPS, n2_rooted)
                pool.wait_ge(idx_ready, 1)
                for j in range(2):
                    pool.wait_ge(h2_stored[j], 8 * NC)
                    pool.wait_ge(x_stored[j], 8 * NC)

                def gather(e):
                    if e >= 3:
                        pool.wait_ge(g_turned, 3 * (e - 2))
                    for dst, src, at in ((XG, h2s, idxs), (XGP, h2p, idxp)):
                        pool.indirect_dma_start(dst[e % 3], None, src[:, :], bass.IndirectOffsetOnAxis(ap=at[:, e:e + 1], axis=0)
                                                ).then_inc(gathered[e % 3], 16)

                gather(0)
                gather(1)
                for e in range(E):
                    if e + 2 < E:
                        gather(e + 2)
                    pool.wait_ge(down_scaled, 4 * (e + 1))
                    if e >= 1:
                        pool.wait_ge(scattered, 32 * e)
                    pool.indirect_dma_start(ys[:, :], bass.IndirectOffsetOnAxis(ap=idxs[:, e:e + 1], axis=0), YO[e % 2], None,
                                            compute_op=ALU.add, bounds_check=SEQS[1] - 1).then_inc(scattered, 16)
                    pool.indirect_dma_start(yp[:, :], bass.IndirectOffsetOnAxis(ap=idxp[:, e:e + 1], axis=0), YOP[e % 2], None,
                                            compute_op=ALU.add, bounds_check=SEQS[0] - 1).then_inc(scattered, 16)
                pool.wait_ge(scattered, 32 * E)

            @block.scalar
            def _(act):
                link = counter(act, act_chain)
                def square(c):
                    act.wait_ge(x_loaded[c % 4], 16 * (c // 4 + 1))
                    link(act.activation(XSF[:, 0:D], XN[c % 4], ACT.Square, accum_out=ss[:, c:c + 1]), squared)

                square(0)
                for c in range(NC):
                    if c + 1 < NC:
                        square(c + 1)
                    act.wait_ge(rooted, c + 1)
                    link(act.mul(XN[c % 4], XN[c % 4], rs[:, c:c + 1]), scaled)
                act.wait_ge(par_loaded, 16)
                link(act.activation(NEGA, pr("alog"), ACT.Exp), softplus_exp)
                act.wait_ge(softplus_in, 1)
                link(act.activation(SPE, SPE, ACT.Exp, scale=-1.0), softplus_exp)

                def evac(u):
                    sl, kind, f, g = UNITS[u]
                    act.wait_ge(proj_made, u + 1)
                    src = ps[:, u % 2, :]
                    if kind == "xbc":
                        t0, n = GROUPS[g]
                        if g == 0 and f >= 2:
                            act.wait_ge(conv_done, f - 1)
                        if g == 0 and f < 2:
                            act.wait_ge(pads_ready, 6)
                        if g == 0:
                            link(act.copy(RAW[f % 2][:, 2:258], src[:, 0:256]))
                            link(act.copy(RAW[f % 2][:, 260:516], src[:, 256:512]), proj_read)
                        else:
                            link(act.copy(RAW[f % 2][:, t0 + 4:t0 + 4 + n], src[:, 0:n]), proj_read)
                    elif kind == "z":
                        if u == U_Z:
                            act.wait_ge(wm_ready, 1)
                        link(act.copy(Z[:, g, f * 256:(f + 1) * 256], src[:, 0:256]), proj_read)
                    elif kind == "qk":
                        t0, n = GROUPS[g]
                        link(act.mul(QK[:, f, t0:t0 + n], src[:, 0:n], 1.0 if f < 2 else HD ** -0.5), proj_read)
                    elif kind == "v":
                        link(act.copy(V[:, g, :, 0:HD], src[:, 0:256].rearrange("p (h e) -> p h e", h=MH)), proj_read)
                    elif kind == "o":
                        link(act.copy(O[:, g, :], src[:, 0:256]), proj_read)
                    else:
                        link(act.copy(Z[:, g, f * 256:(f + 1) * 256], src[:, 0:256]), proj_read)

                def conv_tanh(f):
                    act.wait_ge(conv_done, f + 1)
                    if f >= 2:
                        act.wait_ge(xs_turned, 3 * min(f - 1, 4))
                        act.wait_ge(xbc_made, f - 1)
                    link(act.activation(XF[f % 2][:, 0:1282], ACC[f % 2][:, 0:1282], ACT.Tanh, scale=0.5), tanh_done)

                def keep_xs(f):
                    for j, (c0, n) in enumerate(((0, 4), (4, 4), (8, 2))):
                        act.wait_ge(xs_turned, 3 * f + j + 1)
                        link(act.mul(XS[:, c0:c0 + n, f * P:(f + 1) * P],
                                     ps[:, 2 + j % 2, 0:n * P].rearrange("p (c n) -> p c n", c=n), 0.5), xs_kept)

                for u in range(0, 3):
                    evac(u)
                act.wait_ge(dt_made, 1)
                link(act.activation(LND, LND, ACT.Ln), ln_done)
                for u in range(3, 6):
                    evac(u)
                conv_tanh(0)
                act.wait_ge(cs_read, 1)
                link(act.activation(ECS, CS, ACT.Exp))
                link(act.activation(TMC, TMC, ACT.Exp))
                for g in range(2):
                    link(act.activation(DECG[64 * g:64 * g + 64], TOT[64 * g:64 * g + 64, :, :, 4 * g:4 * g + 4], ACT.Exp),
                         state_exps)
                for u in range(6, 9):
                    evac(u)
                conv_tanh(1)
                evac(9)
                keep_xs(0)
                for u in range(10, 12):
                    evac(u)
                conv_tanh(2)
                act.wait_ge(mcol_read, 1)
                link(act.activation(SC, DRC, ACT.Exp, scale=-1.0))
                link(act.activation(EML, BM, ACT.Exp, scale=-1.0), m_exps)
                keep_xs(1)
                for u in range(12, 15):
                    evac(u)
                conv_tanh(3)
                act.wait_ge(wm_diff, 1)
                link(act.activation(WM, WMX, ACT.Exp), wm_ready)
                keep_xs(2)
                for u in range(15, 18):
                    evac(u)
                conv_tanh(4)
                keep_xs(3)
                conv_tanh(5)
                for u in range(U_Z, U_Z + Z_AHEAD):
                    evac(u)
                act.wait_ge(xbc_made, 5)
                for j, (c0, n) in enumerate(((0, 4), (4, 4), (8, 2))):
                    act.wait_ge(b_turned, j + 1)
                    link(act.copy(BT[:, c0:c0 + n, :], ps[:, 2 + j % 2, 0:n * P].rearrange("p (c n) -> p c n", c=n)), b_kept)
                for n in range(len(STEPS)):
                    for u in z_units(n):
                        evac(u)
                def ssd_exp(c, d):
                    act.wait_ge(d_masked, 2 * c + d + 1)
                    link(act.activation(DM[:, c % 2, d, :], DM[:, c % 2, d, :], ACT.Exp), d_exp)

                evac(U_QK - 2)
                ssd_exp(0, 0)
                evac(U_QK - 1)
                ssd_exp(0, 1)
                for c in range(NC + 1):
                    if c >= 1:
                        act.wait_ge(y_gated, c)
                        link(act.activation(ZF[:, (c - 1) * 512:c * 512], XS[:, c - 1, :], ACT.Square,
                                            accum_out=ssb[:, 0:1]), y_squared)
                    if c < NC:
                        link(act.activation(TMP[:, 1024:1536], Z[:, c, :], ACT.Tanh, scale=0.5), z_tanh)
                    if c >= 1:
                        act.wait_ge(y_rooted, c)
                        link(act.mul(XS[:, c - 1, :], XS[:, c - 1, :], rsb[:, 0:1]), y_done)
                    if c < NC:
                        if c + 1 < NC:
                            ssd_exp(c + 1, 0)
                        evac(U_QK + 3 * c)
                        evac(U_QK + 3 * c + 1)
                        if c + 1 < NC:
                            ssd_exp(c + 1, 1)
                        evac(U_QK + 3 * c + 2)
                evac(U_ATT - 2)
                evac(U_ATT - 1)
                for i in range(NC):
                    evac(U_ATT + i)
                act.wait_ge(mrow_made, 1)
                link(act.copy(MR, ps[0:8 * NC, 3, 0:P]), mrow_kept)
                def ml_exp(c, d):
                    act.wait_ge(md_masked, 2 * c + d + 1)
                    link(act.activation(DMM[:, c % 2, d], DMM[:, c % 2, d], ACT.Exp), md_exp)

                ml_exp(0, 0)
                ml_exp(0, 1)
                for c in range(NC):
                    if c + 1 < NC:
                        ml_exp(c + 1, 0)
                    if c >= 2:
                        act.wait_ge(h_done, c - 1)
                    link(act.activation(OTH[c % 2], O[:, c, :], ACT.Tanh, scale=0.5), o_tanh)
                    evac(U_ATT + NC + c)
                    if c + 1 < NC:
                        ml_exp(c + 1, 1)
                def attn_exps(c):
                    nk, c0 = attn_keys(c)
                    act.wait_ge(s_shift, c + 1)
                    if c >= 2:
                        act.wait_ge(a_done, c - 1)
                    for h in range(AH):
                        v = PSC[c % 2][:, h, 0:nk * P]
                        link(act.activation(v, v, ACT.Exp, bias=ANMX[c % 2][:, h:h + 1], accum_out=ADEN[c % 2][:, h:h + 1]))
                    link(act.activation(AESK[c % 2], AESK[c % 2], ACT.Exp), sink_exp)

                attn_exps(0)
                act.wait_ge(h_summed, NC)
                for c in range(NC):
                    nk, c0 = attn_keys(c)
                    for h in range(AH):
                        act.wait_ge(p_turned, AH * c + h + 1)
                        if h == 0 and c >= 1:
                            act.wait_ge(o_made, c)
                        link(act.copy(TMP[:, h * 384:h * 384 + nk * P], ps[:, 6 + h % 2, 0:nk * P]), p_kept)
                    if c + 1 < NC:
                        attn_exps(c + 1)
                def route_exp(c):
                    act.wait_ge(lg_shift, c + 1)
                    link(act.activation(AFT, AFT, ACT.Exp, accum_out=den[:, 0:1]), lg_exp)

                for c in range(NC):
                    act.wait_ge(op_added, 2 * c + 2)
                    link(act.activation(JUNK, XO[c % 2], ACT.Square, accum_out=ssb[:, 0:1]), n2_squared)
                    act.wait_ge(n2_rooted, c + 1)
                    if c >= 2:
                        act.wait_ge(h2_stored[c % 2], 16 * (c // 2))
                        act.wait_ge(h2t_made, 2 * (c - 1))
                    link(act.mul(H2[c % 2], XO[c % 2], rsb[:, 0:1]), n2_scaled)
                    if c >= 1:
                        route_exp(c - 1)
                route_exp(NC - 1)
                for e in range(E):
                    for f in range(KF):
                        act.wait_ge(gu_made, KF * e + f + 1)
                        if e + f >= 1:
                            act.wait_ge(hid_made, KF * e + f)
                        link(act.activation(THG, ps[:, 2 + f % 2, 0:TOK], ACT.Tanh, scale=0.5), gate_tanh)
                    if e >= 2:
                        act.wait_ge(scattered, 32 * (e - 1))
                    for j in range(4):
                        act.wait_ge(down_part, 4 * e + j + 1)
                        hf = j % 2
                        if j < 2:
                            link(act.mul(YO[e % 2][:, hf * 512:(hf + 1) * 512], ps[:, 4 + j, :], gts[:, e:e + 1]), down_scaled)
                        else:
                            link(act.mul(YOP[e % 2][:, hf * 512:(hf + 1) * 512], ps[0:CAPP, 4 + j, :], gtp[:, e:e + 1]), down_scaled)

            @block.vector
            def _(dve):
                link = counter(dve, dve_chain)

                def tt(out, a, b, op, to=dve_chain):
                    link(dve.tensor_tensor(out, a, b, op), to)

                def ts(out, a, x, y, op0, op1=None, to=dve_chain):
                    if op1 is None:
                        link(dve.tensor_scalar(out, a, x, None, op0), to)
                    else:
                        link(dve.tensor_scalar(out, a, x, y, op0, op1), to)

                def stt(out, a, x, b, op0, op1, to=dve_chain):
                    link(dve.scalar_tensor_tensor(out=out, in0=a, scalar=x, in1=b, op0=op0, op1=op1), to)

                def wide(a, n):
                    return a.unsqueeze(2).to_broadcast([a.shape[0], a.shape[1], n])

                def quarter(b):
                    return ps[:, b, :].rearrange("p (k t) -> p k t", k=4)

                dve.wait_ge(par_loaded, 16)
                def keep_gates(c):
                    dve.wait_ge(gate_rows, c + 1)
                    link(dve.tensor_copy(GT[:, c * P:(c + 1) * P], ps[0:32, [3, 1][c % 2], 0:P]), gate_rows_kept)

                for c in range(NC):
                    for j in range(2):
                        dve.wait_ge(ht_made, 2 * c + j + 1)
                        tt(hT[:, 4 * j:4 * j + 4, c * P:(c + 1) * P], quarter(4 + 2 * (c % 2) + j), wide(pr("gmix")[:, 4 * j:4 * j + 4], P),
                           ALU.mult, ht_copied)
                    if c >= 2:
                        keep_gates(c - 2)
                keep_gates(NC - 2)
                keep_gates(NC - 1)
                dve.wait_ge(gates_made, 1)
                tt(G, ps[:, 2, 0:NC * 32].rearrange("p (c n) -> p c n", c=NC),
                   pr("gbias").unsqueeze(1).to_broadcast([P, NC, 32]), ALU.add)
                link(dve.tensor_copy(SPV[:, :, 0:16], G[:, :, 0:16]))
                ts(SPV[:, :, 16:24], G[:, :, 24:32], -1.0, None, ALU.mult)
                ts(SPT, SPV, -1.0, None, ALU.mult)
                tt(SPE, SPV, SPT, ALU.max, softplus_in)
                dve.wait_ge(softplus_exp, 2)
                ts(SPT, SPE, 2.0, None, ALU.add)
                link(dve.reciprocal(SPT, SPT))
                tt(SPT, SPE, SPT, ALU.mult)
                tt(SP2, SPT, SPT, ALU.mult)
                ts(SPP, SP2, 1.0 / 17, None, ALU.mult)
                for k in (15, 13, 11, 9, 7, 5, 3):
                    stt(SPP, SPP, 1.0 / k, SP2, ALU.add, ALU.mult)
                stt(SPP, SPP, 1.0, SPT, ALU.add, ALU.mult)
                ts(SPP, SPP, 2.0, None, ALU.mult)
                stt(SPV, SPV, 0.0, SPP, ALU.max, ALU.add)
                ts(LND, SPV[:, :, 0:16], 1e-19, None, ALU.max, to=dt_made)
                ts(NEGA, NEGA, -1.0, None, ALU.mult)
                for d in range(2):
                    tt(AL[:, :, d, 0:8], SPV[:, :, 8 * d:8 * d + 8], NEGA[:, 8 * d:8 * d + 8].unsqueeze(1).to_broadcast([P, NC, 8]),
                       ALU.mult)
                    ts(AL[:, :, d, 8:12], SPV[:, :, 16 + 4 * d:20 + 4 * d], -1.0, None, ALU.mult, to=al_made)

                def conv(f):
                    dve.wait_ge(proj_read, 3 * f + 3)
                    if f >= 2:
                        dve.wait_ge(tanh_done, f - 1)
                    w = pr("convw")[:, 5 * f:5 * f + 5]
                    raw, acc = RAW[f % 2], ACC[f % 2][:, 0:1282]
                    ts(acc, raw[:, 0:1282], w[:, 0:1], pr("convb")[:, f:f + 1], ALU.mult, ALU.add)
                    for j in range(1, 5):
                        stt(acc, raw[:, j:j + 1282], w[:, j:j + 1], acc, ALU.mult, ALU.add,
                            conv_done if j == 4 else dve_chain)

                def silu(f):
                    dve.wait_ge(tanh_done, f + 1)
                    th = XF[f % 2][:, 0:1282]
                    acc = ACC[f % 2][:, 0:1282]
                    if f < 4:
                        stt(th, th, 1.0, acc, ALU.add, ALU.mult, xbc_made)
                    else:
                        ts(th, th, 0.5, 0.5, ALU.mult, ALU.add)
                        tt(BC[:, f - 4, 0:1282], th, acc, ALU.mult, xbc_made)

                conv(0)
                dve.wait_ge(cs_made, 1)
                link(dve.tensor_copy(CS, ps[:, 5, 0:240].rearrange("p (c d n) -> p c d n", c=NC, d=2)))
                link(dve.tensor_copy(TOT, ps[:, 6, 0:240].rearrange("p (c d n) -> p c d n", c=NC, d=2)))
                tt(TMC, TOT[:, :, :, 0:8], CS[:, :, :, 0:8], ALU.subtract)
                for d in range(2):
                    tt(U[:, :, d, :], G[:, :, 16 + 4 * d:20 + 4 * d], CS[:, :, d, 8:12], ALU.subtract,
                       cs_read if d == 1 else dve_chain)
                conv(1)
                silu(0)
                dve.wait_ge(state_exps, 2)
                for d in range(2):
                    tt(WS[:, :, d, :], TMC[:, :, d, :], SPV[:, :, 8 * d:8 * d + 8], ALU.mult, ws_made if d == 1 else dve_chain)
                dve.wait_ge(ln_done, 1)
                for d in range(2):
                    tt(CS[:, :, d, 0:8], CS[:, :, d, 0:8], LND[:, :, 8 * d:8 * d + 8], ALU.subtract)
                dve.wait_ge(urow_made, 1)
                for d in range(2):
                    for j, (t0, n) in enumerate(GROUPS):
                        link(dve.tensor_copy(UROW[:, d, t0:t0 + n], ps[0:4, 2 + 3 * d + j, 0:n]))
                link(dve.tensor_copy(GROW, ps[0:4, 4, 256:276].rearrange("p (d c) -> p d c", d=2)), rows_read)
                for d in range(2):
                    for i in range(NC):
                        c = scan_chunk(d, i)
                        u, m = UROW[:, d, c * P:(c + 1) * P], MROW[:, d, c * P:(c + 1) * P]
                        if i in (0, NP):
                            link(dve.memset(MPREV[:, d, c:c + 1], NEG))
                        if d == 1:
                            u, m = u[:, ::-1], m[:, ::-1]
                        link(dve.tensor_tensor_scan(m, u, u, MPREV[:, d, c:c + 1], ALU.max, ALU.max))
                        if has_next(i):
                            cn = scan_chunk(d, i + 1)
                            tt(MPREV[:, d, cn:cn + 1], GROW[:, d, c:c + 1], m[:, P - 1:P], ALU.add)
                for d in range(2):
                    tt(UROW[:, d, :].rearrange("p (c t) -> p c t", c=NC), MROW[:, d, :].rearrange("p (c t) -> p c t", c=NC),
                       MPREV[:, d, :].unsqueeze(2).to_broadcast([4, NC, P]), ALU.subtract, rows_made)
                conv(2)
                silu(1)
                dve.wait_ge(mcol_made, 1)
                link(dve.tensor_copy(MCOL, ps[:, 5, 0:80].rearrange("p (c d n) -> p c d n", c=NC, d=2)), mcol_kept)
                link(dve.tensor_copy(DRC, ps[:, 5, 80:160].rearrange("p (c d n) -> p c d n", c=NC, d=2)))
                tt(BM, MCOL, CS[:, :, :, 8:12], ALU.add, mcol_read)
                conv(3)
                silu(2)
                dve.wait_ge(mlast_made, 1)
                tt(WMX, U, ps[:, 6, 0:80].rearrange("p (c d n) -> p c d n", c=NC, d=2), ALU.subtract, wm_diff)
                link(dve.tensor_copy(SOLD, ps[:, 6, 256:296].rearrange("p (d c n) -> p d c n", d=2, c=NC)))
                conv(4)
                silu(3)
                conv(5)
                silu(4)
                silu(5)
                link(dve.memset(PREV[:, 0, 0, :], 0.0))
                link(dve.memset(PREV[:, 0, NP, :], 0.0))
                link(dve.memset(PREV[:, 1, NP - 1, :], 0.0))
                link(dve.memset(PREV[:, 1, NC - 1, :], 0.0))
                for n, i in enumerate(STEPS):
                    dve.wait_ge(state_made, n + 1)
                    for d in range(2):
                        c, cn = scan_chunk(d, i), scan_chunk(d, i + 1)
                        tt(TMP[:, 0:256].rearrange("p (h e) -> p h e", h=4), PREV[:, d, c, :].rearrange("p (h e) -> p h e", h=4),
                           wide(DECG[:, c, d, :], HD), ALU.mult)
                        tt(PREV[:, d, cn, :], ps[:, 4, 256 * d:256 * d + 256], TMP[:, 0:256], ALU.add,
                           state_kept if d == 1 else dve_chain)

                def heads(a, h=SH):
                    return a.rearrange("p (h e) -> p h e", h=h)

                def ssd_exponents(c, d):
                    dve.wait_ge(csb_made, 2 * c + d + 1)
                    if c >= 2:
                        dve.wait_ge(y_made, c - 1)
                    tt(DM[:, c % 2, d, :].rearrange("p (h t) -> p h t", h=SH),
                       ps[:, 2:4, :].rearrange("p b (h t) -> p (b h) t", h=4),
                       wide(CS[:, c, d, 0:8], P), ALU.subtract, csb_read)

                def ssd_weights(c):
                    dve.wait_ge(cb_made, c + 1)
                    for d in range(2):
                        dve.wait_ge(d_exp, 2 * c + d + 1)
                        cb = ps[:, 4, 0:256].rearrange("p (g t) -> p g t", g=2)
                        for g in range(2):
                            v = DM[:, c % 2, d, g * 512:(g + 1) * 512].rearrange("p (h t) -> p h t", h=4)
                            tt(v, v, cb[:, g, :].unsqueeze(1).to_broadcast([P, 4, P]), ALU.mult, w_made)

                def ssd_output(c):
                    dve.wait_ge(y_made, c + 1)
                    dve.wait_ge(xsd_made, c + 1)
                    dve.wait_ge(z_tanh, c + 1)
                    y, t, zt = TMP[:, 0:512], TMP[:, 512:1024], TMP[:, 1024:1536]
                    tt(y, ps[:, 5, :], y, ALU.add)
                    for d in range(2):
                        tt(t.rearrange("p (g h e) -> p g h e", g=2, h=4),
                           ps[:, 6:8, 256 * d:256 * d + 256].rearrange("p g (h e) -> p g h e", h=4),
                           ECS[:, c, d, 0:8].rearrange("p (g h) -> p g h", g=2).unsqueeze(3).to_broadcast([P, 2, 4, HD]), ALU.mult, y_read if d == 1 else dve_chain)
                        tt(y, y, t, ALU.add)
                    stt(zt, zt, 1.0, Z[:, c, :], ALU.add, ALU.mult)
                    tt(XS[:, c, :], y, zt, ALU.mult, y_gated)

                ssd_exponents(0, 0)
                ssd_exponents(0, 1)
                ssd_weights(0)
                for c in range(NC + 1):
                    if c >= 1:
                        ssd_output(c - 1)
                    if c + 1 < NC:
                        ssd_exponents(c + 1, 0)
                        ssd_exponents(c + 1, 1)
                        ssd_weights(c + 1)
                dve.wait_ge(y_done, NC)
                for d, c in ((0, 0), (0, NP), (1, NP - 1), (1, NC - 1)):
                    link(dve.memset(PREVM[:, d, c], 0.0))

                def weigh_keys(n):
                    dve.wait_ge(kt_turned, n + 1)
                    if n >= 2:
                        dve.wait_ge(mstate_made, n - 1)
                    for d in range(2):
                        c = scan_chunk(d, STEPS[n])
                        tt(heads(WK[n % 2][:, 256 * d:256 * d + 256], 4), heads(ps[:, 4 + 2 * (n % 2), 256 * d:256 * d + 256], 4),
                           wide(WM[:, c, d, :], HD), ALU.mult, wk_made)

                weigh_keys(0)
                for n, i in enumerate(STEPS):
                    if n + 1 < len(STEPS):
                        weigh_keys(n + 1)
                    dve.wait_ge(mstate_made, n + 1)
                    for d in range(2):
                        c, cn = scan_chunk(d, i), scan_chunk(d, i + 1)
                        tmp = TMP[:, 1024:1154].rearrange("p (h e) -> p h e", h=2)
                        tt(tmp, PREVM[:, d, c], wide(SOLD[:, d, c, :], 65), ALU.mult)
                        tt(PREVM[:, d, cn], ps[:, 5 + 2 * (n % 2), 256 * d:256 * d + 130].rearrange("p (h e) -> p h e", h=2),
                           tmp, ALU.add, mstate_kept)

                def ml_exponents(c, d):
                    dve.wait_ge(mb_made, 2 * c + d + 1)
                    if c >= 2:
                        dve.wait_ge(nd_made, c - 1)
                    tt(DMM[:, c % 2, d], wide(U[:, c, d, :], P), quarter(3), ALU.subtract, mb_read)

                def ml_weights(c):
                    dve.wait_ge(st_made, c + 1)
                    for d in range(2):
                        dve.wait_ge(md_exp, 2 * c + d + 1)
                        tt(DMM[:, c % 2, d], DMM[:, c % 2, d], quarter(2), ALU.mult, mw_made)

                nd = [heads(TMP[:, 260 * d:260 * d + 260], 4) for d in range(2)]
                hs, hd = heads(SCR[:, 3392:3648], 4), heads(SCR[:, 3648:3904], 4)
                t4 = heads(TMP[:, 520:780], 4)

                def ml_read(c):
                    dve.wait_ge(nd_made, c + 1)
                    for d in range(2):
                        tt(t4.rearrange("p (j q) e -> p q j e", q=2),
                           ps[:, 4:8:3, 130 * d:130 * d + 130].rearrange("p q (j e) -> p q j e", j=2),
                           SC[:, c, d, :].rearrange("p (j q) -> p q j", q=2).unsqueeze(3).to_broadcast([P, 2, 2, 65]), ALU.mult)
                        tt(nd[d], heads(ps[:, 5 + d, 0:260], 4), t4, ALU.add, nd_read)

                def ml_output(c):
                    for d in range(2):
                        dn = den[:, 4 * d:4 * d + 4]
                        raw = nd[d][:, :, HD:HD + 1].rearrange("p h e -> p (h e)")
                        stt(dn, raw, -1.0, raw, ALU.mult, ALU.max)
                        tt(dn, dn, EML[:, c, d, :], ALU.max)
                    link(dve.reciprocal(rec, den))
                    for d in range(2):
                        tt(hd if d else hs, nd[d][:, :, 0:HD], wide(rec[:, 4 * d:4 * d + 4], HD), ALU.mult)
                    tt(hs, hs, hd, ALU.add)
                    tt(hd, hs, hs, ALU.mult)
                    link(dve.tensor_reduce(out=ssb[:, 0:4], in_=hd, axis=AX, op=ALU.add), h_summed)

                def ml_gate(c):
                    dve.wait_ge(h_rooted, c + 1)
                    tt(hs, hs, wide(rsb[:, 0:4], HD), ALU.mult)
                    dve.wait_ge(o_tanh, c + 1)
                    stt(O[:, c, :], OTH[c % 2], 1.0, SCR[:, 3392:3648], ALU.add, ALU.mult, h_done)

                def attn_square(c):
                    dve.wait_ge(proj_read, U_ATT + NC + c + 1)
                    tt(SCR[:, 2560:2944], Z[:, c, 0:384], Z[:, c, 0:384], ALU.mult)
                    link(dve.tensor_reduce(out=QKS[:, c, :], in_=heads(SCR[:, 2560:2944], 6), axis=AX, op=ALU.add), a_squared)

                def attn_norm(c):
                    dve.wait_ge(a_rooted, c + 1)
                    if c >= 2:
                        dve.wait_ge(a_turned, c - 1)
                    n = QKN[c % 2]
                    tt(n[:, 0:256].rearrange("p (j g e) -> p g j e", j=2, g=2),
                       Z[:, c, 0:256].rearrange("p (g j e) -> p g j e", j=2, g=2),
                       QKS[:, c, 0:4].rearrange("p (g j) -> p g j", g=2).unsqueeze(3).to_broadcast([P, 2, 2, HD]), ALU.mult)
                    tt(heads(n[:, 256:384], 2), heads(Z[:, c, 256:384], 2), wide(QKS[:, c, 4:6], HD), ALU.mult, a_normed)

                def keep_turned(c):
                    dve.wait_ge(a_turned, c + 1)
                    b = (c + 1) % 2
                    ts(QT[:, :, c * P:(c + 1) * P], ps[:, b, 0:256].rearrange("p (j t) -> p j t", j=2), pr("qg"), HD ** -0.5,
                       ALU.mult, ALU.mult)
                    ts(KT[:, c * P:(c + 1) * P], ps[:, b, 256:384], pr("kg"), None, ALU.mult, to=a_kept)

                def attn_shift(c):
                    nk, c0 = attn_keys(c)
                    b0 = (c0 - c + 1) * P
                    m, e, n = AMX[c % 2], AESK[c % 2], ANMX[c % 2]
                    dve.wait_ge(s_made, c + 1)
                    v = PSC[c % 2][:, :, 0:nk * P]
                    if c >= 2:
                        dve.wait_ge(p_turned, AH * (c - 1))
                    tt(v, ps[:, 2:6, 0:nk * P], bia[:, :, b0:b0 + nk * P], ALU.add, s_read)
                    link(dve.tensor_reduce(out=m, in_=v, axis=AX, op=ALU.max))
                    tt(m, m, pr("sink"), ALU.max)
                    tt(e, pr("sink"), m, ALU.subtract)
                    ts(n, m, -1.0, None, ALU.mult, to=s_shift)

                ml_exponents(0, 0)
                ml_exponents(0, 1)
                ml_weights(0)
                for c in range(NC):
                    if c >= 1:
                        ml_read(c - 1)
                    if c + 1 < NC:
                        ml_exponents(c + 1, 0)
                    if c >= 2:
                        ml_gate(c - 2)
                    if c >= 1:
                        ml_output(c - 1)
                    if c + 1 < NC:
                        ml_exponents(c + 1, 1)
                    if c >= 1:
                        attn_square(c - 1)
                    if c in (4, 5):
                        attn_norm(c - 4)
                    if c + 1 < NC:
                        ml_weights(c + 1)
                ml_read(NC - 1)
                keep_turned(0)
                attn_norm(2)
                keep_turned(1)
                attn_norm(3)
                keep_turned(2)
                attn_shift(0)
                ml_gate(NC - 2)
                ml_output(NC - 1)
                attn_norm(4)
                keep_turned(3)
                attn_square(NC - 1)
                def attn_output(c):
                    dve.wait_ge(sink_exp, c + 1)
                    r = ADEN[c % 2]
                    tt(r, r, AESK[c % 2], ALU.add)
                    link(dve.reciprocal(r, r))
                    dve.wait_ge(o_made, c + 1)
                    tt(heads(Z[:, c, 0:256], 4), heads(ps[:, c % 2, 0:256], 4), wide(r, HD), ALU.mult, a_done)

                attn_shift(1)
                for c in range(NC):
                    attn_output(c)
                    if c == 0:
                        ml_gate(NC - 1)
                    if c + 4 < NC:
                        keep_turned(c + 4)
                    if c + 2 < NC:
                        attn_shift(c + 2)

                def keep_y(c):
                    for j in range(2):
                        dve.wait_ge(yt_made, 2 * c + j + 1)
                        tt(hT[:, 4 * j:4 * j + 4, ORDER[c] * P:(ORDER[c] + 1) * P], quarter(2 + j), wide(pr("gy")[:, 4 * j:4 * j + 4], P),
                           ALU.mult, yt_copied)

                def add_x(c, hf):
                    dve.wait_ge(op_made, 2 * c + hf + 1)
                    tt(XO[c % 2][:, hf * 512:(hf + 1) * 512], ps[:, hf, :], XO[c % 2][:, hf * 512:(hf + 1) * 512], ALU.add, op_added)

                def keep_h2(c):
                    if c >= 1:
                        dve.wait_ge(lg_made, c)
                    for j in range(2):
                        dve.wait_ge(h2t_made, 2 * c + j + 1)
                        tt(H2T[:, 4 * j:4 * j + 4, :], quarter(4 + j), wide(pr("gffn")[:, 4 * j:4 * j + 4], P), ALU.mult, h2t_copied)

                def route_shift(c):
                    dve.wait_ge(lg_made, c + 1)
                    link(dve.tensor_reduce(out=mx[:, 0:1], in_=ps[:, 6, 0:E], axis=AX, op=ALU.max))
                    ts(AFT, ps[:, 6, 0:E], mx[:, 0:1], None, ALU.subtract, to=lg_shift)

                def route(c):
                    dve.wait_ge(lg_exp, c + 1)
                    link(dve.reciprocal(rec[:, 0:1], den[:, 0:1]))
                    g, j = (2, ORDER[c]) if ORDER[c] < NP else divmod(ORDER[c] - NP, 4)
                    ts(AFTM[:, j, g * E:(g + 1) * E], AFT, rec[:, 0:1], None, ALU.mult, to=aff_made)

                def best_eight(values, places, rows, r, last):
                    v8 = values[:, 8 * r:8 * r + 8]
                    link(dve.max(v8, rows))
                    link(dve.max_index(places[:, 8 * r:8 * r + 8], v8, rows))
                    if not last:
                        link(dve.match_replace(rows, v8, rows, -1.0))

                def sample_rounds(lo, hi):
                    for r in range(lo, hi):
                        best_eight(VALS, idxus, AFF, r, r == CAPS // 8 - 1)

                keep_y(0)
                for c in range(NC - 1):
                    dve.wait_ge([xo_loaded0, xo_loaded1][c % 2], 16 * (c // 2 + 1))
                    add_x(c, 0)
                    keep_y(c + 1)
                    if c >= 1:
                        keep_h2(c - 1)
                    add_x(c, 1)
                    if c >= 1:
                        route_shift(c - 1)
                        route(c - 1)
                dve.wait_ge(aff_turned, 1)
                link(dve.tensor_copy(AFF, ps[0:2 * E, 7, :]))
                sample_rounds(0, 4)
                dve.wait_ge([xo_loaded0, xo_loaded1][(NC - 1) % 2], 16 * ((NC - 1) // 2 + 1))
                keep_h2(NC - 2)
                add_x(NC - 1, 0)
                sample_rounds(4, 6)
                add_x(NC - 1, 1)
                route_shift(NC - 2)
                sample_rounds(6, 8)
                route(NC - 2)
                keep_h2(NC - 1)
                sample_rounds(8, 9)
                route_shift(NC - 1)
                sample_rounds(9, 10)
                route(NC - 1)
                sample_rounds(10, CAPS // 8)
                dve.wait_ge(aff_turned, 2)
                link(dve.tensor_copy(AFP, ps[0:E, 5, 0:SEQS[0]]))
                for r in range(CAPP // 8):
                    best_eight(VALP, idxup, AFP, r, r == CAPP // 8 - 1)
                link(dve.tensor_copy(IDFS, idxus[:, :]))
                link(dve.tensor_copy(REV[:, 0:CAPS], VALS[:, ::-1]))
                link(dve.tensor_copy(REV[:, CAPS:2 * CAPS], IDFS[:, ::-1]))
                link(dve.tensor_copy(IDFP, idxup[:, :]), top_done)
                dve.wait_ge(topt_made, 1)
                link(dve.tensor_copy(TC[:, 0:4 * E], ps[:, 7, 0:4 * E]))
                link(dve.tensor_copy(TC[0:CAPP, 4 * E:6 * E], ps[0:CAPP, 7, 4 * E:6 * E]))
                va, vb, ia, ib = TC[:, 0:E], TC[:, E:2 * E], TC[:, 2 * E:3 * E], TC[:, 3 * E:4 * E]
                ts(ib, ib, SEQS[1] / 2, None, ALU.add)
                tt(TC[:, 6 * E:7 * E], va, vb, ALU.is_ge)
                tt(gts, va, vb, ALU.max)
                ts(gts, gts, 0.5, None, ALU.mult)
                tt(ia, ia, ib, ALU.subtract)
                tt(ia, ia, TC[:, 6 * E:7 * E], ALU.mult)
                tt(ia, ia, ib, ALU.add)
                link(dve.tensor_copy(idxs[:, :], ia))
                link(dve.tensor_copy(idxp[:, :], TC[0:CAPP, 5 * E:6 * E]))
                ts(gtp, TC[0:CAPP, 4 * E:5 * E], 0.5, None, ALU.mult, to=idx_ready)

                def copy_tokens(e, j):
                    k0, n = THIRDS[j]
                    dve.wait_ge(g_turned, 3 * e + j + 1)
                    tt(XT[e % 2][:, k0:k0 + n, :], ps[:, j % 2, 0:n * TOK].rearrange("p (k t) -> p k t", k=n),
                       wide(pr("gffn")[:, k0:k0 + n], TOK), ALU.mult, g_copied)

                for j in range(3):
                    copy_tokens(0, j)
                for e in range(E):
                    for f in range(KF):
                        dve.wait_ge(gate_tanh, KF * e + f + 1)
                        if f == 0 and e >= 1:
                            dve.wait_ge(down_made, e)
                        stt(HID[:, f, :], THG, 1.0, ps[:, 2 + f % 2, 0:TOK], ALU.add, ALU.mult)
                        tt(HID[:, f, :], HID[:, f, :], ps[:, 2 + f % 2, TOK:2 * TOK], ALU.mult, hid_made)
                        if f == KF - 2 and e + 1 < E:
                            copy_tokens(e + 1, 0)
                    if e + 1 < E:
                        copy_tokens(e + 1, 1)
                        copy_tokens(e + 1, 2)

            @block.tensor
            def _(pe):
                fence = counter(pe, pe_fence)

                def mm(out, a, b, start=True, stop=True):
                    return pe.matmul(out, a, b, start=start, stop=stop)

                def keep_clock(bank, n):
                    for _ in range(n):
                        mm(ps[:, bank, 0:3 * P], ident, cstt[:, 0:3 * P])

                def turn_x(c):
                    pe.wait_ge(scaled, c + 1)
                    for j in range(2):
                        if c >= 2:
                            pe.wait_ge(ht_copied, 2 * c - 3 + j)
                        for k in range(4):
                            last = pe.transpose(ps[:, 4 + 2 * (c % 2) + j, k * P:(k + 1) * P],
                                                XN[c % 4][:, (4 * j + k) * P:(4 * j + k + 1) * P], ident)
                        last.then_inc(ht_made, 1)

                def gates(c):
                    pe.wait_ge(ht_copied, 2 * c + 2)
                    if c >= 2:
                        pe.wait_ge(gate_rows_kept, c - 1)
                    for k in range(KD):
                        last = mm(ps[0:32, [3, 1][c % 2], 0:P], wg[:, k, :], hT[:, k, c * P:(c + 1) * P], k == 0, k == KD - 1)
                    last.then_inc(gate_rows, 1)

                turn_x(0)
                turn_x(1)
                pe.wait_ge(wg_loaded, 32)
                for c in range(NC):
                    gates(c)
                    if c + 2 < NC:
                        turn_x(c + 2)
                for c in range(NC):
                    pe.wait_ge(gate_rows_kept, c + 1)
                    last = pe.transpose(ps[:, 2, c * 32:(c + 1) * 32], GT[:, c * P:(c + 1) * P], ident[0:32, 0:32])
                last.then_inc(gates_made, 1)

                def unit(u):
                    sl, kind, f, g = UNITS[u]
                    pe.wait_ge([ring_loaded0, ring_loaded1][sl % 2], 16 * (sl // 2 + 1))
                    if u >= 2:
                        pe.wait_ge(proj_read, u - 1)
                    for k in range(KD):
                        if kind in ("xbc", "qk"):
                            t0, n = GROUPS[g]
                            last = mm(ps[:, u % 2, 0:n], ring[sl % 2][:, k, (f % 2) * P:(f % 2 + 1) * P], hT[:, k, t0:t0 + n],
                                      k == 0, k == KD - 1)
                        else:
                            last = mm(ps[:, u % 2, 0:256], hT[:, k, g * P:(g + 1) * P], ring[sl % 2][:, k, :], k == 0, k == KD - 1)
                    last.then_inc(proj_made, 1)
                    if u in LAST_UNIT:
                        pe.wait_ge(proj_made, u + 1)
                        pe.sem_inc(slice_used, 1)

                def turn_xs(f):
                    pe.wait_ge(xbc_made, f + 1)
                    for j, (c0, n) in enumerate(((0, 4), (4, 4), (8, 2))):
                        if f or j == 2:
                            pe.wait_ge(xs_kept, 3 * f + (1 if j == 2 else 0))
                        for c in range(c0, c0 + n):
                            last = pe.transpose(ps[:, 2 + j % 2, (c - c0) * P:(c - c0 + 1) * P],
                                                XF[f % 2][:, tcol(c):tcol(c) + P], ident)
                        last.then_inc(xs_turned, 1)

                pe.wait_ge(gate_rows_kept, NC)
                for u in range(0, 6):
                    unit(u)
                pe.wait_ge(al_made, 2)
                csp = ps[:, 5, 0:240].rearrange("p (c d n) -> p c d n", c=NC, d=2)
                for d in range(2):
                    mm(csp[:, :, d, :], tri[d], AL[:, :, d, :])
                last = mm(ps[:, 6, 0:240], ones1.to_broadcast([P, P]), AL)
                last.then_inc(cs_made, 1)
                for u in range(6, 9):
                    unit(u)
                pe.wait_ge(cs_read, 1)
                for d in range(2):
                    for c in range(NC):
                        pe.transpose(ps[0:4, 2 + 3 * d + c // 4, (c % 4) * P:(c % 4 + 1) * P], U[:, c, d, :], ident)
                for d in range(2):
                    for c in range(NC):
                        last = mm(ps[0:4, 4, 256 + d * NC + c:257 + d * NC + c], AL[:, c, d, 8:12], ones1)
                last.then_inc(urow_made, 1)
                unit(9)
                pe.wait_ge(rows_read, 1)
                turn_xs(0)
                for u in range(10, 12):
                    unit(u)
                pe.wait_ge(rows_made, 2)
                for d in range(2):
                    for c in range(NC):
                        for row, at in ((MROW, 0), (UROW, 80)):
                            last = mm(ps[:, 5, at + c * 8 + d * 4:at + c * 8 + d * 4 + 4], row[:, d, c * P:(c + 1) * P], ident[0:4, 0:4])
                last.then_inc(mcol_made, 1)
                turn_xs(1)
                for u in range(12, 15):
                    unit(u)
                pe.wait_ge(mcol_kept, 1)
                pe.wait_ge(m_exps, 1)
                mlp = ps[:, 6, 0:80].rearrange("p (c d n) -> p c d n", c=NC, d=2)
                sop = ps[:, 6, 256:296].rearrange("p (d c n) -> p d c n", d=2, c=NC)
                for d in range(2):
                    at = ident[:, last_of(d):last_of(d) + 1]
                    mm(mlp[:, :, d, :], at.to_broadcast([P, P]), MCOL[:, :, d, :])
                    for q in range(2):
                        last = mm(sop[64 * q:64 * q + 64, d], at.to_broadcast([P, HD]),
                                  SC[:, :, d, :].rearrange("p c (j q) -> p c j q", q=2)[:, :, :, q])
                last.then_inc(mlast_made, 1)
                turn_xs(2)
                for u in range(15, 18):
                    unit(u)
                turn_xs(3)
                for u in range(U_Z, U_Z + Z_AHEAD):
                    unit(u)
                pe.wait_ge(xbc_made, 5)
                pe.wait_ge(xs_kept, 12)
                for j, (c0, n) in enumerate(((0, 4), (4, 4), (8, 2))):
                    if j == 2:
                        pe.wait_ge(b_kept, 1)
                    for c in range(c0, c0 + n):
                        last = pe.transpose(ps[:, 2 + j % 2, (c - c0) * P:(c - c0 + 1) * P], BC[:, 0, tcol(c):tcol(c) + P], ident)
                    last.then_inc(b_turned, 1)
                pe.wait_ge(b_kept, 3)
                for n, i in enumerate(STEPS):
                    for u in z_units(n):
                        unit(u)
                    pe.wait_ge(dxs_made, 2 * n + 2)
                    if n >= 1:
                        pe.wait_ge(state_kept, n)
                    for d in range(2):
                        for g in range(2):
                            last = mm(ps[64 * g:64 * g + 64, 4, 256 * d:256 * d + 256], BT[:, scan_chunk(d, i), 64 * g:64 * g + 64],
                                      DXS[:, n % 2, d, 256 * g:256 * g + 256])
                    last.then_inc(state_made, 1)

                def ssd_cumulative(c, d):
                    if 2 * c + d >= 1:
                        pe.wait_ge(csb_read, 2 * c + d)
                    for h in range(SH):
                        last = mm(ps[:, 2 + h // 4, (h % 4) * P:(h % 4 + 1) * P],
                                  AL[:, c, d, h:h + 1].to_broadcast([P, P]), tri[d])
                    last.then_inc(csb_made, 1)

                def ssd_products(c):
                    t = tcol(c)
                    if c >= 1:
                        pe.wait_ge(w_made, 4 * c)
                    fence(mm(ps[:, 4, 0:P], BC[0:64, 0, t:t + P], BC[0:64, 1, t:t + P]))
                    mm(ps[:, 4, P:2 * P], BC[64:P, 0, t:t + P], BC[64:P, 1, t:t + P]).then_inc(cb_made, 1)

                def ssd_sum(c):
                    t = tcol(c)
                    pe.wait_ge(w_made, 4 * (c + 1))
                    if c >= 1:
                        pe.wait_ge(y_read, c)
                    for h in range(SH):
                        for d in range(2):
                            mm(ps[:, 5, h * HD:(h + 1) * HD], DM[:, c % 2, d, h * P:(h + 1) * P], XS[:, c, h * HD:(h + 1) * HD],
                               d == 0, d == 1)
                    for d in range(2):
                        for g in range(2):
                            last = mm(ps[:, 6 + g, 256 * d:256 * d + 256], BC[64 * g:64 * g + 64, 1, t:t + P],
                                      PREV[64 * g:64 * g + 64, d, c, :])
                    last.then_inc(y_made, 1)

                ssd_cumulative(0, 0)
                unit(U_QK - 2)
                ssd_cumulative(0, 1)
                unit(U_QK - 1)
                pe.wait_ge(state_kept, len(STEPS))
                ssd_products(0)
                for c in range(NC):
                    if c + 1 < NC:
                        ssd_cumulative(c + 1, 0)
                    unit(U_QK + 3 * c)
                    unit(U_QK + 3 * c + 1)
                    if c + 1 < NC:
                        ssd_cumulative(c + 1, 1)
                    unit(U_QK + 3 * c + 2)
                    if c + 1 < NC:
                        ssd_products(c + 1)
                    ssd_sum(c)
                unit(U_ATT - 2)
                unit(U_ATT - 1)
                pe.wait_ge(y_gated, NC)
                pe.wait_ge(v_ones, 1)
                pe.wait_ge(proj_read, U_ATT)

                def turn_keys(n):
                    if n >= 2:
                        pe.wait_ge(wk_made, 2 * (n - 1))
                    for d in range(2):
                        c = scan_chunk(d, STEPS[n])
                        for q in range(2):
                            last = pe.transpose(ps[:, 4 + 2 * (n % 2), 256 * d + q * P:256 * d + (q + 1) * P],
                                                QK[:, 2 + q, c * P:(c + 1) * P], ident)
                    last.then_inc(kt_turned, 1)

                turn_keys(0)
                unit(U_ATT)
                for n, i in enumerate(STEPS):
                    if n + 1 < len(STEPS):
                        turn_keys(n + 1)
                    unit(U_ATT + 1 + n)
                    pe.wait_ge(wk_made, 2 * n + 2)
                    if n >= 2:
                        pe.wait_ge(mstate_kept, 2 * (n - 1))
                    for d in range(2):
                        c = scan_chunk(d, i)
                        for h in range(MH):
                            q = h % 2
                            last = mm(ps[64 * q:64 * q + 64, 5 + 2 * (n % 2), 256 * d + 65 * (h // 2):256 * d + 65 * (h // 2) + 65],
                                      WK[n % 2][:, 256 * d + HD * h:256 * d + HD * (h + 1)], V[:, c, h, :])
                    last.then_inc(mstate_made, 1)
                for u in range(U_ATT + 1 + len(STEPS), U_ATT + NC):
                    unit(u)
                pe.wait_ge(mstate_kept, 2 * len(STEPS))
                pe.transpose(ps[0:8 * NC, 3, 0:P], MCOL.rearrange("p c d n -> p (c d n)"), ident).then_inc(mrow_made, 1)
                pe.wait_ge(mrow_kept, 1)

                def ml_rows(c, d):
                    if 2 * c + d >= 1:
                        pe.wait_ge(mb_read, 2 * c + d)
                    for h in range(MH):
                        r = 8 * c + 4 * d + h
                        last = mm(ps[:, 3, h * P:(h + 1) * P], ident[0:8 * NC, r:r + 1].to_broadcast([8 * NC, P]), MR)
                    last.then_inc(mb_made, 1)

                def ml_products(c):
                    if c >= 1:
                        pe.wait_ge(mw_made, 2 * c)
                    for h in (0, 2, 1, 3):
                        if h == 1:
                            fence(last)
                        b = 64 * (h % 2)
                        last = mm(ps[:, 2, h * P:(h + 1) * P], QK[b:b + 64, 2 + h // 2, c * P:(c + 1) * P],
                                  QK[b:b + 64, h // 2, c * P:(c + 1) * P])
                    last.then_inc(st_made, 1)

                def ml_sum(c):
                    pe.wait_ge(mw_made, 2 * c + 2)
                    if c >= 1:
                        pe.wait_ge(nd_read, 2 * c)
                    for d in range(2):
                        for h in range(MH):
                            mm(ps[:, 5 + d, 65 * h:65 * h + 65], DMM[:, c % 2, d, h, :], V[:, c, h, :])
                    for h in (0, 2, 1, 3):
                        b = 64 * (h % 2)
                        for d in range(2):
                            last = mm(ps[:, 4 + 3 * (h % 2), 130 * d + 65 * (h // 2):130 * d + 65 * (h // 2) + 65],
                                      QK[b:b + 64, h // 2, c * P:(c + 1) * P], PREVM[b:b + 64, d, c, h // 2, :])
                    last.then_inc(nd_made, 1)

                ml_rows(0, 0)
                ml_products(0)
                ml_rows(0, 1)
                for c in range(NC):
                    if c + 1 < NC:
                        ml_rows(c + 1, 0)
                    unit(U_ATT + NC + c)
                    if c + 1 < NC:
                        ml_rows(c + 1, 1)
                        ml_products(c + 1)
                    ml_sum(c)
                def turn_qk(c):
                    if c < QK_FIRST:
                        pe.wait_ge(a_normed, c + 1)
                    else:
                        pe.wait_ge(a_normed_late, c + 1 - QK_FIRST)
                    if c >= 2:
                        pe.wait_ge(a_kept, c - 1)
                    if c >= 5:
                        pe.wait_ge(a_done, c - 4)
                    for j in range(3):
                        last = pe.transpose(ps[:, (c + 1) % 2, j * P:(j + 1) * P], QKN[c % 2][:, j * P:(j + 1) * P], ident)
                    last.then_inc(a_turned, 1)

                def scores(c):
                    nk, c0 = attn_keys(c)
                    pe.wait_ge(a_kept, min(c + 2, NC))
                    if c >= 1:
                        pe.wait_ge(s_read, c)
                    for h in range(AH):
                        g, j = h // 2, h % 2
                        last = mm(ps[:, 2 + h, 0:nk * P], QT[64 * g:64 * g + 64, j, c * P:(c + 1) * P],
                                  KT[64 * g:64 * g + 64, c0 * P:(c0 + nk) * P])
                    last.then_inc(s_made, 1)

                pe.wait_ge(proj_read, len(UNITS))
                keep_clock(3, 5)
                for c in range(3):
                    turn_qk(c)
                pe.wait_ge(nd_read, 2 * NC)
                scores(0)
                keep_clock(7, 3)
                turn_qk(3)
                scores(1)
                keep_clock(7, 2)
                for c in range(NC):
                    nk, c0 = attn_keys(c)
                    pe.wait_ge(sink_exp, c + 1)
                    for h in range(AH):
                        if AH * c + h >= 2:
                            pe.wait_ge(p_kept, AH * c + h - 1)
                        for b in range(nk):
                            last = pe.transpose(ps[:, 6 + h % 2, b * P:(b + 1) * P], PSC[c % 2][:, h, b * P:(b + 1) * P], ident)
                        last.then_inc(p_turned, 1)
                    pe.wait_ge(a_kept, min(c + 4, NC))
                    if c >= 2:
                        pe.wait_ge(a_done, c - 1)
                    for h in range(AH):
                        pe.wait_ge(p_kept, AH * c + h + 1)
                        g = h // 2
                        for b in range(nk):
                            last = mm(ps[:, c % 2, HD * h:HD * h + HD],
                                      TMP[:, h * 384 + b * P:h * 384 + (b + 1) * P],
                                      Z[:, c0 + b, 384 + 64 * g:448 + 64 * g], b == 0, b == nk - 1)
                    last.then_inc(o_made, 1)
                    if c + 4 < NC:
                        turn_qk(c + 4)
                    if c + 2 < NC:
                        scores(c + 2)
                pe.wait_ge(a_done, NC)
                pe.wait_ge(y_done, NC)

                def turn_y(c):
                    at = ORDER[c]
                    tiles = [Z[:, at, 0:P], Z[:, at, P:2 * P]] + [XS[:, at, k * P:(k + 1) * P] for k in range(4)] \
                        + [O[:, at, 0:P], O[:, at, P:2 * P]]
                    for j in range(2):
                        if c >= 1:
                            pe.wait_ge(yt_copied, 2 * c - 1 + j)
                        for k in range(4):
                            last = pe.transpose(ps[:, 2 + j, k * P:(k + 1) * P], tiles[4 * j + k], ident)
                        last.then_inc(yt_made, 1)

                turn_y(0)
                pe.wait_ge(wo_loaded, 16)

                def out_proj(c, hf):
                    pe.wait_ge(yt_copied, 2 * c + 2)
                    if c >= 1:
                        pe.wait_ge(op_added, 2 * c - 1 + hf)
                    for k in range(KD):
                        last = mm(ps[:, hf, :], hT[:, k, ORDER[c] * P:(ORDER[c] + 1) * P], WO[:, k, hf * 512:(hf + 1) * 512], k == 0, k == KD - 1)
                    last.then_inc(op_made, 1)

                for c in range(NC + 1):
                    if c == NC - 1:
                        pe.wait_ge(aff_made, NC - NP)
                        for j in range(4):
                            last = pe.transpose(ps[0:2 * E, 7, j * P:(j + 1) * P], AFTM[:, j, 0:2 * E], ident)
                        last.then_inc(aff_turned, 1)
                    if c < NC:
                        out_proj(c, 0)
                    if c + 1 < NC:
                        turn_y(c + 1)
                    if c >= 1:
                        pe.wait_ge(n2_scaled, c)
                        for j in range(2):
                            if c >= 2:
                                pe.wait_ge(h2t_copied, 2 * c - 3 + j)
                            for k in range(4):
                                last = pe.transpose(ps[:, 4 + j, k * P:(k + 1) * P],
                                                    H2[(c - 1) % 2][:, (4 * j + k) * P:(4 * j + k + 1) * P], ident)
                            last.then_inc(h2t_made, 1)
                    if c < NC:
                        out_proj(c, 1)
                    if c >= 1:
                        pe.wait_ge(h2t_copied, 2 * c)
                        if c >= 2:
                            pe.wait_ge(lg_shift, c - 1)
                        for k in range(KD):
                            last = mm(ps[:, 6, 0:E], H2T[:, k, :], pr("router")[:, k * E:(k + 1) * E], k == 0, k == KD - 1)
                        last.then_inc(lg_made, 1)
                pe.wait_ge(aff_made, NC)
                for j in range(NP):
                    last = pe.transpose(ps[0:E, 5, j * P:(j + 1) * P], AFTM[:, j, 2 * E:3 * E], ident)
                last.then_inc(aff_turned, 1)
                pe.wait_ge(top_done, 1)
                for at, src, rev in ((0, VALS, REV[:, 0:CAPS]), (2 * E, IDFS, REV[:, CAPS:2 * CAPS])):
                    mm(ps[:, 7, at:at + E], src[0:E, :], ident[0:E, 0:E])
                    mm(ps[:, 7, at + E:at + 2 * E], rev, ident[0:2 * E, E:2 * E])
                mm(ps[0:CAPP, 7, 4 * E:5 * E], VALP, ident[0:E, 0:E])
                mm(ps[0:CAPP, 7, 5 * E:6 * E], IDFP, ident[0:E, 0:E]).then_inc(topt_made, 1)
                keep_clock(6, 10)
                pe.wait_ge(idx_ready, 1)

                def turn_tokens(e, j):
                    k0, n = THIRDS[j]
                    pe.wait_ge(gathered[e % 3], 32 * (e // 3 + 1))
                    if e >= 1 or j == 2:
                        pe.wait_ge(g_copied, 3 * e + (1 if j == 2 else 0))
                    for k in range(n):
                        src = slice((k0 + k) * P, (k0 + k + 1) * P)
                        pe.transpose(ps[:, j % 2, k * TOK:k * TOK + CAPS], XG[e % 3][:, src], ident)
                        last = pe.transpose(ps[:, j % 2, k * TOK + CAPS:(k + 1) * TOK], XGP[e % 3][:, src], ident[0:CAPP, 0:CAPP])
                    last.then_inc(g_turned, 1)

                for j in range(3):
                    turn_tokens(0, j)
                for e in range(E):
                    pe.wait_ge([ew_loaded0, ew_loaded1][e % 2], 48 * (e // 2 + 1))
                    pe.wait_ge(g_copied, 3 * e + 3)
                    for f in range(KF):
                        n = KF * e + f
                        if n >= 2:
                            pe.wait_ge(hid_made, n - 1)
                        for w, at in ((EG, 0), (EU, TOK)):
                            for k in range(KD):
                                last = mm(ps[:, 2 + f % 2, at:at + TOK], w[e % 2][:, k, f * P:(f + 1) * P], XT[e % 2][:, k, :],
                                          k == 0, k == KD - 1)
                        last.then_inc(gu_made, 1)
                        if f == KF - 2 and e + 1 < E:
                            turn_tokens(e + 1, 0)
                    if e + 1 < E:
                        turn_tokens(e + 1, 1)
                        turn_tokens(e + 1, 2)
                    pe.wait_ge(hid_made, KF * e + KF)
                    if e >= 1:
                        pe.wait_ge(down_scaled, 4 * e)
                    for j in range(4):
                        hf = j % 2
                        m = CAPS if j < 2 else CAPP
                        t0 = 0 if j < 2 else CAPS
                        for f in range(KF):
                            last = mm(ps[0:m, 4 + j, :], HID[:, f, t0:t0 + m], ED[e % 2][:, f, hf * 512:(hf + 1) * 512],
                                      f == 0, f == KF - 1)
                        last.then_inc(down_part, 1)
                    pe.wait_ge(down_part, 4 * e + 4)
                    pe.sem_inc(down_made, 1)
          nc.gpsimd.dma_reset(rng)
          nc.all_engine_barrier()
          nc.sync.sem_clear(rng)
          nc.all_engine_barrier()


_BIG = [("w_in", D_IN), ("w_out", D), ("w_gate", FF), ("w_up", FF), ("w_down", D)]


def constants():
    i = np.arange(P)
    eye = np.eye(P, dtype=np.float32)
    le = (i[:, None] <= i[None, :]).astype(np.float32)
    cst = np.concatenate([eye, le, le.T, np.ones((P, 1), np.float32)], axis=1)
    rel = np.arange(-(NREL // 2), NREL // 2 + 1)
    half, exact = 16, 8
    n = np.abs(rel)
    large = exact + (np.log(np.maximum(n, 1) / exact) / np.log(128 / exact) * (half - exact)).astype(np.int32)
    bucket = (rel > 0).astype(np.int32) * half + np.where(n < exact, n, np.minimum(large, half - 1))
    hot = np.zeros((33, NREL), np.float32)
    hot[bucket, np.arange(NREL)] = 1.0
    hot[32] = np.where(n <= 128, 0.0, NEG)
    return np.ascontiguousarray(cst), hot


def parameters(x):
    def col(a, k):
        return a.reshape(DEPTH, k, P).transpose(0, 2, 1)

    def row(a):
        a = a.reshape(DEPTH, 1, -1)
        return np.broadcast_to(a, (DEPTH, P, a.shape[2]))

    def twice(a):
        return np.concatenate([a, a], axis=1)[:, :, None]

    cw = x["ssd_conv_w"].reshape(DEPTH, 5, 6, P).transpose(0, 3, 2, 1).reshape(DEPTH, P, 30)
    rt = x["router"].reshape(DEPTH, KD, P, E).transpose(0, 2, 1, 3).reshape(DEPTH, P, KD * E)
    parts = dict(gmix=col(x["mix_norm"], 8), gffn=col(x["ffn_norm"], 8),
                 gy=np.concatenate([np.ones((DEPTH, P, 2), np.float32), col(x["ssd_norm"], 4), col(x["mlstm_norm"], 2)], axis=2),
                 convw=cw, convb=col(x["ssd_conv_b"], 6), qg=twice(x["attn_q_norm"]), kg=twice(x["attn_k_norm"]),
                 sink=row(x["attn_sink"]),
                 gbias=np.concatenate([row(x["ssd_dt_bias"]), row(x["mlstm_i_bias"]), row(x["mlstm_f_bias"])], axis=2),
                 alog=row(x["ssd_a_log"]), dskip=row(x["ssd_d"]), router=rt)
    return np.ascontiguousarray(np.concatenate([parts[n] for n in PAR], axis=2)).reshape(DEPTH * P, NPAR)


def kernel(**inputs):
    import concourse.bacc as bacc
    from concourse.bass_utils import run_bass_kernel_spmd

    x = {k: np.asarray(v) for k, v in inputs.items()}
    cst, hot = constants()
    table = np.concatenate([x["rel_bias"], np.ones((1, AH), np.float32)], axis=0)
    arrays = {n: np.ascontiguousarray(x[n]).reshape(-1, w) for n, w in _BIG}
    arrays.update(flip=np.ascontiguousarray(np.eye(P, dtype=np.float32)[::-1]), par=parameters(x), cst=cst, onehot=np.concatenate([hot, table], axis=1),
                  x_prompt=np.ascontiguousarray(x["x_prompt"][0]), x_sample=np.ascontiguousarray(x["x_sample"][0]))
    nc = bacc.Bacc("TRN2", target_bir_lowering=False, num_devices=1)
    f32 = mybir.dt.float32
    ap = {n: nc.dram_tensor(n, a.shape, f32, kind="ExternalInput").ap() for n, a in arrays.items()}
    yp = nc.dram_tensor("y_prompt", (SEQS[0], D), f32, kind="ExternalOutput").ap()
    ys = nc.dram_tensor("y_sample", (SEQS[1], D), f32, kind="ExternalOutput").ap()
    btab = nc.dram_tensor("bias_table", (AH, 512), f32, kind="Internal").ap()
    h2p = nc.dram_tensor("h2_prompt", (SEQS[0], D), f32, kind="Internal").ap()
    h2s = nc.dram_tensor("h2_sample", (SEQS[1], D), f32, kind="Internal").ap()
    program(nc, ap["w_in"], ap["w_out"], ap["w_gate"], ap["w_up"], ap["w_down"], ap["par"], ap["cst"], ap["onehot"],
            ap["x_prompt"], ap["x_sample"], yp, ys, btab, h2p, h2s, ap["flip"])
    r = run_bass_kernel_spmd(nc, [arrays], core_ids=[0]).results[0]
    return r["y_prompt"][None], r["y_sample"][None]
```
